# Optimizing a Trainium2 kernel written in Bass

```python
import jax, jax.numpy as jnp
from jax import lax
import numpy as np

D_MODEL = 2048
BATCH = 1
SEQ = 256
DEPTH = 1
DEC_BATCH = 8
DEC_SEQ = 4
PAST_LEN = 2048
PAGE_SIZE = 128

D_MIX = D_MODEL
D_CONV = D_MIX // 2
D_POOL = D_MIX - D_CONV
CONV_HEADS = 8
CONV_WIDTH = 31
POOL_WINDOWS = (2, 4, 8, 16)
N_POOL_GROUPS = len(POOL_WINDOWS)
POOL_GROUP_DIM = D_POOL // N_POOL_GROUPS
POOL_MAX_W = max(POOL_WINDOWS)
N_EXPERT_GROUPS = 4
EXPERTS_PER_GROUP = 8
N_EXPERTS = N_EXPERT_GROUPS * EXPERTS_PER_GROUP
TOP_K_IN_GROUP = 2
D_EXPERT = 512
PROJ_COLS = 2 * D_CONV + D_POOL
EPS = 1e-6

kernel_name = "hymba_conv_pool_hiermoe_step"

def rmsnorm(x, g):
    xf = x.astype(jnp.float32)
    y = xf * lax.rsqrt(jnp.mean(xf * xf, axis=-1, keepdims=True) + EPS)
    return (y * g.astype(jnp.float32)).astype(x.dtype)

def layernorm(x, g, b):
    xf = x.astype(jnp.float32)
    mu = jnp.mean(xf, axis=-1, keepdims=True)
    var = jnp.mean(jnp.square(xf - mu), axis=-1, keepdims=True)
    y = (xf - mu) * lax.rsqrt(var + EPS)
    return (y * g.astype(jnp.float32) + b.astype(jnp.float32)).astype(x.dtype)

def conv_mixer(v, gate, buf, w_dw, b_dw, ln_g, ln_b):
    a = v * jax.nn.sigmoid(gate)
    ext = jnp.concatenate([buf.astype(a.dtype), a], axis=1)
    y = lax.conv_general_dilated(
        ext, w_dw[:, None, :], window_strides=(1,), padding='VALID',
        dimension_numbers=('NWC', 'WIO', 'NWC'), feature_group_count=D_CONV)
    y = layernorm(y + b_dw, ln_g, ln_b)
    return jax.nn.silu(y), ext[:, -(CONV_WIDTH - 1):]

def pool_mixer(u, buf, pos0, w_pool, pool_scale):
    B, T, _ = u.shape
    P = POOL_MAX_W - 1
    ext = jnp.concatenate([buf.astype(u.dtype), u], axis=1)
    c = jnp.cumsum(ext.astype(jnp.float32), axis=1)
    c = jnp.pad(c, ((0, 0), (1, 0), (0, 0)))
    pos = pos0 + jnp.arange(T, dtype=jnp.float32)
    means = []
    for g, w in enumerate(POOL_WINDOWS):
        sl = slice(g * POOL_GROUP_DIM, (g + 1) * POOL_GROUP_DIM)
        s = c[:, P + 1:P + 1 + T, sl] - c[:, P + 1 - w:P + 1 - w + T, sl]
        cnt = jnp.minimum(pos + 1.0, float(w))
        means.append(s / cnt[None, :, None])
    mean = jnp.concatenate(means, axis=-1)
    s = (mean - u.astype(jnp.float32)).astype(u.dtype)
    s = s.reshape(B, T, N_POOL_GROUPS, POOL_GROUP_DIM)
    out = jnp.einsum('btgc,gcd->btgd', s, w_pool).reshape(B, T, D_POOL) * pool_scale
    return out, ext[:, -P:]

def hier_moe(h, w_rg, b_rg, w_re, b_re, w_gate, w_up, w_down):
    B, T, D = h.shape
    hf = h.reshape(-1, D)
    N = hf.shape[0]
    glog = (hf @ w_rg).astype(jnp.float32) + b_rg.astype(jnp.float32)
    gprob = jax.nn.softmax(glog, axis=-1)
    g_sel = jnp.argmax(glog, axis=-1)
    p_g = jnp.take_along_axis(gprob, g_sel[:, None], axis=-1)
    elog = ((hf @ w_re).astype(jnp.float32) + b_re.astype(jnp.float32)).reshape(N, N_EXPERT_GROUPS, EXPERTS_PER_GROUP)
    elog_sel = jnp.take_along_axis(elog, g_sel[:, None, None], axis=1)[:, 0]
    top_v, top_i = lax.top_k(elog_sel, TOP_K_IN_GROUP)
    w_top = jax.nn.softmax(top_v, axis=-1) * p_g
    expert_id = g_sel[:, None] * EXPERTS_PER_GROUP + top_i
    gates = jnp.sum(jax.nn.one_hot(expert_id, N_EXPERTS, dtype=jnp.float32) * w_top[..., None], axis=1)
    y = jnp.zeros((N, D), jnp.float32)
    for e in range(N_EXPERTS):
        a = jax.nn.silu(hf @ w_gate[e]) * (hf @ w_up[e])
        y = y + gates[:, e:e + 1] * (a @ w_down[e]).astype(jnp.float32)
    return y.astype(h.dtype).reshape(B, T, D)

def layer(x, pos0, conv_buf, pool_buf, g_mix, w_in, w_dw, b_dw, ln_g, ln_b, w_pool, pool_scale, w_out,
          g_ffn, w_rg, b_rg, w_re, b_re, w_gate, w_up, w_down):
    h = rmsnorm(x, g_mix)
    p = h @ w_in
    v, gate, u = p[..., :D_CONV], p[..., D_CONV:2 * D_CONV], p[..., 2 * D_CONV:]
    yc, new_conv = conv_mixer(v, gate, conv_buf, w_dw, b_dw, ln_g, ln_b)
    yp, new_pool = pool_mixer(u, pool_buf, pos0, w_pool, pool_scale)
    x = x + jnp.concatenate([yc, yp], axis=-1) @ w_out
    x = x + hier_moe(rmsnorm(x, g_ffn), w_rg, b_rg, w_re, b_re, w_gate, w_up, w_down)
    return x, new_conv, new_pool

def setup_inputs(seed: int = 0) -> dict:
    key = jax.random.key(seed)
    ks = jax.random.split(key, 24)
    f = jnp.float32
    nrm = lambda k, shape, s: jax.random.normal(k, shape, f) * s
    return {
        "x_prompt": nrm(ks[0], (BATCH, SEQ, D_MODEL), 1.0),
        "x_sample": nrm(ks[1], (DEC_BATCH, DEC_SEQ, D_MODEL), 1.0),
        "state_conv": nrm(ks[2], (DEPTH, DEC_BATCH, CONV_WIDTH - 1, D_CONV), 0.5),
        "state_pool": nrm(ks[3], (DEPTH, DEC_BATCH, POOL_MAX_W - 1, D_POOL), 1.0),
        "g_mix": 1.0 + nrm(ks[4], (DEPTH, D_MODEL), 0.02),
        "w_in": nrm(ks[5], (DEPTH, D_MODEL, PROJ_COLS), D_MODEL ** -0.5),
        "w_dw": nrm(ks[6], (DEPTH, CONV_WIDTH, D_CONV), CONV_WIDTH ** -0.5),
        "b_dw": nrm(ks[7], (DEPTH, D_CONV), 0.02),
        "ln_g": 1.0 + nrm(ks[8], (DEPTH, D_CONV), 0.02),
        "ln_b": nrm(ks[9], (DEPTH, D_CONV), 0.02),
        "w_pool": nrm(ks[10], (DEPTH, N_POOL_GROUPS, POOL_GROUP_DIM, POOL_GROUP_DIM), POOL_GROUP_DIM ** -0.5),
        "pool_scale": 1.0 + nrm(ks[11], (DEPTH, D_POOL), 0.1),
        "w_out": nrm(ks[12], (DEPTH, D_MIX, D_MODEL), 0.5 * D_MIX ** -0.5),
        "g_ffn": 1.0 + nrm(ks[13], (DEPTH, D_MODEL), 0.02),
        "w_rg": nrm(ks[14], (DEPTH, D_MODEL, N_EXPERT_GROUPS), D_MODEL ** -0.5),
        "b_rg": nrm(ks[15], (DEPTH, N_EXPERT_GROUPS), 0.01),
        "w_re": nrm(ks[16], (DEPTH, D_MODEL, N_EXPERTS), D_MODEL ** -0.5),
        "b_re": nrm(ks[17], (DEPTH, N_EXPERTS), 0.01),
        "w_gate": nrm(ks[18], (DEPTH, N_EXPERTS, D_MODEL, D_EXPERT), D_MODEL ** -0.5),
        "w_up": nrm(ks[19], (DEPTH, N_EXPERTS, D_MODEL, D_EXPERT), D_MODEL ** -0.5),
        "w_down": nrm(ks[20], (DEPTH, N_EXPERTS, D_EXPERT, D_MODEL), D_EXPERT ** -0.5),
        "g_final": 1.0 + nrm(ks[21], (D_MODEL,), 0.02),
    }

def reference(x_prompt, x_sample, state_conv, state_pool, g_mix, w_in, w_dw, b_dw, ln_g, ln_b, w_pool,
              pool_scale, w_out, g_ffn, w_rg, b_rg, w_re, b_re, w_gate, w_up, w_down, g_final):
    xp, xs = x_prompt, x_sample
    conv_p, conv_s, pool_p, pool_s = [], [], [], []
    for l in range(DEPTH):
        wl = (g_mix[l], w_in[l], w_dw[l], b_dw[l], ln_g[l], ln_b[l], w_pool[l], pool_scale[l], w_out[l],
              g_ffn[l], w_rg[l], b_rg[l], w_re[l], b_re[l], w_gate[l], w_up[l], w_down[l])
        zc = jnp.zeros((xp.shape[0], CONV_WIDTH - 1, D_CONV), xp.dtype)
        zp = jnp.zeros((xp.shape[0], POOL_MAX_W - 1, D_POOL), xp.dtype)
        xp, ncp, npp = layer(xp, 0, zc, zp, *wl)
        xs, ncs, nps = layer(xs, PAST_LEN, state_conv[l], state_pool[l], *wl)
        conv_p.append(ncp); conv_s.append(ncs); pool_p.append(npp); pool_s.append(nps)
    y_prompt = rmsnorm(xp, g_final)
    y_sample = rmsnorm(xs, g_final)
    return (y_prompt, y_sample, jnp.stack(conv_p), jnp.stack(conv_s), jnp.stack(pool_p), jnp.stack(pool_s))


_drawn_inputs = setup_inputs


def setup_inputs(seed=0):
    import zlib

    import numpy as np

    out = dict(_drawn_inputs(seed))
    spreads = {}
    factors = {'ln_g': 3.552, 'b_rg': 68.228, 'g_final': 21.127, 'ln_b': 10.268, 'b_re': 6.452}
    for name, (base, spread) in spreads.items():
        noise = np.random.default_rng([zlib.crc32(name.encode()), seed]).standard_normal(out[name].shape)
        drawn = base * np.exp(spread * noise) if base else spread * noise
        out[name] = __import__('jax').numpy.asarray(drawn.astype(out[name].dtype))
    for name, factor in factors.items():
        out[name] = (out[name] * factor).astype(out[name].dtype)
    return out
```

```python
import concourse.bass as bass
from concourse import mybir
from contextlib import ExitStack

F32 = mybir.dt.float32
I32 = mybir.dt.int32
ALU = mybir.AluOpType
ACT = mybir.ActivationFunctionType
AXX = mybir.AxisListType.X

P = 128
D = 2048
KT = D // P
SEQ, NSEQ, SLEN = 256, 8, 4
NS = NSEQ * SLEN
NTOK = SEQ + NS
TR = 96
TT = NTOK // TR
LASTP = SEQ - 2 * TR
CT = 8
DC = CT * P
W, HC = 31, 30
HP = 15
AEXT = HC + NTOK
ULINE = HP + SEQ + NSEQ * (HP + SLEN)
SM0 = HP + SEQ
NE, NG, EG = 32, 4, 8
FE = 512
NR = NG + NE
EPS = 1e-6
BIG = 1e30

BLK = 64
CAP = 64
NTH = (NTOK - 1) // CAP
OVP = max((2 * NTOK // CAP + 1) // 2, 4)
PAIRS = NE // 2
NCOL = PAIRS + OVP
NSLOT = NCOL * P
RW = D + 16

GU_WORDS = KT * 2 * FE
WD_WORDS = (FE // P) * D
O_HT = 0
O_UL = O_HT + KT * NTOK
O_HIST = O_UL + CT * ULINE
O_ST = O_HIST + CT * NSEQ * HC
O_PROW = O_ST + CT * NTOK
O_AW = O_PROW + DC
O_HW = O_AW + 2 * AEXT
O_ACC = O_HW + 2 * NSEQ * (HC + SLEN)
O_VW = O_ACC + 2 * NTOK
O_SG = O_VW + 2 * NTOK
assert O_SG + 2 * NTOK <= GU_WORDS and CT * NTOK <= GU_WORDS - O_AW
O_MIX = GU_WORDS
O_WS = O_MIX + CT * NTOK
O_YC = O_MIX + KT * NTOK
O_AK = O_YC + CT * NTOK
AK = HC + NS
UK = HP + NS
O_UK = O_AK + CT * AK
assert 2 * TT * (P + NCOL) <= 4 * NTOK
assert O_UK + CT * UK <= GU_WORDS + WD_WORDS and 4 * ULINE <= CT * NTOK

WSLOT = KT * 2 * P


class Chain:

    def __init__(self, engine, sem):
        self.engine, self.sem, self.base, self.n = engine, sem, 0, 0

    def step(self, ins):
        ins.then_inc(self.sem, 1)
        self.n += 1

    def link(self, ins):
        self.step(ins)
        self.engine.wait_ge(self.sem, self.base + self.n)

    def loop(self, i, per):
        self.start, self.per = self.base + self.n, per
        self.base, self.n = self.start + i * per, 0

    def end(self, times):
        assert self.n == self.per, (self.n, self.per)
        self.base, self.n = self.start + times * self.per, 0


def hybrid_decoder_step(nc, x_prompt, x_sample, state_conv, state_pool, g_mix, w_in, w_dw, b_dw, ln_g, ln_b,
                        w_pool, pool_scale, w_out, g_ffn, w_rg, b_rg, w_re, b_re, w_gate, w_up, w_down,
                        g_final, y_prompt, y_sample, conv_p, conv_s, pool_p, pool_s):
    ctx = ExitStack()
    with ctx:
        def sb(name, shape, dt=F32):
            return ctx.enter_context(nc.sbuf_tensor(name, shape, dt))

        def sem(name):
            return ctx.enter_context(nc.semaphore(name))

        rows_dram = nc.dram_tensor("token_rows", [NTOK, RW], F32).ap()
        yexp_dram = nc.dram_tensor("expert_rows", [NSLOT, D], F32).ap()

        arena = sb("arena", [P, GU_WORDS + WD_WORDS])
        stage = sb("stage", [P, 2 * WSLOT])
        x1r = sb("x1r", [TR, TT, RW])
        xT = sb("xT", [P, KT * NTOK])
        ysb = sb("ysb", [P, 2, 2 * FE])
        x1w = sb("x1w", [P, 4 * NTOK])
        wr = sb("wr", [P, KT * NR])
        ident = sb("ident", [P, P])
        ones = sb("ones", [P, P])
        earlier = sb("earlier", [TR, TR])
        pv = sb("pv", [64, P])
        pvT = sb("pvT", [P, 64])
        wdT = sb("wdT", [P, CT * 32])
        wdw = sb("wdw", [P, 2, 32])
        rcol = sb("rcol", [P, 16])
        nmean = sb("nmean", [P, NTOK])
        lnv = sb("lnv", [P, NTOK])
        lnr = sb("lnr", [P, NTOK])
        lnt = sb("lnt", [P, NTOK])
        a_sb = sb("a_sb", [P, 256])
        sl_sb = sb("sl_sb", [P, 256])
        aT = sb("aT", [P, 256])
        ss = sb("ss", [TR, TT])
        ssp = sb("ssp", [TR, TT * 4])
        va = sb("va", [TR, TT])
        sq = sb("sq", [TR, TT])
        rs = sb("rs", [TR, TT])
        tn = sb("tn", [TR, TT])
        xrs = sb("xrs", [P, 1])
        zero = sb("zero", [P, TR])
        lgg = sb("lgg", [TR, TT, NG])
        lge = sb("lge", [TR, TT, NE])
        bias = sb("bias", [TR, NR])
        io_i = sb("io_i", [TR, P], I32)
        iof = sb("iof", [TR, P])
        tid_i = sb("tid_i", [TR, TT], I32)
        tid = sb("tid", [TR, 2, TT])
        r4 = sb("r4", [TR, TT, NG])
        r4b = sb("r4b", [TR, TT, NG])
        r4c = sb("r4c", [TR, TT, NG])
        r4d = sb("r4d", [TR, TT, NG])
        g1 = sb("g1", [TR, TT, 1])
        g2 = sb("g2", [TR, TT, 1])
        pg = sb("pg", [TR, TT, 1])
        m1 = sb("m1", [TR, TT, 1])
        m2 = sb("m2", [TR, TT, 1])
        ix = sb("ix", [TR, TT, 1])
        dl = sb("dl", [TR, TT, 1])
        ex = sb("ex", [TR, TT, 1])
        den = sb("den", [TR, TT, 1])
        wt = sb("wt", [TR, 2, TT])
        sel = sb("sel", [TR, TT, NE])
        ra = sb("ra", [TR, TT, NE])
        rb = sb("rb", [TR, TT, NE])
        rc = sb("rc", [TR, TT, NE])
        oh1 = sb("oh1", [TR, TT, NE])
        oh2 = sb("oh2", [TR, TT, NE])
        pick = sb("pick", [TR, TT, NE])
        rank = sb("rank", [TR, TT, NE])
        cnt = sb("cnt", [TR, NE])
        nov = sb("nov", [TR, NE])
        cs = sb("cs", [TR, 2, NE])
        slot = sb("slot", [TR, 2, TT])
        slot_i = sb("slot_i", [TR, 2 * TT], I32)
        hi_i = sb("hi_i", [TR, 2 * TT], I32)
        lo_i = sb("lo_i", [TR, 2 * TT], I32)
        hi = sb("hi", [TR, 2 * TT, 1])
        lo = sb("lo", [TR, 2 * TT, 1])
        tab_i = sb("tab_i", [P, NCOL], I32)
        cur_i = sb("cur_i", [P, 1], I32)
        ecmp = sb("ecmp", [TR, 2 * OVP, NE])
        eid = sb("eid", [TR, 2 * OVP, 1])
        eid_i = sb("eid_i", [TR, 2 * OVP + 1], I32)

        ps = [ctx.enter_context(nc.psum_tensor(f"bank{b}", [P, 512], F32)) for b in range(8)]

        def words(t, off, n, parts=P):
            return t[0:parts, off:off + n]

        def dyn(t, off, n, parts=P):
            return t[0:parts, bass.DynSlice(off, n)]

        hT = words(arena, O_HT, KT * NTOK).rearrange("p (k t) -> p k t", k=KT)
        uline = words(arena, O_UL, CT * ULINE).rearrange("p (j t) -> p j t", j=CT)
        crow = words(arena, O_ST, 2 * DC, 120).rearrange("p (a c) -> p a c", a=2)
        prow = words(arena, O_PROW, DC, 120)
        sT = words(arena, O_ST, CT * NTOK).rearrange("p (j t) -> p j t", j=CT)
        aw = words(arena, O_AW, 2 * AEXT).rearrange("p (c t) -> p c t", c=2)
        hw = words(arena, O_HW, 2 * NSEQ * (HC + SLEN)).rearrange("p (c s t) -> p c s t", c=2, s=NSEQ)
        acc = words(arena, O_ACC, 2 * NTOK).rearrange("p (c t) -> p c t", c=2)
        vw = words(arena, O_VW, 2 * NTOK).rearrange("p (c t) -> p c t", c=2)
        sg = words(arena, O_SG, 2 * NTOK).rearrange("p (c t) -> p c t", c=2)
        sqw = words(arena, O_AW, CT * NTOK).rearrange("p (j t) -> p j t", j=CT)
        mixT = words(arena, O_MIX, KT * NTOK).rearrange("p (k t) -> p k t", k=KT)
        ws = words(arena, O_WS, 4 * ULINE).rearrange("p (a j t) -> p a j t", a=2, j=2)
        yc = words(arena, O_YC, CT * NTOK).rearrange("p (j t) -> p j t", j=CT)
        ak = words(arena, O_AK, CT * AK).rearrange("p (j t) -> p j t", j=CT)
        uk = words(arena, O_UK, CT * UK).rearrange("p (j t) -> p j t", j=CT)
        strow = words(arena, O_HT, 2 * DC, AK).rearrange("p (a c) -> p a c", a=2)
        wgu = words(arena, 0, GU_WORDS).rearrange("p (k g f) -> p k g f", k=KT, g=2)
        wdn = words(arena, GU_WORDS, WD_WORDS).rearrange("p (q d) -> p q d", q=FE // P)
        wsl = [words(stage, a * WSLOT, WSLOT).rearrange("p (k c) -> p k c", k=KT) for a in range(2)]
        xg = words(stage, 0, RW)
        xgT = words(stage, WSLOT, D).rearrange("p (k s) -> p k s", k=KT)
        xTk = xT[:, :].rearrange("p (k t) -> p k t", k=KT)
        gfin = words(xT, 0, D, TR)
        yg = words(arena, 0, 6 * D, TR).rearrange("p (c d) -> p c d", c=6)
        wdr = words(arena, O_WS, DC, W)
        diag = words(x1w, 0, TT * TR, TR).rearrange("p (t c) -> p t c", t=TT)
        ohl = words(x1w, 0, 2 * TT * P, TR).rearrange("p (c s) -> p c s", c=2 * TT)
        ohh = words(x1w, 2 * TT * P, 2 * TT * NCOL, TR).rearrange("p (c s) -> p c s", c=2 * TT)
        x1wk = x1w[:, :].rearrange("p (k t) -> p k t", k=4)
        wr3 = wr[:, :].rearrange("p (k c) -> p k c", k=KT)
        wdT3 = wdT[:, :].rearrange("p (j w) -> p j w", j=CT)
        ssp3 = ssp[:, :].rearrange("p (t o) -> p t o", t=TT)
        pgm, pgf, pbd, plg, plb, pps = (pvT[:, a:b] for a, b in ((0, 16), (16, 32), (32, 40), (40, 48), (48, 56), (56, 64)))

        x_in = [sem(f"x_in{t}") for t in range(TT)]
        pv_in = sem("pv_in")
        wdr_in = sem("wdr_in")
        st_in = sem("st_in")
        wr_in = sem("wr_in")
        bias_in = sem("bias_in")
        gfin_in = sem("gfin_in")
        slot_in = [sem(f"slot_in{a}") for a in range(2)]
        gu_in = [sem(f"gu_in{c}") for c in range(4)]
        wd_in = [sem(f"wd_in{q}") for q in range(4)]
        st_out = sem("st_out")
        rows_out = [sem(f"rows_out{t}") for t in range(TT)]
        y_out = [sem(f"y_out{s}") for s in range(2)]
        fin_out = sem("fin_out")
        cleared = sem("cleared")
        const_ready = sem("const_ready")
        pool_chain = sem("pool_chain")
        work_ready = sem("work_ready")
        keep_ready = sem("keep_ready")
        s_ready = sem("s_ready")
        cur_ready = sem("cur_ready")
        xg_in = sem("xg_in")
        gather_count = sem("gather_count")
        yg_in = [sem(f"yg_in{t}") for t in range(TT)]
        pvT_mm = sem("pvT_mm")
        xT_mm = sem("xT_mm")
        rbc_mm = sem("rbc_mm")
        wdT_mm = sem("wdT_mm")
        hist_mm = sem("hist_mm")
        vg_mm = sem("vg_mm")
        u_mm = sem("u_mm")
        sum_mm = sem("sum_mm")
        sumsq_mm = sem("sumsq_mm")
        st_mm = sem("st_mm")
        wp_mm = sem("wp_mm")
        o_mm = sem("o_mm")
        row_mm = sem("row_mm")
        router_mm = sem("router_mm")
        rank_mm = sem("rank_mm")
        tab_mm = sem("tab_mm")
        xgT_mm = sem("xgT_mm")
        xg_used = sem("xg_used")
        gu_used = sem("gu_used")
        at_mm = sem("at_mm")
        wd_used = sem("wd_used")
        pvT_ready = sem("pvT_ready")
        xT_ready = sem("xT_ready")
        wdT_ready = sem("wdT_ready")
        hist_ready = sem("hist_ready")
        v_evac = sem("v_evac")
        g_evac = sem("g_evac")
        u_evac = [sem("u_evac0"), sem("u_evac1")]
        sqrt_done = sem("sqrt_done")
        nmean_ready = sem("nmean_ready")
        sq_ready = sem("sq_ready")
        st_ready = sem("st_ready")
        wp_ready = sem("wp_ready")
        mix_ready = sem("mix_ready")
        row_evac = sem("row_evac")
        exp_done = sem("exp_done")
        sl_ready = sem("sl_ready")
        aT_ready = sem("aT_ready")
        y0_ready = sem("y0_ready")
        act_chain = sem("act_chain")
        dve_chain = sem("dve_chain")
        conv_chain = sem("conv_chain")
        diag_ready = sem("diag_ready")
        hT_ready = sem("hT_ready")
        glu_ready = sem("glu_ready")
        centred = sem("centred")
        var_ready = sem("var_ready")
        yn_ready = sem("yn_ready")
        wrs_ready = sem("wrs_ready")
        x1_ready = [sem("x1_ready0"), sem("x1_ready1")]
        rstd_ready = sem("rstd_ready")
        act_in = sem("act_in")
        pick_ready = sem("pick_ready")
        oh_ready = sem("oh_ready")
        route_ready = sem("route_ready")
        xs_ready = sem("xs_ready")
        xgT_ready = sem("xgT_ready")
        a_ready = sem("a_ready")
        y1_ready = sem("y1_ready")
        fin_sum = sem("fin_sum")
        out_ready = sem("out_ready")

        block = ctx.enter_context(nc.Block())

        win = w_in[0].rearrange("(k p) c -> p k c", p=P)
        wout = w_out[0].rearrange("(k p) c -> p k c", p=P)
        wpool = w_pool[0].rearrange("g (a p) d -> p (g a) d", p=P)
        wgate = w_gate[0].rearrange("e (k p) f -> p e k f", p=P)
        wup = w_up[0].rearrange("e (k p) f -> p e k f", p=P)
        wdown = w_down[0].rearrange("e (q p) d -> p e q d", p=P)
        xs_rows = x_sample.rearrange("b t d -> (b t) d")
        COL = 2 * P

        @block.sync
        def _(sp):
            for t in range(TT - 1):
                sp.dma_start(x1r[:, t, 0:D], x_prompt[0, t * TR:(t + 1) * TR, :]).then_inc(x_in[t], 16)
            sp.dma_start(x1r[0:LASTP, TT - 1, 0:D], x_prompt[0, (TT - 1) * TR:SEQ, :]).then_inc(x_in[TT - 1], 16)
            sp.dma_start(x1r[LASTP:TR, TT - 1, 0:D], xs_rows).then_inc(x_in[TT - 1], 16)
            sp.dma_start(wsl[0], win[:, :, 0:COL]).then_inc(slot_in[0], 16)
            sp.dma_start(wsl[1], win[:, :, DC:DC + COL]).then_inc(slot_in[1], 16)
            with sp.Fori(1, 4) as g:
                for a in range(2):
                    sp.wait_ge(vg_mm, 4 * g + 2 * a - 2)
                    sp.dma_start(wsl[a], win[:, :, bass.DynSlice(g * COL + a * DC, COL)]).then_inc(slot_in[a], 16)
            for c in range(4):
                sp.wait_ge(vg_mm if c < 2 else u_mm, 14 + 2 * c if c < 2 else 2 * c - 2)
                sp.dma_start(wsl[c % 2], win[:, :, 2 * DC + c * COL:2 * DC + (c + 1) * COL]).then_inc(slot_in[c % 2], 16)
            sp.wait_ge(u_mm, 6)
            sp.dma_start(wsl[0][:, 0:CT, :], wpool).then_inc(slot_in[0], 16)

            def load_gu(e, c):
                for g, src in ((0, wgate), (1, wup)):
                    w = src[:, bass.DynSlice(e, 1), 4 * c:4 * c + 4, :].rearrange("p o k f -> p (o k) f")
                    sp.dma_start(wgu[:, 4 * c:4 * c + 4, g, :], w).then_inc(gu_in[c], 16)

            def load_wd(e, q):
                w = wdown[:, bass.DynSlice(e, 1), q, :].rearrange("p o d -> p (o d)")
                sp.dma_start(wdn[:, q, :], w).then_inc(wd_in[q], 16)

            for c in range(8):
                if c == 0:
                    sp.wait_ge(u_mm, CT)
                elif c == 1:
                    sp.wait_ge(wp_mm, CT)
                else:
                    sp.wait_ge(o_mm, 2 * c - 2)
                sp.dma_start(wsl[(c + 1) % 2], wout[:, :, c * COL:(c + 1) * COL]).then_inc(slot_in[(c + 1) % 2], 16)
                if c == 1:
                    sp.wait_ge(st_out, 16 * 6)
                if c in (1, 3, 4, 5):
                    load_gu(0, (1, 3, 4, 5).index(c))
            sp.wait_ge(o_mm, KT)
            for q in range(4):
                load_wd(0, q)

            def load_expert(e, n):
                for c in range(4):
                    sp.wait_ge(gu_used, 4 * n + c - 3)
                    load_gu(e, c)
                for q in range(4):
                    sp.wait_ge(wd_used, 4 * n + q - 3)
                    load_wd(e, q)

            with sp.Fori(1, NE) as e:
                load_expert(e, e)
            sp.wait_ge(route_ready, 1)
            n_over = sp.value_load(eid_i[0:1, 2 * OVP:2 * OVP + 1], min_val=0, max_val=2 * OVP)
            with sp.Fori(0, OVP) as j:
                with sp.If(n_over > 2 * j):
                    for s in range(2):
                        e = sp.value_load(eid_i[0:1, bass.DynSlice(2 * j + s, 1)], min_val=0, max_val=NE - 1)
                        load_expert(e, NE + 2 * j + s)
            for t in range(TT):
                sp.wait_ge(out_ready, t + 1)
                if t < TT - 1:
                    sp.dma_start(y_prompt[0, t * TR:(t + 1) * TR, :], yg[:, 2 * t, :]).then_inc(fin_out, 16)
                else:
                    sp.dma_start(y_prompt[0, t * TR:SEQ, :], yg[0:LASTP, 2 * t, :]).then_inc(fin_out, 16)
                    sp.dma_start(y_sample.rearrange("b t d -> (b t) d"), yg[LASTP:TR, 2 * t, :]).then_inc(fin_out, 16)
            sp.wait_ge(fin_out, 16 * (TT + 1))

        @block.tensor
        def _(pe):
            pe.wait_ge(const_ready, 1)
            pe.wait_ge(pv_in, 16 * 6)
            pe.transpose(ps[7][:, 0:64], pv[:, :], ident[0:64, 0:64]).then_inc(pvT_mm, 1)
            for k in range(KT):
                if k >= 4:
                    pe.wait_ge(xT_ready, k - 3)
                for t in range(TT):
                    if k == 0:
                        pe.wait_ge(x_in[t], 16 if t < TT - 1 else 32)
                    last = pe.transpose(ps[k % 4][:, t * TR:(t + 1) * TR], x1r[:, t, k * P:(k + 1) * P], ident[0:TR, 0:TR])
                last.then_inc(xT_mm, 1)
            pe.wait_ge(wdr_in, 16)
            for j in range(CT):
                last = pe.transpose(ps[5][:, 32 * j:32 * j + W], wdr[:, j * P:(j + 1) * P], ident[0:W, 0:W])
            last.then_inc(wdT_mm, 1)
            pe.wait_ge(const_ready, 2)
            pe.wait_ge(diag_ready, 1)
            for t in range(TT):
                last = pe.matmul(ps[4][:, t * TR:(t + 1) * TR], ones[0:TR, :], diag[:, t, :], start=True, stop=True)
            last.then_inc(rbc_mm, 1)
            pe.wait_ge(st_in, 16 * 3)
            pe.wait_ge(xT_ready, KT)
            pe.wait_ge(pvT_ready, 1)
            for b in range(4):
                for j in (2 * b, 2 * b + 1):
                    for a in range(2):
                        o = (j % 2) * 240 + a * 120
                        last = pe.transpose(ps[b][:, o:o + 120], crow[:, a, j * P:(j + 1) * P], ident[0:120, 0:120])
                last.then_inc(hist_mm, 1)
            for b in range(2):
                for j in range(4 * b, 4 * b + 4):
                    o = (j % 4) * 120
                    last = pe.transpose(ps[6 + b][:, o:o + 120], prow[:, j * P:(j + 1) * P], ident[0:120, 0:120])
                last.then_inc(hist_mm, 1)
            pe.wait_ge(hist_ready, 4)
            pe.wait_ge(hT_ready, KT)

            def dense(bank, a, cc, rhs, order=range(KT)):
                for n, k in enumerate(order):
                    last = pe.matmul(ps[bank][:, 0:NTOK], wsl[a][:, k, cc * P:(cc + 1) * P], rhs[:, k, :],
                                     start=(n == 0), stop=(n == KT - 1))
                return last

            with pe.Fori(0, 4) as g:
                for a in range(2):
                    pe.wait_ge(slot_in[a], 16 * g + 16)
                    if a:
                        pe.wait_ge(v_evac, 2 * g + 1)
                    for cc in range(2):
                        dense(2 * a + cc, a, cc, hT).then_inc(vg_mm, 1)
                pe.wait_ge(v_evac, 2 * g + 2)

            def pool_inputs(r):
                for c in range(2):
                    pe.wait_ge(slot_in[c], 16 * (5 + r))
                    if r == 0:
                        pe.wait_ge(v_evac if c == 0 else g_evac, CT)
                    else:
                        pe.wait_ge(u_evac[c], 2)
                    for cc in range(2):
                        dense(2 * c + cc, c, cc, hT).then_inc(u_mm, 1)

            pool_inputs(0)
            pe.wait_ge(conv_chain, 4 * 4 * W)
            for j in range(CT):
                last = pe.matmul(ps[4][:, 0:NTOK], ones[:, :], yc[:, j, :], start=(j == 0), stop=(j == CT - 1))
            last.then_inc(sum_mm, 1)
            pool_inputs(1)
            pe.wait_ge(sq_ready, 1)
            for j in range(CT):
                last = pe.matmul(ps[5][:, 0:NTOK], ones[:, :], sqw[:, j, :], start=(j == 0), stop=(j == CT - 1))
            last.then_inc(sumsq_mm, 1)
            pe.wait_ge(keep_ready, CT // 2)
            pe.wait_ge(hist_ready, 6)
            for b in range(2):
                for j in range(4 * b, 4 * b + 4):
                    last = pe.transpose(ps[6 + b][0:AK, (j % 4) * P:(j % 4 + 1) * P], ak[:, j, :], ident[:, :])
                last.then_inc(st_mm, 1)
            pe.wait_ge(u_evac[0], 4)
            pe.wait_ge(u_evac[1], 4)
            for b in range(2):
                for j in range(4 * b, 4 * b + 4):
                    last = pe.transpose(ps[b][0:UK, (j % 4) * P:(j % 4 + 1) * P], uk[:, j, :], ident[:, :])
                last.then_inc(st_mm, 1)
            pe.wait_ge(slot_in[0], 16 * 7)
            pe.wait_ge(s_ready, 2 * NG)
            pe.wait_ge(st_ready, 2)
            for i in range(CT):
                g, dd = i // 2, i % 2
                if i >= 2:
                    pe.wait_ge(wp_ready, i - 1)
                for a in range(2):
                    last = pe.matmul(ps[6 + i % 2][:, 0:NTOK], wsl[0][:, 2 * g + a, dd * P:(dd + 1) * P], sT[:, 2 * g + a, :],
                                     start=(a == 0), stop=(a == 1))
                last.then_inc(wp_mm, 1)
            pe.wait_ge(st_ready, 4)
            pe.wait_ge(wp_ready, CT)
            pe.wait_ge(mix_ready, CT)
            pe.wait_ge(wrs_ready, 1)
            pe.wait_ge(var_ready, 1)
            for t in range(TT):
                pe.matmul(ps[5 + t][0:TR, 0:NR], zero[:, :], wr3[:, 0, :], start=True, stop=False)

            def rows_and_router(o, q):
                pe.wait_ge(x1_ready[q % 2], 2 * o + q // 2 + 1)
                if q == 0:
                    pe.wait_ge(row_evac, TT * o + 1)
                for t in range(TT):
                    last = pe.transpose(ps[2 + t][0:TR, q * P:(q + 1) * P], x1wk[:, q, t * TR:(t + 1) * TR], ident[:, :])
                last.then_inc(row_mm, 1)
                for t in range(TT):
                    pe.matmul(ps[5 + t][0:TR, 0:NR], x1wk[:, q, t * TR:(t + 1) * TR], dyn(wr, (4 * o + q) * NR, NR),
                              start=False, stop=False)

            order = list(range(CT, KT)) + list(range(CT))
            with pe.Fori(0, 4) as o:
                for q in range(4):
                    a = 1 - q // 2
                    if q % 2 == 0:
                        pe.wait_ge(slot_in[a], 16 * o + (16 * 7 if a else 16 * 8))
                    dense(q % 2, a, q % 2, mixT, order).then_inc(o_mm, 1)
                    if q:
                        rows_and_router(o, q - 1)
                rows_and_router(o, 3)
            for t in range(TT):
                last = pe.matmul(ps[5 + t][0:TR, 0:NR], zero[:, :], wr3[:, 0, :], start=False, stop=True)
            last.then_inc(router_mm, 1)
            pe.wait_ge(pick_ready, 1)
            for t in range(TT):
                for b in range(t + 1):
                    pe.matmul(ps[0][0:TR, t * NE:(t + 1) * NE], (ones[0:TR, 0:TR] if b < t else earlier[:, :]), pick[:, b, :],
                              start=(b == 0), stop=(b == t))
            for b in range(TT):
                last = pe.matmul(ps[0][0:TR, TT * NE:(TT + 1) * NE], ones[0:TR, 0:TR], pick[:, b, :],
                                 start=(b == 0), stop=(b == TT - 1))
            last.then_inc(rank_mm, 1)
            pe.wait_ge(oh_ready, 1)
            for c in range(2 * TT):
                last = pe.matmul(ps[1][:, 0:NCOL], ohl[:, c, :], ohh[:, c, :], start=(c == 0), stop=(c == 2 * TT - 1))
            last.then_inc(tab_mm, 1)

            pe.wait_ge(route_ready, 1)
            n_over = pe.value_load(eid_i[0:1, 2 * OVP:2 * OVP + 1], min_val=0, max_val=2 * OVP)

            def pair(i):
                pe.wait_ge(xs_ready, i + 1)
                for b in range(4):
                    if b >= 2:
                        pe.wait_ge(xgT_ready, 4 * i + b - 1)
                    for k in range(4 * b, 4 * b + 4):
                        last = pe.transpose(ps[b % 2][:, (k % 4) * P:(k % 4 + 1) * P], xg[:, k * P:(k + 1) * P], ident[:, :])
                    last.then_inc(xgT_mm, 1)
                pe.wait_ge(xgT_ready, 4 * i + 4)
                for s in range(2):
                    n = 2 * i + s
                    for c in range(4):
                        pe.wait_ge(gu_in[c], 32 * n + 32)
                        for k in range(4 * c, 4 * c + 4):
                            for h in range(2):
                                last = pe.matmul(ps[4 + s][BLK * h:BLK * (h + 1), :], xgT[:, k, BLK * s:BLK * (s + 1)],
                                                 wgu[:, k, :, 256 * h:256 * (h + 1)], start=(k == 0), stop=(k == KT - 1))
                        last.then_inc(gu_used, 1)
                    pe.wait_ge(a_ready, n + 1)
                    for j in range(2):
                        last = pe.transpose(ps[6][:, j * P:(j + 1) * P], a_sb[:, j * P:(j + 1) * P], ident[:, :])
                    last.then_inc(at_mm, 1)
                    pe.wait_ge(aT_ready, n + 1)
                    for q in range(4):
                        half, j = q // 2, q % 2
                        pe.wait_ge(wd_in[q], 16 * n + 16)
                        for m in range(2):
                            for h in range(2):
                                last = pe.matmul(ps[2 + m][BLK * h:BLK * (h + 1), :],
                                                 aT[:, j * P + BLK * half:j * P + BLK * (half + 1)],
                                                 wdn[:, q, 1024 * h + 512 * m:1024 * h + 512 * (m + 1)],
                                                 start=(q == 0), stop=(q == 3))
                        last.then_inc(wd_used, 1)

            with pe.Fori(0, PAIRS) as i:
                pair(i)
            with pe.Fori(0, OVP) as j:
                with pe.If(n_over > 2 * j):
                    pair(PAIRS + j)

        @block.scalar
        def _(act):
            vecs = ((g_mix, 0, 16), (g_ffn, 16, 32), (b_dw, 32, 40), (ln_g, 40, 48), (ln_b, 48, 56), (pool_scale, 56, 64))
            for v, a, b in vecs:
                act.dma_start(pv[a:b, :], v[0].rearrange("(j p) -> j p", p=P)).then_inc(pv_in, 16)
            act.dma_start(wdr, w_dw[0]).then_inc(wdr_in, 16)
            srow = state_conv[0].rearrange("s t c -> (s t) c")
            for a in range(2):
                act.dma_start(crow[:, a, :], srow[120 * a:120 * (a + 1), :]).then_inc(st_in, 16)
            act.dma_start(prow, state_pool[0].rearrange("s t c -> (s t) c")).then_inc(st_in, 16)
            act.dma_start(wr3[:, :, 0:NG], w_rg[0].rearrange("(k p) c -> p k c", p=P)).then_inc(wr_in, 16)
            act.dma_start(wr3[:, :, NG:NR], w_re[0].rearrange("(k p) c -> p k c", p=P)).then_inc(wr_in, 16)
            act.dma_start(bias[:, 0:NG], b_rg[0:1, :].to_broadcast([TR, NG])).then_inc(bias_in, 16)
            act.dma_start(bias[:, NG:NR], b_re[0:1, :].to_broadcast([TR, NE])).then_inc(bias_in, 16)
            act.dma_start(conv_s[0, :, 0:HC - SLEN, :], state_conv[0, :, SLEN:HC, :]).then_inc(st_out, 16)
            act.dma_start(pool_s[0, :, 0:HP - SLEN, :], state_pool[0, :, SLEN:HP, :]).then_inc(st_out, 16)

            act.wait_ge(pvT_mm, 1)
            act.copy(pvT[:, :], ps[7][:, 0:64]).then_inc(pvT_ready, 1)
            for k in range(KT):
                act.wait_ge(xT_mm, k + 1)
                act.copy(xTk[:, k, :], ps[k % 4][:, 0:NTOK]).then_inc(xT_ready, 1)
                if k == 8:
                    act.wait_ge(act_in, 1)
                    act.activation(sq[:, :], va[:, :], ACT.Sqrt).then_inc(sqrt_done, 1)
            act.wait_ge(wdT_mm, 1)
            act.copy(wdT3[:, :, 0:W], ps[5][:, 0:256].rearrange("p (j w) -> p j w", j=CT)[:, :, 0:W]).then_inc(wdT_ready, 1)
            act.copy(wdT3[:, :, W:32].rearrange("p j o -> p (j o)"), pbd).then_inc(wdT_ready, 1)
            for b in range(4):
                act.wait_ge(hist_mm, b + 1)
                act.copy(words(arena, O_HIST + 480 * b, 480), ps[b][:, 0:480]).then_inc(hist_ready, 1)
            for b in range(2):
                act.wait_ge(hist_mm, 5 + b)
                for j in range(4):
                    dst = uline[:, 4 * b + j, SM0:ULINE].rearrange("p (s t) -> p s t", s=NSEQ)[:, :, 0:HP]
                    last = act.copy(dst, ps[6 + b][:, 120 * j:120 * (j + 1)].rearrange("p (s t) -> p s t", s=NSEQ))
                last.then_inc(hist_ready, 1)
            with act.Fori(0, 4) as g:
                for cc in range(2):
                    act.wait_ge(vg_mm, 4 * g + cc + 1)
                    act.copy(vw[:, cc, :], ps[cc][:, 0:NTOK]).then_inc(v_evac, 1)
                for cc in range(2):
                    act.wait_ge(vg_mm, 4 * g + cc + 3)
                    act.activation(sg[:, cc, :], ps[2 + cc][:, 0:NTOK], ACT.Sigmoid).then_inc(g_evac, 1)
                act.wait_ge(glu_ready, 2 * g + 2)

            def pool_lines(r):
                for c in range(4):
                    j = 4 * r + c
                    act.wait_ge(u_mm, j + 1)
                    act.copy(uline[:, j, HP:SM0], ps[c][:, 0:SEQ])
                    act.copy(uk[:, j, :], ps[c][:, SEQ - HP:NTOK])
                    act.copy(uline[:, j, SM0:ULINE].rearrange("p (s t) -> p s t", s=NSEQ)[:, :, HP:HP + SLEN],
                             ps[c][:, SEQ:NTOK].rearrange("p (s t) -> p s t", s=NSEQ)).then_inc(u_evac[c // 2], 1)

            pool_lines(0)
            act.wait_ge(sum_mm, 1)
            act.activation(nmean[:, :], ps[4][:, 0:NTOK], ACT.Copy, scale=-1.0 / DC).then_inc(nmean_ready, 1)
            act.wait_ge(centred, 1)
            act.wait_ge(keep_ready, 4)
            act.activation(words(arena, O_AW, CT * NTOK), words(arena, O_YC, CT * NTOK), ACT.Square).then_inc(sq_ready, 1)
            pool_lines(1)
            act.wait_ge(var_ready, 1)
            act.activation(lnr[:, :], lnv[:, :], ACT.Sqrt).then_inc(sqrt_done, 1)
            for n, (b, r) in enumerate(((6, AK), (7, AK), (0, UK), (1, UK))):
                act.wait_ge(st_mm, n + 1)
                act.copy(strow[0:r, n // 2, (n % 2) * 512:(n % 2 + 1) * 512], ps[b][0:r, :]).then_inc(st_ready, 1)
            act.wait_ge(st_ready, 4)
            act.dma_start(conv_p[0, 0], strow[0:HC, 0, :]).then_inc(st_out, 16)
            act.dma_start(conv_s[0, :, HC - SLEN:HC, :], strow[HC:AK, 0, :]).then_inc(st_out, 16)
            act.dma_start(pool_p[0, 0], strow[0:HP, 1, :]).then_inc(st_out, 16)
            act.dma_start(pool_s[0, :, HP - SLEN:HP, :], strow[HP:UK, 1, :]).then_inc(st_out, 16)
            for i in range(CT):
                act.wait_ge(wp_mm, i + 1)
                act.activation(mixT[:, CT + i, :], ps[6 + i % 2][:, 0:NTOK], ACT.Copy, scale=pps[:, i:i + 1]).then_inc(wp_ready, 1)
            act.wait_ge(yn_ready, 1)
            for j in range(CT):
                act.activation(mixT[:, j, :], yc[:, j, :], ACT.Silu, bias=plb[:, j:j + 1], scale=plg[:, j:j + 1]).then_inc(mix_ready, 1)
            act.sem_inc(row_evac, 1)
            act.wait_ge(cleared, 16 * OVP)
            with act.Fori(0, 4) as o:
                act.wait_ge(row_mm, 4 * o + 4)
                for t in range(TT):
                    act.copy(x1r[:, t, bass.DynSlice(512 * o, 512)], ps[2 + t][0:TR, :]).then_inc(act_chain, 1)
                for t in range(TT):
                    act.activation(ysb[0:TR, t % 2, (t // 2) * 512:(t // 2 + 1) * 512], ps[2 + t][0:TR, :], ACT.Square,
                                   accum_out=dyn(ssp, 4 * t + o, 1, TR)).then_inc(row_evac, 1)
                act.wait_ge(act_chain, TT * o + TT)
                for t in range(TT):
                    act.dma_start(rows_dram[t * TR:(t + 1) * TR, bass.DynSlice(512 * o, 512)],
                                  x1r[:, t, bass.DynSlice(512 * o, 512)]).then_inc(rows_out[t], 16)
                act.wait_ge(row_evac, TT * o + TT + 1)
            act.wait_ge(act_in, 2)
            act.activation(sq[:, :], va[:, :], ACT.Sqrt).then_inc(sqrt_done, 1)
            act.wait_ge(rstd_ready, 1)
            for t in range(TT):
                act.dma_start(rows_dram[t * TR:(t + 1) * TR, D:RW], x1r[:, t, D:RW]).then_inc(rows_out[t], 16)
            act.wait_ge(act_in, 3)
            act.activation(r4b[:, :, :], r4[:, :, :], ACT.Exp).then_inc(exp_done, 1)
            act.wait_ge(act_in, 4)
            act.activation(ex[:, :, :], dl[:, :, :], ACT.Exp).then_inc(exp_done, 1)
            act.wait_ge(xT_ready, KT)
            act.wait_ge(x1_ready[0], 8)
            act.wait_ge(x1_ready[1], 8)
            act.dma_start(gfin, g_final[None, :].to_broadcast([TR, D])).then_inc(gfin_in, 16)

            act.wait_ge(route_ready, 1)
            n_over = act.value_load(eid_i[0:1, 2 * OVP:2 * OVP + 1], min_val=0, max_val=2 * OVP)

            for s in range(2):
                act.sem_inc(y_out[s], 16)

            def pair(i):
                for s in range(2):
                    n = 2 * i + s
                    act.wait_ge(y_out[s], 32 * i + 16)
                    act.wait_ge(gu_used, 4 * n + 4)
                    act.activation(sl_sb[:, :], ps[4 + s][:, 0:256], ACT.Silu).then_inc(sl_ready, 1)
                    act.wait_ge(at_mm, n + 1)
                    act.copy(aT[:, :], ps[6][:, 0:256]).then_inc(aT_ready, 1)
                    act.wait_ge(wd_used, 4 * n + 4)
                    act.copy(ysb[:, s, 0:512], ps[2][:, :]).then_inc(y0_ready, 1)
                    act.wait_ge(y0_ready, n + 1)
                    act.wait_ge(y1_ready, n + 1)
                    for h in range(2):
                        act.dma_start(yexp_dram[bass.DynSlice(BLK * n, BLK), 1024 * h:1024 * (h + 1)],
                                      ysb[BLK * h:BLK * (h + 1), s, :]).then_inc(y_out[s], 16)

            with act.Fori(0, PAIRS) as i:
                pair(i)
            with act.Fori(0, OVP) as j:
                with act.If(n_over > 2 * j):
                    pair(PAIRS + j)
            for t in range(TT):
                act.wait_ge(fin_sum, t + 1)
                act.activation(yg[:, 2 * t + 1, :], yg[:, 2 * t, :], ACT.Square, accum_out=ss[:, t:t + 1]).then_inc(act_chain, 1)
                act.wait_ge(act_in, 5 + t)
                act.activation(sq[:, t:t + 1], va[:, t:t + 1], ACT.Sqrt).then_inc(sqrt_done, 1)

        @block.vector
        def _(dve):
            ch = Chain(dve, dve_chain)
            link = ch.link

            def rsqrt(v, root, r, tmp, n):
                dve.wait_ge(sqrt_done, n)
                link(dve.reciprocal(r, root))
                link(dve.tensor_tensor(tmp, r, r, ALU.mult))
                link(dve.tensor_tensor(tmp, tmp, v, ALU.mult))
                link(dve.tensor_scalar(tmp, tmp, -0.5, 1.5, ALU.mult, ALU.add))
                link(dve.tensor_tensor(r, r, tmp, ALU.mult))

            for t in range(TT):
                dve.wait_ge(x_in[t], 16 if t < TT - 1 else 32)
                link(dve.tensor_tensor_reduce(out=words(arena, O_MIX, D, TR), in0=x1r[:, t, 0:D], in1=x1r[:, t, 0:D],
                                              scale=1.0, scalar=0.0, op0=ALU.mult, op1=ALU.add, accum_out=ss[:, t:t + 1]))
            dve.tensor_scalar(va[:, :], ss[:, :], 1.0 / D, EPS, ALU.mult, ALU.add).then_inc(act_in, 1)
            dve.wait_ge(act_in, 1)
            rsqrt(va[:, :], sq[:, :], rs[:, :], tn[:, :], 1)
            dve.wait_ge(const_ready, 1)
            for t in range(TT):
                last = dve.tensor_scalar(diag[:, t, :], ident[0:TR, 0:TR], rs[:, t:t + 1], None, ALU.mult)
            last.then_inc(diag_ready, 1)
            dve.wait_ge(rbc_mm, 1)
            dve.wait_ge(pvT_ready, 1)
            for k in range(KT):
                dve.wait_ge(xT_ready, k + 1)
                dve.scalar_tensor_tensor(out=hT[:, k, :], in0=xTk[:, k, :], scalar=pgm[:, k:k + 1], in1=ps[4][:, 0:NTOK],
                                         op0=ALU.mult, op1=ALU.mult).then_inc(hT_ready, 1)
            dve.wait_ge(wr_in, 32)
            for k in range(KT):
                last = dve.tensor_scalar(wr3[:, k, :], wr3[:, k, :], pgf[:, k:k + 1], None, ALU.mult)
            last.then_inc(wrs_ready, 1)
            PERC = 4 * W
            with dve.Fori(0, 4) as g:
                for cc in range(2):
                    dve.wait_ge(g_evac, 2 * g + cc + 1)
                    dve.tensor_tensor(aw[:, cc, HC:AEXT], vw[:, cc, :], sg[:, cc, :], ALU.mult).then_inc(glu_ready, 1)
                dve.wait_ge(glu_ready, 2 * g + 2)
                dve.wait_ge(work_ready, g + 1)
                for cc in range(2):
                    new = aw[:, cc, HC + SEQ:AEXT].rearrange("p (s t) -> p s t", s=NSEQ)
                    ch_new = dve.tensor_copy(hw[:, cc, :, HC:HC + SLEN], new)
                ch_new.then_inc(dve_chain, 1)
                dve.wait_ge(dve_chain, ch.n + g + 1)
                for w in range(W):
                    for part in range(4):
                        cc, sample = part % 2, part >= 2
                        if sample:
                            src = hw[:, cc, :, w:w + SLEN]
                            dst = acc[:, cc, SEQ:NTOK].rearrange("p (s t) -> p s t", s=NSEQ)
                            fin = dyn(arena, O_YC + (2 * g + cc) * NTOK + SEQ, NS).rearrange("p (s t) -> p s t", s=NSEQ)
                        else:
                            src, dst = aw[:, cc, w:w + SEQ], acc[:, cc, 0:SEQ]
                            fin = dyn(arena, O_YC + (2 * g + cc) * NTOK, SEQ)
                        if w == 0:
                            ins = dve.tensor_scalar(dst, src, wdw[:, cc, 0:1], wdw[:, cc, W:W + 1], ALU.mult, ALU.add)
                        else:
                            dve.wait_ge(conv_chain, PERC * g + 4 * w + part - 3)
                            ins = dve.scalar_tensor_tensor(out=(fin if w == W - 1 else dst), in0=src, scalar=wdw[:, cc, w:w + 1],
                                                           in1=dst, op0=ALU.mult, op1=ALU.add)
                        ins.then_inc(conv_chain, 1)
                dve.wait_ge(conv_chain, PERC * g + PERC)
                dve.wait_ge(keep_ready, g + 1)
            ch.n += 4
            dve.wait_ge(nmean_ready, 1)
            dve.wait_ge(conv_chain, 4 * PERC)
            dve.tensor_tensor(yc, yc, nmean[:, None, :].to_broadcast([P, CT, NTOK]), ALU.add).then_inc(centred, 1)
            dve.wait_ge(sumsq_mm, 1)
            dve.tensor_scalar(lnv[:, :], ps[5][:, 0:NTOK], 1.0 / DC, EPS, ALU.mult, ALU.add).then_inc(var_ready, 1)
            dve.wait_ge(var_ready, 1)
            dve.wait_ge(centred, 1)
            rsqrt(lnv[:, :], lnr[:, :], nmean[:, :], lnt[:, :], 2)
            dve.tensor_tensor(yc, yc, nmean[:, None, :].to_broadcast([P, CT, NTOK]), ALU.mult).then_inc(yn_ready, 1)
            with dve.Fori(0, 4) as o:
                for q in range(4):
                    dve.wait_ge(o_mm, 4 * o + q + 1)
                    dve.tensor_tensor(x1wk[:, q, :], ps[q % 2][:, 0:NTOK], dyn(xT, (4 * o + q) * NTOK, NTOK),
                                      ALU.add).then_inc(x1_ready[q % 2], 1)
            dve.wait_ge(row_evac, 4 * TT + 1)
            link(dve.tensor_reduce(ss[:, :], ssp3, AXX, ALU.add))
            dve.tensor_scalar(va[:, :], ss[:, :], 1.0 / D, EPS, ALU.mult, ALU.add).then_inc(act_in, 1)
            dve.wait_ge(act_in, 2)
            rsqrt(va[:, :], sq[:, :], rs[:, :], tn[:, :], 3)
            dve.tensor_copy(x1r[:, :, D:RW], rs[:, :, None].to_broadcast([TR, TT, RW - D])).then_inc(rstd_ready, 1)
            dve.wait_ge(router_mm, 1)
            dve.wait_ge(bias_in, 32)
            for t in range(TT):
                ch.step(dve.scalar_tensor_tensor(out=lgg[:, t, :], in0=ps[5 + t][0:TR, 0:NG], scalar=rs[:, t:t + 1],
                                                 in1=bias[:, 0:NG], op0=ALU.mult, op1=ALU.add))
                ch.step(dve.scalar_tensor_tensor(out=lge[:, t, :], in0=ps[5 + t][0:TR, NG:NR], scalar=rs[:, t:t + 1],
                                                 in1=bias[:, NG:NR], op0=ALU.mult, op1=ALU.add))
            dve.wait_ge(dve_chain, ch.n)
            gl = lgg[:, :, :]

            def over(a, n):
                return a.to_broadcast([TR, TT, n])

            link(dve.tensor_reduce(g1[:, :, :], gl, AXX, ALU.max))
            dve.tensor_tensor(r4[:, :, :], gl, over(g1[:, :, :], NG), ALU.subtract).then_inc(act_in, 1)
            dve.wait_ge(act_in, 3)
            dve.wait_ge(const_ready, 3)
            iota4 = iof[:, None, 0:NG].to_broadcast([TR, TT, NG])
            iota32 = iof[:, None, 0:NE].to_broadcast([TR, TT, NE])

            def first(onehot, values, top, tmp, n, iota):
                link(dve.tensor_tensor(tmp, values, over(top, n), ALU.is_equal))
                link(dve.tensor_scalar(tmp, tmp, -64.0, 64.0, ALU.mult, ALU.add))
                link(dve.tensor_tensor(tmp, tmp, iota, ALU.add))
                link(dve.tensor_reduce(ix[:, :, :], tmp, AXX, ALU.min))
                link(dve.tensor_tensor(onehot, iota, over(ix[:, :, :], n), ALU.is_equal))

            first(r4c[:, :, :], gl, g1[:, :, :], r4d[:, :, :], NG, iota4)
            dve.wait_ge(exp_done, 1)
            link(dve.tensor_reduce(g2[:, :, :], r4b[:, :, :], AXX, ALU.add))
            link(dve.reciprocal(pg[:, :, :], g2[:, :, :]))
            link(dve.tensor_scalar(r4c[:, :, :], r4c[:, :, :], BIG, -BIG, ALU.mult, ALU.add))
            link(dve.tensor_tensor(sel[:, :, :].rearrange("p t (g e) -> p (t g) e", g=NG),
                                   r4c[:, :, :].rearrange("p t g -> p (t g)")[:, :, None].to_broadcast([TR, TT * NG, EG]),
                                   lge[:, :, :].rearrange("p t (g e) -> p (t g) e", g=NG), ALU.add))
            link(dve.tensor_reduce(m1[:, :, :], sel[:, :, :], AXX, ALU.max))
            first(oh1[:, :, :], sel[:, :, :], m1[:, :, :], ra[:, :, :], NE, iota32)
            link(dve.scalar_tensor_tensor(out=sel[:, :, :].rearrange("p t e -> p (t e)"), in0=oh1[:, :, :].rearrange("p t e -> p (t e)"),
                                          scalar=-2 * BIG, in1=sel[:, :, :].rearrange("p t e -> p (t e)"), op0=ALU.mult, op1=ALU.add))
            link(dve.tensor_reduce(m2[:, :, :], sel[:, :, :], AXX, ALU.max))
            dve.tensor_tensor(dl[:, :, :], m2[:, :, :], m1[:, :, :], ALU.subtract).then_inc(act_in, 1)
            first(oh2[:, :, :], sel[:, :, :], m2[:, :, :], ra[:, :, :], NE, iota32)
            dve.tensor_tensor(pick[:, :, :], oh1[:, :, :], oh2[:, :, :], ALU.add).then_inc(pick_ready, 1)
            dve.wait_ge(exp_done, 2)
            link(dve.tensor_scalar(den[:, :, :], ex[:, :, :], 1.0, None, ALU.add))
            link(dve.reciprocal(den[:, :, :], den[:, :, :]))
            w0 = wt[:, 0, :][:, :, None]
            w1 = wt[:, 1, :][:, :, None]
            link(dve.tensor_tensor(w0, den[:, :, :], pg[:, :, :], ALU.mult))
            link(dve.tensor_tensor(w1, w0, ex[:, :, :], ALU.mult))
            dve.wait_ge(rank_mm, 1)
            link(dve.tensor_copy(rank[:, :, :].rearrange("p t e -> p (t e)"), ps[0][0:TR, 0:TT * NE]))
            link(dve.tensor_copy(cnt[:, :], ps[0][0:TR, TT * NE:(TT + 1) * NE]))
            link(dve.tensor_scalar(nov[:, :], cnt[:, :], float(CAP), None, ALU.is_gt))
            link(dve.tensor_scalar(rb[:, :, :], rank[:, :, :], float(CAP), None, ALU.is_ge))
            for b in range(2, NTH + 1):
                link(dve.scalar_tensor_tensor(out=nov[:, :], in0=cnt[:, :], scalar=float(CAP * b), in1=nov[:, :], op0=ALU.is_gt, op1=ALU.add))
                link(dve.scalar_tensor_tensor(out=rb[:, :, :], in0=rank[:, :, :], scalar=float(CAP * b), in1=rb[:, :, :],
                                              op0=ALU.is_ge, op1=ALU.add))
            link(dve.tensor_copy(cs[:, 0, :], nov[:, :]))
            at, sh = 0, 1
            while sh < NE:
                dve.tensor_copy(cs[:, 1 - at, 0:sh], cs[:, at, 0:sh])
                link(dve.tensor_tensor(cs[:, 1 - at, sh:NE], cs[:, at, sh:NE], cs[:, at, 0:NE - sh], ALU.add))
                at, sh = 1 - at, 2 * sh
            incl = cs[:, at, :]
            link(dve.tensor_tensor(ecmp[:, :, :], incl[:, None, :].to_broadcast([TR, 2 * OVP, NE]),
                                   iof[:, 0:2 * OVP, None].to_broadcast([TR, 2 * OVP, NE]), ALU.is_le))
            link(dve.tensor_reduce(eid[:, :, :], ecmp[:, :, :], AXX, ALU.add))
            link(dve.tensor_scalar(eid_i[:, 0:2 * OVP], eid[:, :, :].rearrange("p j o -> p (j o)"), float(NE - 1), None, ALU.min))
            link(dve.tensor_copy(eid_i[:, 2 * OVP:2 * OVP + 1], incl[:, NE - 1:NE]))
            link(dve.tensor_tensor(cnt[:, :], incl, nov[:, :], ALU.subtract))
            link(dve.tensor_tensor(cnt[:, :], cnt[:, :], iof[:, 0:NE], ALU.subtract))
            link(dve.tensor_scalar(cnt[:, :], cnt[:, :], float(NE - 1), None, ALU.add))
            link(dve.tensor_tensor(ra[:, :, :], rb[:, :, :], cnt[:, None, :].to_broadcast([TR, TT, NE]), ALU.add))
            link(dve.tensor_scalar(rc[:, :, :], rank[:, :, :], float(CAP), None, ALU.is_ge))
            link(dve.tensor_tensor(ra[:, :, :], ra[:, :, :], rc[:, :, :], ALU.mult))
            link(dve.tensor_tensor(ra[:, :, :], ra[:, :, :], iota32, ALU.add))
            link(dve.scalar_tensor_tensor(out=rb[:, :, :], in0=rb[:, :, :], scalar=-float(CAP), in1=rank[:, :, :], op0=ALU.mult, op1=ALU.add))
            link(dve.scalar_tensor_tensor(out=ra[:, :, :], in0=ra[:, :, :], scalar=float(BLK), in1=rb[:, :, :], op0=ALU.mult, op1=ALU.add))
            for c, oh in ((0, oh1), (1, oh2)):
                link(dve.tensor_tensor(rc[:, :, :], ra[:, :, :], oh[:, :, :], ALU.mult))
                link(dve.tensor_reduce(slot[:, c, :], rc[:, :, :], AXX, ALU.add))
            link(dve.tensor_copy(slot_i[:, :], slot[:, :, :].rearrange("p c t -> p (c t)")))
            link(dve.tensor_scalar(hi_i[:, :], slot_i[:, :], 7, None, ALU.logical_shift_right))
            link(dve.tensor_scalar(lo_i[:, :], slot_i[:, :], P - 1, None, ALU.bitwise_and))
            link(dve.tensor_copy(hi[:, :, :].rearrange("p c o -> p (c o)"), hi_i[:, :]))
            link(dve.tensor_copy(lo[:, :, :].rearrange("p c o -> p (c o)"), lo_i[:, :]))
            link(dve.tensor_tensor(ohl, iof[:, None, 0:P].to_broadcast([TR, 2 * TT, P]),
                                   lo[:, :, :].to_broadcast([TR, 2 * TT, P]), ALU.is_equal))
            link(dve.tensor_tensor(ohh, iof[:, None, 0:NCOL].to_broadcast([TR, 2 * TT, NCOL]),
                                   hi[:, :, :].to_broadcast([TR, 2 * TT, NCOL]), ALU.is_equal))
            dve.tensor_tensor(ohh, ohh,
                              tid[:, :, :].rearrange("p c t -> p (c t)")[:, :, None].to_broadcast([TR, 2 * TT, NCOL]),
                              ALU.mult).then_inc(oh_ready, 1)
            dve.wait_ge(tab_mm, 1)
            dve.tensor_copy(tab_i[:, :], ps[1][:, 0:NCOL]).then_inc(route_ready, 1)
            dve.wait_ge(route_ready, 1)
            n_over = dve.value_load(eid_i[0:1, 2 * OVP:2 * OVP + 1], min_val=0, max_val=2 * OVP)

            def last_norm(t):
                dve.wait_ge(act_chain, 4 * TT + t + 1)
                dve.tensor_scalar(va[:, t:t + 1], ss[:, t:t + 1], 1.0 / D, EPS, ALU.mult, ALU.add).then_inc(act_in, 1)
                dve.wait_ge(act_in, 5 + t)
                rsqrt(va[:, t:t + 1], sq[:, t:t + 1], rs[:, t:t + 1], tn[:, t:t + 1], 4 + t)
                a = yg[:, 2 * t, :]
                dve.scalar_tensor_tensor(out=a, in0=a, scalar=rs[:, t:t + 1], in1=gfin, op0=ALU.mult,
                                         op1=ALU.mult).then_inc(out_ready, 1)

            def pair(i):
                dve.wait_ge(xg_in, 16 * i + 16)
                dve.tensor_scalar(xg[:, 0:D], xg[:, 0:D], xg[:, D:D + 1], None, ALU.mult).then_inc(xs_ready, 1)
                for b in range(4):
                    dve.wait_ge(xgT_mm, 4 * i + b + 1)
                    dve.tensor_tensor(xgT[:, 4 * b:4 * b + 4, :], ps[b % 2][:, :].rearrange("p (k s) -> p k s", k=4),
                                      pgf[:, 4 * b:4 * b + 4, None].to_broadcast([P, 4, P]), ALU.mult).then_inc(xgT_ready, 1)
                for s in range(2):
                    n = 2 * i + s
                    dve.wait_ge(sl_ready, n + 1)
                    dve.tensor_tensor(a_sb[:, :], sl_sb[:, :], ps[4 + s][:, 256:512], ALU.mult).then_inc(a_ready, 1)
                    dve.wait_ge(wd_used, 4 * n + 4)
                    dve.tensor_copy(ysb[:, s, 512:1024], ps[3][:, :]).then_inc(y1_ready, 1)

            with dve.Fori(0, PAIRS) as i:
                pair(i)
            with dve.Fori(0, OVP) as j:
                with dve.If(n_over > 2 * j):
                    pair(PAIRS + j)
            dve.wait_ge(gfin_in, 16)
            for t in range(TT):
                a, b = yg[:, 2 * t, :], yg[:, 2 * t + 1, :]
                dve.wait_ge(yg_in[t], 32)
                link(dve.scalar_tensor_tensor(out=a, in0=a, scalar=wt[:, 0, t:t + 1], in1=x1r[:, t, 0:D], op0=ALU.mult, op1=ALU.add))
                dve.scalar_tensor_tensor(out=a, in0=b, scalar=wt[:, 1, t:t + 1], in1=a, op0=ALU.mult, op1=ALU.add).then_inc(fin_sum, 1)
                if t:
                    last_norm(t - 1)
            last_norm(TT - 1)

        @block.gpsimd
        def _(pool):
            ch = Chain(pool, pool_chain)
            link = ch.link
            link(pool.memset(ident[:, :], 0.0))
            pool.affine_select(out=ident[:, :], in_=ident[:, :], compare_op=ALU.not_equal, fill=1.0, base=0,
                               pattern=[[-1, P]], channel_multiplier=1).then_inc(const_ready, 1)
            pool.wait_ge(const_ready, 1)
            pool.memset(ones[:, :], 1.0).then_inc(const_ready, 1)
            link(pool.memset(aw[:, :, 0:HC], 0.0))
            link(pool.memset(uline[:, :, 0:HP], 0.0))
            link(pool.memset(zero[:, :], 0.0))
            for t in range(HP):
                ch.step(pool.memset(rcol[:, t:t + 1], 1.0 / (t + 1)))
            link(pool.memset(earlier[:, :], 1.0))
            link(pool.affine_select(out=earlier[:, :], in_=earlier[:, :], compare_op=ALU.is_gt, fill=0.0, base=0,
                                    pattern=[[1, TR]], channel_multiplier=-1))
            link(pool.iota(io_i[:, :], pattern=[[1, P]], base=0, channel_multiplier=0))
            link(pool.tensor_copy(iof[:, :], io_i[:, :]))
            link(pool.iota(tid_i[:, :], pattern=[[TR, TT]], base=0, channel_multiplier=1))
            link(pool.tensor_copy(tid[:, 0, :], tid_i[:, :]))
            pool.wait_ge(const_ready, 2)
            pool.tensor_copy(tid[:, 1, :], tid_i[:, :]).then_inc(const_ready, 1)
            link(pool.memset(ysb[:, :, :], 0.0))

            def clear_overflow(c):
                pool.dma_start(yexp_dram[bass.DynSlice((PAIRS + c) * P, P), :],
                               ysb[:, :, :].rearrange("p a c -> p (a c)")).then_inc(cleared, 16)

            pool.wait_ge(wdT_ready, 2)
            pool.wait_ge(hist_ready, 4)
            with pool.Fori(0, 4) as g:
                pool.tensor_copy(wdw[:, :, :], dyn(wdT, 64 * g, 64).rearrange("p (c w) -> p c w", c=2))
                pool.tensor_copy(hw[:, :, :, 0:HC], dyn(arena, O_HIST + 2 * NSEQ * HC * g, 2 * NSEQ * HC)
                                 .rearrange("p (c s t) -> p c s t", c=2, s=NSEQ)).then_inc(work_ready, 1)
                clear_overflow(g)
                pool.wait_ge(glu_ready, 2 * g + 2)
                pool.tensor_copy(dyn(arena, O_AK + 2 * AK * g, 2 * AK).rearrange("p (c t) -> p c t", c=2),
                                 aw[:, :, AEXT - AK:AEXT]).then_inc(keep_ready, 1)
                pool.wait_ge(conv_chain, 4 * W * (g + 1))
            for c in range(4, OVP):
                clear_overflow(c)
            for g in range(NG):
                pool.wait_ge(u_evac[g % 2], 2 * (g // 2) + 2)
                x = uline[:, 2 * g:2 * g + 2, :]
                src, n = x, 1
                for step in range(g + 1):
                    dst = ws[:, step % 2, :, :]
                    lo_ = 2 * n - 1
                    link(pool.tensor_tensor(dst[:, :, lo_:ULINE], src[:, :, lo_:ULINE], src[:, :, lo_ - n:ULINE - n], ALU.add))
                    src, n = dst, 2 * n
                ch.step(pool.tensor_tensor(src[:, :, HP:HP + n - 1], src[:, :, HP:HP + n - 1],
                                           rcol[:, None, 0:n - 1].to_broadcast([P, 2, n - 1]), ALU.mult))
                link(pool.tensor_scalar(src[:, :, HP + n - 1:ULINE], src[:, :, HP + n - 1:ULINE], 1.0 / n, None, ALU.mult))
                ch.step(pool.tensor_tensor(sT[:, 2 * g:2 * g + 2, 0:SEQ], src[:, :, HP:SM0], x[:, :, HP:SM0], ALU.subtract))
                for a in range(2):
                    new = [v[:, a, SM0:ULINE].rearrange("p (s t) -> p s t", s=NSEQ)[:, :, HP:HP + SLEN] for v in (src, x)]
                    ins = pool.tensor_tensor(sT[:, 2 * g + a, SEQ:NTOK].rearrange("p (s t) -> p s t", s=NSEQ), new[0], new[1], ALU.subtract)
                    ins.then_inc(s_ready, 1)
                pool.wait_ge(s_ready, 2 * g + 2)
            pool.wait_ge(o_mm, KT)
            for t in range(TT):
                pool.wait_ge(rows_out[t], 16 * 5)
            pool.wait_ge(route_ready, 1)
            n_over = pool.value_load(eid_i[0:1, 2 * OVP:2 * OVP + 1], min_val=0, max_val=2 * OVP)

            def pair(i):
                pool.tensor_copy(cur_i[:, :], dyn(tab_i, i, 1)).then_inc(cur_ready, 1)
                pool.wait_ge(cur_ready, i + 1)
                pool.sem_inc(gather_count, 1)
                pool.indirect_dma_start(out=xg, out_offset=None, in_=rows_dram,
                                        in_offset=bass.IndirectOffsetOnAxis(ap=cur_i[:, 0:1], axis=0)).then_inc(xg_in, 16)

            pair(0)
            with pool.Fori(1, PAIRS) as i:
                pool.wait_ge(xgT_mm, 4 * i)
                pair(i)
            with pool.Fori(0, OVP) as j:
                with pool.If(n_over > 2 * j):
                    pool.wait_ge(xgT_mm, 4 * (PAIRS + j))
                    pair(PAIRS + j)
                    for s in range(2):
                        pool.wait_ge(y_out[s], 32 * (PAIRS + j) + 48)
            pool.wait_ge(cleared, 16 * OVP)
            for s in range(2):
                pool.wait_ge(y_out[s], 32 * PAIRS + 16)
            for t in range(TT):
                for c in range(2):
                    pool.indirect_dma_start(out=yg[:, 2 * t + c, :], out_offset=None, in_=yexp_dram,
                                            in_offset=bass.IndirectOffsetOnAxis(ap=slot_i[:, c * TT + t:c * TT + t + 1], axis=0)
                                            ).then_inc(yg_in[t], 16)


_INS = ["x_prompt", "x_sample", "state_conv", "state_pool", "g_mix", "w_in", "w_dw", "b_dw", "ln_g", "ln_b", "w_pool",
        "pool_scale", "w_out", "g_ffn", "w_rg", "b_rg", "w_re", "b_re", "w_gate", "w_up", "w_down", "g_final"]
_OUTS = [(1, SEQ, D), (NSEQ, SLEN, D), (1, 1, HC, DC), (1, NSEQ, HC, DC), (1, 1, HP, DC), (1, NSEQ, HP, DC)]


def kernel(**inputs):
    import numpy as _np
    import concourse.bacc as _bacc
    from concourse import mybir as _mybir
    from concourse.bass_utils import run_bass_kernel_spmd as _run

    nc = _bacc.Bacc("TRN2", target_bir_lowering=False, num_devices=1)
    arrays, args = {}, []
    for name in _INS:
        a = _np.ascontiguousarray(inputs[name])
        arrays[f"in_{name}_dram"] = a
        args.append(nc.dram_tensor(f"in_{name}_dram", a.shape, _mybir.dt.from_np(a.dtype), kind="ExternalInput").ap())
    for i, shape in enumerate(_OUTS):
        args.append(nc.dram_tensor(f"out_{i}_dram", shape, _mybir.dt.float32, kind="ExternalOutput").ap())
    hybrid_decoder_step(nc, *args)
    r = _run(nc, [arrays], core_ids=[0])
    return tuple(r.results[0][f"out_{i}_dram"] for i in range(len(_OUTS)))
```

```python
import concourse.bass as bass
from concourse import mybir
from contextlib import ExitStack

F32 = mybir.dt.float32
I32 = mybir.dt.int32
ALU = mybir.AluOpType
ACT = mybir.ActivationFunctionType
AXX = mybir.AxisListType.X

P = 128
D = 2048
KT = D // P
SEQ, NSEQ, SLEN = 256, 8, 4
NS = NSEQ * SLEN
NTOK = SEQ + NS
TR = 96
TT = NTOK // TR
LASTP = SEQ - 2 * TR
CT = 8
DC = CT * P
W, HC = 31, 30
PERC = 2 * W + 4
HP = 15
AEXT = HC + NTOK
ULINE = HP + SEQ + NSEQ * (HP + SLEN)
SM0 = HP + SEQ
NE, NG, EG = 32, 4, 8
FE = 512
NR = NG + NE
EPS = 1e-6
BIG = 1e30

BLK = 64
CAP = 64
OVP = (2 * NTOK // CAP + 1) // 2
PAIRS = NE // 2
NCOL = PAIRS + OVP
NBLK = 2 * NCOL
PAD = 4096
RW = D + 16

GU_WORDS = KT * 2 * FE
WD_WORDS = (FE // P) * D
O_HT = 0
O_UL = O_HT + KT * NTOK
O_HIST = O_UL + CT * ULINE
O_ST = O_HIST + CT * NSEQ * HC
O_PROW = O_ST + CT * NTOK
O_AW = O_PROW + DC
O_HW = O_AW + 2 * AEXT
O_ACC = O_HW + 2 * NSEQ * (HC + SLEN)
O_VW = O_ACC + 2 * NTOK
O_SG = O_VW + 2 * NTOK
assert O_SG + 2 * NTOK <= GU_WORDS and CT * NTOK <= GU_WORDS - O_AW
O_MIX = GU_WORDS
O_WS = O_MIX + CT * NTOK
O_YC = O_MIX + KT * NTOK
O_AK = O_YC + CT * NTOK
AK = HC + NS
UK = HP + NS
O_UK = O_AK + CT * AK
assert 2 * TT * (P + NCOL) <= 4 * NTOK and 2 * TT * NBLK <= KT * NR
assert O_UK + CT * UK <= GU_WORDS + WD_WORDS and 4 * ULINE <= CT * NTOK

WSLOT = KT * 2 * P
assert 2 * WSLOT <= RW + 3 * D


class Chain:

    def __init__(self, engine, sem):
        self.engine, self.sem, self.base, self.n = engine, sem, 0, 0

    def step(self, ins):
        ins.then_inc(self.sem, 1)
        self.n += 1

    def link(self, ins):
        self.step(ins)
        self.engine.wait_ge(self.sem, self.base + self.n)

    def loop(self, i, per):
        self.start, self.per = self.base + self.n, per
        self.base, self.n = self.start + i * per, 0

    def end(self, times):
        assert self.n == self.per, (self.n, self.per)
        self.base, self.n = self.start + times * self.per, 0


def hybrid_decoder_step(nc, x_prompt, x_sample, state_conv, state_pool, g_mix, w_in, w_dw, b_dw, ln_g, ln_b,
                        w_pool, pool_scale, w_out, g_ffn, w_rg, b_rg, w_re, b_re, w_gate, w_up, w_down,
                        g_final, y_prompt, y_sample, conv_p, conv_s, pool_p, pool_s):
    ctx = ExitStack()
    with ctx:
        def sb(name, shape, dt=F32):
            return ctx.enter_context(nc.sbuf_tensor(name, shape, dt))

        def sem(name):
            return ctx.enter_context(nc.semaphore(name))

        rows_dram = nc.dram_tensor("token_rows", [NTOK, RW], F32).ap()
        yexp_dram = nc.dram_tensor("expert_rows", [NTOK * 4, D // 2], F32).ap()

        arena = sb("arena", [P, GU_WORDS + WD_WORDS])
        stage = sb("stage", [P, RW + 3 * D])
        x1r = sb("x1r", [TR, TT, RW])
        xT = sb("xT", [P, KT * NTOK])
        ysb = sb("ysb", [P, 2, 2 * FE])
        x1w = sb("x1w", [P, 4 * NTOK])
        wr = sb("wr", [P, KT * NR])
        ident = sb("ident", [P, P])
        ones = sb("ones", [P, P])
        earlier = sb("earlier", [TR, TR])
        pv = sb("pv", [64, P])
        pvT = sb("pvT", [P, 64])
        wdT = sb("wdT", [P, CT * 32])
        wdw = sb("wdw", [P, 2, 32])
        rcol = sb("rcol", [P, 16])
        nmean = sb("nmean", [P, NTOK])
        lnv = sb("lnv", [P, NTOK])
        lnr = sb("lnr", [P, NTOK])
        lnt = sb("lnt", [P, NTOK])
        a_sb = sb("a_sb", [P, 256])
        sl_sb = sb("sl_sb", [P, 256])
        aT = sb("aT", [P, 256])
        ss = sb("ss", [TR, TT])
        ssp = sb("ssp", [TR, TT * 4])
        va = sb("va", [TR, TT])
        sq = sb("sq", [TR, TT])
        rs = sb("rs", [TR, TT])
        tn = sb("tn", [TR, TT])
        xrs = sb("xrs", [P, 1])
        zero = sb("zero", [P, TR])
        lg = sb("lg", [TR, TT, NR])
        bias = sb("bias", [TR, NR])
        io_i = sb("io_i", [TR, P], I32)
        iof = sb("iof", [TR, P])
        tid_i = sb("tid_i", [TR, TT], I32)
        r4 = sb("r4", [TR, TT, NG])
        r4b = sb("r4b", [TR, TT, NG])
        r4c = sb("r4c", [TR, TT, NG])
        r4d = sb("r4d", [TR, TT, NG])
        g1 = sb("g1", [TR, TT, 1])
        g2 = sb("g2", [TR, TT, 1])
        pg = sb("pg", [TR, TT, 1])
        m1 = sb("m1", [TR, TT, 1])
        m2 = sb("m2", [TR, TT, 1])
        ix = sb("ix", [TR, TT, 1])
        dl = sb("dl", [TR, TT, 1])
        ex = sb("ex", [TR, TT, 1])
        den = sb("den", [TR, TT, 1])
        wt = sb("wt", [TR, 2, TT])
        sel = sb("sel", [TR, TT, NE])
        ra = sb("ra", [TR, TT, NE])
        rc = sb("rc", [TR, TT, NE])
        oh1 = sb("oh1", [TR, TT, NE])
        oh2 = sb("oh2", [TR, TT, NE])
        pick = sb("pick", [TR, TT, NE])
        rank = sb("rank", [TR, TT, NE])
        cnt = sb("cnt", [TR, NE])
        rk_i = sb("rk_i", [TR, (TT + 1) * NE], I32)
        rq = sb("rq", [TR, TT + 1, NE])
        rc2 = sb("rc2", [TR, TT, NE])
        cs = sb("cs", [TR, 2, NE])
        slot = sb("slot", [TR, 2, TT])
        slot_i = sb("slot_i", [TR, 2 * TT], I32)
        cut_i = sb("cut_i", [TR, 3 * 2 * TT], I32)
        cut = sb("cut", [TR, 3 * 2 * TT, 1])
        tab_i = sb("tab_i", [P, NCOL], I32)
        cur_i = sb("cur_i", [P, 1], I32)
        dst_i = sb("dst_i", [P, NBLK], I32)
        cur_d = sb("cur_d", [P, 2], I32)
        half = sb("half", [P, 1])
        cdst = sb("cdst", [TR, 2, TT])
        tsrc = sb("tsrc", [TR, 2, TT])
        ecmp = sb("ecmp", [TR, 2 * OVP, NE])
        eid = sb("eid", [TR, 2 * OVP, 1])
        eid_i = sb("eid_i", [TR, 2 * OVP + 1], I32)

        ps = [ctx.enter_context(nc.psum_tensor(f"bank{b}", [P, 512], F32)) for b in range(8)]

        def words(t, off, n, parts=P):
            return t[0:parts, off:off + n]

        def dyn(t, off, n, parts=P):
            return t[0:parts, bass.DynSlice(off, n)]

        hT = words(arena, O_HT, KT * NTOK).rearrange("p (k t) -> p k t", k=KT)
        uline = words(arena, O_UL, CT * ULINE).rearrange("p (j t) -> p j t", j=CT)
        crow = words(arena, O_ST, 2 * DC, 120).rearrange("p (a c) -> p a c", a=2)
        prow = words(arena, O_PROW, DC, 120)
        prod = words(arena, O_ST, 2 * NS * W).rearrange("p (c t w) -> p c t w", c=2, t=NS)
        sT = words(arena, O_ST, CT * NTOK).rearrange("p (j t) -> p j t", j=CT)
        aw = words(arena, O_AW, 2 * AEXT).rearrange("p (c t) -> p c t", c=2)
        hw = words(arena, O_HW, 2 * NSEQ * (HC + SLEN)).rearrange("p (c s t) -> p c s t", c=2, s=NSEQ)
        acc = words(arena, O_ACC, 2 * NTOK).rearrange("p (c t) -> p c t", c=2)
        vw = words(arena, O_VW, 2 * NTOK).rearrange("p (c t) -> p c t", c=2)
        sg = words(arena, O_SG, 2 * NTOK).rearrange("p (c t) -> p c t", c=2)
        sqw = words(arena, O_AW, CT * NTOK).rearrange("p (j t) -> p j t", j=CT)
        mixT = words(arena, O_MIX, KT * NTOK).rearrange("p (k t) -> p k t", k=KT)
        ws = words(arena, O_WS, 4 * ULINE).rearrange("p (a j t) -> p a j t", a=2, j=2)
        yc = words(arena, O_YC, CT * NTOK).rearrange("p (j t) -> p j t", j=CT)
        ak = words(arena, O_AK, CT * AK).rearrange("p (j t) -> p j t", j=CT)
        uk = words(arena, O_UK, CT * UK).rearrange("p (j t) -> p j t", j=CT)
        strow = words(arena, O_HT, 2 * DC, AK).rearrange("p (a c) -> p a c", a=2)
        wgu = words(arena, 0, GU_WORDS).rearrange("p (k g f) -> p k g f", k=KT, g=2)
        wdn = [[words(arena, GU_WORDS + q * D, D) for q in range(4)],
               [words(xT, 0, D), words(xT, D, D), words(stage, RW + 2 * D, D), words(arena, GU_WORDS + 3 * D, D)]]
        wsl = [words(stage, a * WSLOT, WSLOT).rearrange("p (k c) -> p k c", k=KT) for a in range(2)]
        xg = words(stage, 0, RW)
        xgs = words(stage, RW, D)
        xgT = words(stage, RW + D, D).rearrange("p (k s) -> p k s", k=KT)
        xTk = xT[:, :].rearrange("p (k t) -> p k t", k=KT)
        gfin = words(arena, 2 * TT * D, D, TR)
        yg = words(arena, 0, 2 * TT * D, TR).rearrange("p (t c d) -> p t c d", t=TT, c=2)
        wdr = words(arena, O_WS, DC, W)
        diag = words(x1w, 0, TT * TR, TR).rearrange("p (t c) -> p t c", t=TT)
        ohl = ysb[0:TR, :, :].rearrange("p s c -> p (s c)")[:, 0:2 * TT * P].rearrange("p (c s) -> p c s", c=2 * TT)
        ohw = words(x1w, 0, 2 * TT * P, TR).rearrange("p (c s) -> p c s", c=2 * TT)
        ohh = words(x1w, 2 * TT * P, 2 * TT * NCOL, TR).rearrange("p (c s) -> p c s", c=2 * TT)
        ohb = words(wr, 0, 2 * TT * NBLK, TR).rearrange("p (c s) -> p c s", c=2 * TT)
        x1wk = x1w[:, :].rearrange("p (k t) -> p k t", k=4)
        wr3 = wr[:, :].rearrange("p (k c) -> p k c", k=KT)
        wdT3 = wdT[:, :].rearrange("p (j w) -> p j w", j=CT)
        ssp3 = ssp[:, :].rearrange("p (t o) -> p t o", t=TT)
        pgm, pgf, pbd, plg, plb, pps = (pvT[:, a:b] for a, b in ((0, 16), (16, 32), (32, 40), (40, 48), (48, 56), (56, 64)))

        x_in = [sem(f"x_in{t}") for t in range(TT)]
        pv_in = sem("pv_in")
        wdr_in = sem("wdr_in")
        st_in = sem("st_in")
        wr_in = sem("wr_in")
        bias_in = sem("bias_in")
        gfin_in = sem("gfin_in")
        slot_in = [sem(f"slot_in{a}") for a in range(2)]
        gu_in = [sem(f"gu_in{c}") for c in range(4)]
        wd_in = [[sem(f"wd_in{s}{q}") for q in range(4)] for s in range(2)]
        st_out = sem("st_out")
        old_out = sem("old_out")
        rows_out = [sem(f"rows_out{t}") for t in range(TT)]
        y_out = [sem(f"y_out{s}") for s in range(2)]
        fin_out = sem("fin_out")
        prod_ready = sem("prod_ready")
        const_ready = sem("const_ready")
        pool_chain = sem("pool_chain")
        work_ready = sem("work_ready")
        keep_ready = sem("keep_ready")
        s_ready = sem("s_ready")
        cur_ready = sem("cur_ready")
        dcur_ready = sem("dcur_ready")
        ysb_free = [sem(f"ysb_free{s}") for s in range(2)]
        scattered = sem("scattered")
        xg_in = sem("xg_in")
        waited = sem("waited")
        yg_in = [sem(f"yg_in{t}") for t in range(TT)]
        pvT_mm = sem("pvT_mm")
        xT_mm = sem("xT_mm")
        rbc_mm = sem("rbc_mm")
        wdT_mm = sem("wdT_mm")
        hist_mm = sem("hist_mm")
        vg_mm = sem("vg_mm")
        u_mm = sem("u_mm")
        sum_mm = sem("sum_mm")
        sumsq_mm = sem("sumsq_mm")
        st_mm = sem("st_mm")
        wp_mm = sem("wp_mm")
        o_mm = sem("o_mm")
        row_mm = sem("row_mm")
        router_mm = sem("router_mm")
        rank_mm = sem("rank_mm")
        tab_mm = sem("tab_mm")
        xgT_mm = sem("xgT_mm")
        xg_used = sem("xg_used")
        gu_used = sem("gu_used")
        at_mm = sem("at_mm")
        wd_used = sem("wd_used")
        pvT_ready = sem("pvT_ready")
        xT_ready = [sem(f"xT_ready{a}") for a in range(2)]
        wdT_ready = sem("wdT_ready")
        hist_ready = sem("hist_ready")
        v_evac = sem("v_evac")
        g_evac = sem("g_evac")
        u_evac = [sem("u_evac0"), sem("u_evac1")]
        sqrt_done = sem("sqrt_done")
        nmean_ready = sem("nmean_ready")
        sq_ready = sem("sq_ready")
        st_ready = sem("st_ready")
        wp_ready = sem("wp_ready")
        mix_ready = sem("mix_ready")
        row_evac = sem("row_evac")
        exp_done = sem("exp_done")
        sl_ready = sem("sl_ready")
        aT_ready = sem("aT_ready")
        y0_ready = sem("y0_ready")
        act_chain = sem("act_chain")
        dve_chain = sem("dve_chain")
        conv_chain = sem("conv_chain")
        diag_ready = sem("diag_ready")
        hT_ready = sem("hT_ready")
        glu_ready = sem("glu_ready")
        centred = sem("centred")
        var_ready = sem("var_ready")
        yn_ready = sem("yn_ready")
        wrs_ready = sem("wrs_ready")
        x1_ready = [sem("x1_ready0"), sem("x1_ready1")]
        rstd_ready = sem("rstd_ready")
        act_in = sem("act_in")
        pick_ready = sem("pick_ready")
        oh_ready = sem("oh_ready")
        route_ready = sem("route_ready")
        over_ready = sem("over_ready")
        dst_ready = sem("dst_ready")
        xs_ready = sem("xs_ready")
        xgT_ready = sem("xgT_ready")
        a_ready = sem("a_ready")
        y1_ready = sem("y1_ready")
        fin_sum = sem("fin_sum")
        fin_rstd = sem("fin_rstd")
        scaled = sem("scaled")
        gained = sem("gained")
        out_ready = sem("out_ready")

        block = ctx.enter_context(nc.Block())

        win = w_in[0].rearrange("(k p) c -> p k c", p=P)
        wout = w_out[0].rearrange("(k p) c -> p k c", p=P)
        wpool = w_pool[0].rearrange("g (a p) d -> p (g a) d", p=P)
        wgate = w_gate[0].rearrange("e (k p) f -> p e k f", p=P)
        wup = w_up[0].rearrange("e (k p) f -> p e k f", p=P)
        wdown = w_down[0].rearrange("e (q p) d -> p e q d", p=P)
        xs_rows = x_sample.rearrange("b t d -> (b t) d")
        COL = 2 * P

        @block.sync
        def _(sp):
            vecs = ((g_mix, 0, 16), (g_ffn, 16, 32), (b_dw, 32, 40), (ln_g, 40, 48), (ln_b, 48, 56), (pool_scale, 56, 64))
            for t in range(TT - 1):
                sp.dma_start(x1r[:, t, 0:D], x_prompt[0, t * TR:(t + 1) * TR, :]).then_inc(x_in[t], 16)
            sp.dma_start(x1r[0:LASTP, TT - 1, 0:D], x_prompt[0, (TT - 1) * TR:SEQ, :]).then_inc(x_in[TT - 1], 16)
            sp.dma_start(x1r[LASTP:TR, TT - 1, 0:D], xs_rows).then_inc(x_in[TT - 1], 16)
            for v, a, b in vecs:
                sp.dma_start(pv[a:b, :], v[0].rearrange("(j p) -> j p", p=P)).then_inc(pv_in, 16)
            sp.dma_start(wsl[0], win[:, :, 0:COL]).then_inc(slot_in[0], 16)
            sp.dma_start(wsl[1], win[:, :, DC:DC + COL]).then_inc(slot_in[1], 16)
            with sp.Fori(1, 4) as g:
                for a in range(2):
                    sp.wait_ge(vg_mm, 4 * g + 2 * a - 2)
                    sp.dma_start(wsl[a], win[:, :, bass.DynSlice(g * COL + a * DC, COL)]).then_inc(slot_in[a], 16)
            for c in range(4):
                sp.wait_ge(vg_mm if c < 2 else u_mm, 14 + 2 * c if c < 2 else 2 * c - 2)
                sp.dma_start(wsl[c % 2], win[:, :, 2 * DC + (3 - c) * COL:2 * DC + (4 - c) * COL]).then_inc(slot_in[c % 2], 16)
            sp.wait_ge(u_mm, 6)
            sp.dma_start(wsl[0][:, 0:CT, :], wpool).then_inc(slot_in[0], 16)

            def load_gu(e, c):
                for g, src in ((0, wgate), (1, wup)):
                    w = src[:, bass.DynSlice(e, 1), 4 * c:4 * c + 4, :].rearrange("p o k f -> p (o k) f")
                    sp.dma_start(wgu[:, 4 * c:4 * c + 4, g, :], w).then_inc(gu_in[c], 16)

            def load_wd(e, s, q):
                w = wdown[:, bass.DynSlice(e, 1), q, :].rearrange("p o d -> p (o d)")
                sp.dma_start(wdn[s][q], w).then_inc(wd_in[s][q], 16)

            for c in range(8):
                if c == 0:
                    sp.wait_ge(u_mm, CT)
                elif c == 1:
                    sp.wait_ge(wp_mm, CT)
                else:
                    sp.wait_ge(o_mm, 2 * c - 2)
                sp.dma_start(wsl[(c + 1) % 2], wout[:, :, c * COL:(c + 1) * COL]).then_inc(slot_in[(c + 1) % 2], 16)
                if c == 1:
                    sp.wait_ge(st_out, 16 * 4)
                    sp.wait_ge(old_out, 16 * 2)
                if c in (1, 3, 4, 5):
                    load_gu(0, (1, 3, 4, 5).index(c))
            sp.wait_ge(o_mm, KT)
            for q in range(4):
                load_wd(0, 0, q)
            for a in range(2):
                sp.wait_ge(x1_ready[a], 8)
            for q in range(3):
                load_wd(1, 1, q)

            def gate_up_and_last_down(e, n, s):
                for c in range(4):
                    sp.wait_ge(gu_used, 4 * n + c - 3)
                    load_gu(e, c)
                sp.wait_ge(wd_used, 4 * n)
                load_wd(e, s, 3)

            def first_downs(e, n, s):
                for q in range(3):
                    sp.wait_ge(wd_used, 4 * n + q - 7)
                    load_wd(e, s, q)

            with sp.Fori(0, PAIRS - 1) as i:
                gate_up_and_last_down(2 * i + 1, 2 * i + 1, 1)
                first_downs(2 * i + 2, 2 * i + 2, 0)
                gate_up_and_last_down(2 * i + 2, 2 * i + 2, 0)
                first_downs(2 * i + 3, 2 * i + 3, 1)
            gate_up_and_last_down(NE - 1, NE - 1, 1)
            sp.wait_ge(over_ready, 1)
            n_over = sp.value_load(eid_i[0:1, 2 * OVP:2 * OVP + 1], min_val=0, max_val=2 * OVP)
            with sp.Fori(0, OVP) as j:
                with sp.If(n_over > 2 * j):
                    for s in range(2):
                        e = sp.value_load(eid_i[0:1, bass.DynSlice(2 * j + s, 1)], min_val=0, max_val=NE - 1)
                        first_downs(e, NE + 2 * j + s, s)
                        gate_up_and_last_down(e, NE + 2 * j + s, s)
                    for s in range(2):
                        sp.wait_ge(y_out[s], 16 * (PAIRS + j) + 16)
                        sp.sem_inc(scattered, 1)
            sp.wait_ge(gu_used, 4 * NE)
            sp.dma_start(gfin, g_final[None, :].to_broadcast([TR, D])).then_inc(gfin_in, 16)
            for s in range(2):
                sp.wait_ge(y_out[s], 16 * PAIRS)
            by_token = yexp_dram.rearrange("(t c) d -> t (c d)", c=4)
            for t in range(TT):
                sp.dma_start(yg[:, t, :, :].rearrange("p c d -> p (c d)"), by_token[t * TR:(t + 1) * TR, :]).then_inc(yg_in[t], 16)
            for t in range(TT):
                sp.wait_ge(scaled if t < TT - 1 else out_ready, t + 1 if t < TT - 1 else 1)
                if t < TT - 1:
                    sp.dma_start(y_prompt[0, t * TR:(t + 1) * TR, :], yg[:, t, 0, :]).then_inc(fin_out, 16)
                else:
                    sp.dma_start(y_prompt[0, t * TR:SEQ, :], yg[0:LASTP, t, 0, :]).then_inc(fin_out, 16)
                    sp.dma_start(y_sample.rearrange("b t d -> (b t) d"), yg[LASTP:TR, t, 0, :]).then_inc(fin_out, 16)
            sp.wait_ge(fin_out, 16 * (TT + 1))

        @block.tensor
        def _(pe):
            pe.wait_ge(const_ready, 1)
            for k in range(KT):
                if k >= 4:
                    pe.wait_ge(xT_ready[k % 2], (k - 4) // 2 + 1)
                for t in range(TT):
                    if k == 0:
                        pe.wait_ge(x_in[t], 16 if t < TT - 1 else 32)
                    last = pe.transpose(ps[k % 4][:, t * TR:(t + 1) * TR], x1r[:, t, k * P:(k + 1) * P], ident[0:TR, 0:TR])
                last.then_inc(xT_mm, 1)
            pe.wait_ge(pv_in, 16 * 6)
            pe.transpose(ps[7][:, 0:64], pv[:, :], ident[0:64, 0:64]).then_inc(pvT_mm, 1)
            pe.wait_ge(const_ready, 2)
            pe.wait_ge(diag_ready, 1)
            for t in range(TT):
                last = pe.matmul(ps[4][:, t * TR:(t + 1) * TR], ones[0:TR, :], diag[:, t, :], start=True, stop=True)
            last.then_inc(rbc_mm, 1)
            pe.wait_ge(wdr_in, 16)
            for j in range(CT):
                last = pe.transpose(ps[5][:, 32 * j:32 * j + W], wdr[:, j * P:(j + 1) * P], ident[0:W, 0:W])
            last.then_inc(wdT_mm, 1)
            pe.wait_ge(st_in, 16 * 3)
            for a in range(2):
                pe.wait_ge(xT_ready[a], KT // 2)
            pe.wait_ge(pvT_ready, 1)
            for b in range(4):
                for j in (2 * b, 2 * b + 1):
                    for a in range(2):
                        o = (j % 2) * 240 + a * 120
                        last = pe.transpose(ps[b][:, o:o + 120], crow[:, a, j * P:(j + 1) * P], ident[0:120, 0:120])
                last.then_inc(hist_mm, 1)
            for b in range(2):
                for j in range(4 * b, 4 * b + 4):
                    o = (j % 4) * 120
                    last = pe.transpose(ps[6 + b][:, o:o + 120], prow[:, j * P:(j + 1) * P], ident[0:120, 0:120])
                last.then_inc(hist_mm, 1)
            pe.wait_ge(hist_ready, 4)

            def dense(bank, a, cc, rhs, order=range(KT), late=None, each=None):
                for n, k in enumerate(order):
                    if each:
                        pe.wait_ge(each, k + 1)
                    if late and n == KT // 2:
                        pe.wait_ge(*late)
                    last = pe.matmul(ps[bank][:, 0:NTOK], wsl[a][:, k, cc * P:(cc + 1) * P], rhs[:, k, :],
                                     start=(n == 0), stop=(n == KT - 1))
                return last

            with pe.Fori(0, 4) as g:
                for a in range(2):
                    pe.wait_ge(slot_in[a], 16 * g + 16)
                    if a:
                        pe.wait_ge(v_evac, 2 * g + 1)
                    for cc in range(2):
                        dense(2 * a + cc, a, cc, hT, each=hT_ready if a + cc == 0 else None).then_inc(vg_mm, 1)
                pe.wait_ge(v_evac, 2 * g + 2)

            def pool_inputs(m):
                c, r = m % 2, m // 2
                pe.wait_ge(slot_in[c], 16 * (5 + r))
                if r == 0:
                    pe.wait_ge(v_evac if c == 0 else g_evac, CT)
                else:
                    pe.wait_ge(u_evac[c], 2)
                for cc in range(2):
                    dense(2 * c + cc, c, cc, hT).then_inc(u_mm, 1)

            pool_inputs(0)
            pool_inputs(1)
            pe.wait_ge(conv_chain, 4 * PERC)
            for j in range(CT):
                last = pe.matmul(ps[4][:, 0:NTOK], ones[:, :], yc[:, j, :], start=(j == 0), stop=(j == CT - 1))
            last.then_inc(sum_mm, 1)
            pool_inputs(2)
            pe.wait_ge(sq_ready, 1)
            for j in range(CT):
                last = pe.matmul(ps[5][:, 0:NTOK], ones[:, :], sqw[:, j, :], start=(j == 0), stop=(j == CT - 1))
            last.then_inc(sumsq_mm, 1)
            pool_inputs(3)
            pe.wait_ge(keep_ready, CT // 2)
            pe.wait_ge(hist_ready, 6)
            for b in range(2):
                for j in range(4 * b, 4 * b + 4):
                    last = pe.transpose(ps[6 + b][0:AK, (j % 4) * P:(j % 4 + 1) * P], ak[:, j, :], ident[:, :])
                last.then_inc(st_mm, 1)
            pe.wait_ge(u_evac[0], 4)
            pe.wait_ge(u_evac[1], 4)
            for b in range(2):
                for j in range(4 * b, 4 * b + 4):
                    last = pe.transpose(ps[b][0:UK, (j % 4) * P:(j % 4 + 1) * P], uk[:, j, :], ident[:, :])
                last.then_inc(st_mm, 1)
            pe.wait_ge(slot_in[0], 16 * 7)
            pe.wait_ge(s_ready, 2 * NG)
            pe.wait_ge(st_ready, 2)
            for i in range(CT):
                g, dd = i // 2, i % 2
                if i >= 2:
                    pe.wait_ge(wp_ready, i - 1)
                for a in range(2):
                    last = pe.matmul(ps[6 + i % 2][:, 0:NTOK], wsl[0][:, 2 * g + a, dd * P:(dd + 1) * P], sT[:, 2 * g + a, :],
                                     start=(a == 0), stop=(a == 1))
                last.then_inc(wp_mm, 1)
            pe.wait_ge(st_ready, 4)
            pe.wait_ge(wp_ready, CT)
            pe.wait_ge(wrs_ready, 1)
            pe.wait_ge(var_ready, 1)
            for t in range(TT):
                pe.matmul(ps[5 + t][0:TR, 0:NR], zero[:, :], wr3[:, 0, :], start=True, stop=False)

            def rows_and_router(o, q):
                pe.wait_ge(x1_ready[q % 2], 2 * o + q // 2 + 1)
                if q == 0:
                    pe.wait_ge(row_evac, TT * o + 1)
                for t in range(TT):
                    last = pe.transpose(ps[2 + t][0:TR, q * P:(q + 1) * P], x1wk[:, q, t * TR:(t + 1) * TR], ident[:, :])
                last.then_inc(row_mm, 1)
                for t in range(TT):
                    pe.matmul(ps[5 + t][0:TR, 0:NR], x1wk[:, q, t * TR:(t + 1) * TR], dyn(wr, (4 * o + q) * NR, NR),
                              start=False, stop=False)

            order = list(range(CT, KT)) + list(range(CT))
            with pe.Fori(0, 4) as o:
                for q in range(4):
                    a = 1 - q // 2
                    if q % 2 == 0:
                        pe.wait_ge(slot_in[a], 16 * o + (16 * 7 if a else 16 * 8))
                    dense(q % 2, a, q % 2, mixT, order, (mix_ready, CT) if q == 0 else None).then_inc(o_mm, 1)
                    if q:
                        rows_and_router(o, q - 1)
                rows_and_router(o, 3)
            for t in range(TT):
                last = pe.matmul(ps[5 + t][0:TR, 0:NR], zero[:, :], wr3[:, 0, :], start=False, stop=True)
            last.then_inc(router_mm, 1)
            pe.wait_ge(pick_ready, 1)
            for t in range(TT):
                for b in range(t + 1):
                    pe.matmul(ps[0][0:TR, t * NE:(t + 1) * NE], (ones[0:TR, 0:TR] if b < t else earlier[:, :]), pick[:, b, :],
                              start=(b == 0), stop=(b == t))
            for b in range(TT):
                last = pe.matmul(ps[0][0:TR, TT * NE:(TT + 1) * NE], ones[0:TR, 0:TR], pick[:, b, :],
                                 start=(b == 0), stop=(b == TT - 1))
            last.then_inc(rank_mm, 1)
            pe.wait_ge(oh_ready, 1)
            for c in range(2 * TT):
                last = pe.matmul(ps[1][:, 0:NCOL], ohl[:, c, :], ohh[:, c, :], start=(c == 0), stop=(c == 2 * TT - 1))
            last.then_inc(tab_mm, 1)
            pe.wait_ge(oh_ready, 2)
            for c in range(2 * TT):
                last = pe.matmul(ps[7][:, 0:NBLK], ohw[:, c, :], ohb[:, c, :], start=(c == 0), stop=(c == 2 * TT - 1))
            last.then_inc(tab_mm, 1)


            def pair(i):
                pe.wait_ge(xs_ready, i + 1)
                for b in range(4):
                    if b >= 2:
                        pe.wait_ge(xgT_ready, 4 * i + b - 1)
                    for k in range(4 * b, 4 * b + 4):
                        last = pe.transpose(ps[b % 2][:, (k % 4) * P:(k % 4 + 1) * P], xgs[:, k * P:(k + 1) * P], ident[:, :])
                    last.then_inc(xgT_mm, 1)
                pe.wait_ge(xgT_ready, 4 * i + 4)
                for s in range(2):
                    n = 2 * i + s
                    for c in range(4):
                        pe.wait_ge(gu_in[c], 32 * n + 32)
                        for k in range(4 * c, 4 * c + 4):
                            for h in range(2):
                                last = pe.matmul(ps[4 + s][BLK * h:BLK * (h + 1), :], xgT[:, k, BLK * s:BLK * (s + 1)],
                                                 wgu[:, k, :, 256 * h:256 * (h + 1)], start=(k == 0), stop=(k == KT - 1))
                        last.then_inc(gu_used, 1)
                    pe.wait_ge(a_ready, n + 1)
                    for j in range(2):
                        last = pe.transpose(ps[6][:, j * P:(j + 1) * P], a_sb[:, j * P:(j + 1) * P], ident[:, :])
                    last.then_inc(at_mm, 1)
                    pe.wait_ge(aT_ready, n + 1)
                    for q in range(4):
                        half, j = q // 2, q % 2
                        pe.wait_ge(wd_in[s][q], 16 * i + 16)
                        for m in range(2):
                            for h in range(2):
                                last = pe.matmul(ps[2 + m][BLK * h:BLK * (h + 1), :],
                                                 aT[:, j * P + BLK * half:j * P + BLK * (half + 1)],
                                                 wdn[s][q][:, 1024 * h + 512 * m:1024 * h + 512 * (m + 1)],
                                                 start=(q == 0), stop=(q == 3))
                        last.then_inc(wd_used, 1)

            with pe.Fori(0, PAIRS) as i:
                pair(i)
            pe.wait_ge(over_ready, 1)
            n_over = pe.value_load(eid_i[0:1, 2 * OVP:2 * OVP + 1], min_val=0, max_val=2 * OVP)
            with pe.Fori(0, OVP) as j:
                with pe.If(n_over > 2 * j):
                    pair(PAIRS + j)

        @block.scalar
        def _(act):
            for k in range(0, KT, 2):
                act.wait_ge(xT_mm, k + 1)
                act.copy(xTk[:, k, :], ps[k % 4][:, 0:NTOK]).then_inc(xT_ready[0], 1)
                if k == 4:
                    act.wait_ge(act_in, 1)
                    act.activation(sq[:, :], va[:, :], ACT.Sqrt).then_inc(sqrt_done, 1)
            act.wait_ge(pvT_mm, 1)
            act.copy(pvT[:, :], ps[7][:, 0:64]).then_inc(pvT_ready, 1)
            act.wait_ge(wdT_mm, 1)
            act.copy(wdT3[:, :, 0:W], ps[5][:, 0:256].rearrange("p (j w) -> p j w", j=CT)[:, :, 0:W]).then_inc(wdT_ready, 1)
            act.wait_ge(pvT_ready, 1)
            act.copy(wdT3[:, :, W:32].rearrange("p j o -> p (j o)"), pbd).then_inc(wdT_ready, 1)
            for b in range(4):
                act.wait_ge(hist_mm, b + 1)
                act.copy(words(arena, O_HIST + 480 * b, 480), ps[b][:, 0:480]).then_inc(hist_ready, 1)
            for b in range(2):
                act.wait_ge(hist_mm, 5 + b)
                for j in range(4):
                    dst = uline[:, 4 * b + j, SM0:ULINE].rearrange("p (s t) -> p s t", s=NSEQ)[:, :, 0:HP]
                    last = act.copy(dst, ps[6 + b][:, 120 * j:120 * (j + 1)].rearrange("p (s t) -> p s t", s=NSEQ))
                last.then_inc(hist_ready, 1)
            with act.Fori(0, 4) as g:
                for cc in range(2):
                    act.wait_ge(vg_mm, 4 * g + cc + 1)
                    act.copy(vw[:, cc, :], ps[cc][:, 0:NTOK]).then_inc(v_evac, 1)
                for cc in range(2):
                    act.wait_ge(vg_mm, 4 * g + cc + 3)
                    act.activation(sg[:, cc, :], ps[2 + cc][:, 0:NTOK], ACT.Sigmoid).then_inc(g_evac, 1)
                act.wait_ge(glu_ready, 2 * g + 2)

            def pool_line(n):
                c, j = n % 4, CT - 2 - 2 * (n // 2) + n % 2
                act.wait_ge(u_mm, n + 1)
                act.copy(uline[:, j, HP:SM0], ps[c][:, 0:SEQ])
                act.copy(uk[:, j, :], ps[c][:, SEQ - HP:NTOK])
                act.copy(uline[:, j, SM0:ULINE].rearrange("p (s t) -> p s t", s=NSEQ)[:, :, HP:HP + SLEN],
                         ps[c][:, SEQ:NTOK].rearrange("p (s t) -> p s t", s=NSEQ)).then_inc(u_evac[c // 2], 1)

            for n in range(4):
                pool_line(n)
            act.wait_ge(sum_mm, 1)
            act.activation(nmean[:, :], ps[4][:, 0:NTOK], ACT.Copy, scale=-1.0 / DC).then_inc(nmean_ready, 1)
            act.wait_ge(centred, 1)
            act.wait_ge(keep_ready, 4)
            act.activation(words(arena, O_AW, CT * NTOK), words(arena, O_YC, CT * NTOK), ACT.Square).then_inc(sq_ready, 1)
            pool_line(4)
            pool_line(5)
            act.wait_ge(var_ready, 1)
            act.activation(lnr[:, :], lnv[:, :], ACT.Sqrt).then_inc(sqrt_done, 1)
            pool_line(6)
            act.wait_ge(yn_ready, 1)
            for j in range(CT):
                act.activation(mixT[:, j, :], yc[:, j, :], ACT.Silu, bias=plb[:, j:j + 1], scale=plg[:, j:j + 1]).then_inc(mix_ready, 1)
            pool_line(7)
            for n, (b, r) in enumerate(((6, AK), (7, AK), (0, UK), (1, UK))):
                act.wait_ge(st_mm, n + 1)
                act.copy(strow[0:r, n // 2, (n % 2) * 512:(n % 2 + 1) * 512], ps[b][0:r, :]).then_inc(st_ready, 1)
            act.wait_ge(st_ready, 4)
            act.dma_start(conv_p[0, 0], strow[0:HC, 0, :]).then_inc(st_out, 16)
            act.dma_start(conv_s[0, :, HC - SLEN:HC, :], strow[HC:AK, 0, :]).then_inc(st_out, 16)
            act.dma_start(pool_p[0, 0], strow[0:HP, 1, :]).then_inc(st_out, 16)
            act.dma_start(pool_s[0, :, HP - SLEN:HP, :], strow[HP:UK, 1, :]).then_inc(st_out, 16)
            with act.Fori(0, 4) as o:
                act.wait_ge(row_mm, 4 * o + 4)
                for t in range(TT):
                    act.activation(ysb[0:TR, t % 2, (t // 2) * 512:(t // 2 + 1) * 512], ps[2 + t][0:TR, :], ACT.Square,
                                   accum_out=dyn(ssp, 4 * t + o, 1, TR)).then_inc(act_chain, 1)
                act.wait_ge(act_chain, TT * o + TT)
                for t in range(TT):
                    act.wait_ge(row_evac, TT * o + t + 2)
                    act.dma_start(rows_dram[t * TR:(t + 1) * TR, bass.DynSlice(512 * o, 512)],
                                  x1r[:, t, bass.DynSlice(512 * o, 512)]).then_inc(rows_out[t], 16)
            act.wait_ge(act_in, 2)
            act.activation(sq[:, :], va[:, :], ACT.Sqrt).then_inc(sqrt_done, 1)
            act.wait_ge(rstd_ready, 1)
            act.copy(x1r[:, :, D:RW], rs[:, :, None].to_broadcast([TR, TT, RW - D])).then_inc(act_chain, 1)
            act.wait_ge(act_chain, 4 * TT + 1)
            for t in range(TT):
                act.dma_start(rows_dram[t * TR:(t + 1) * TR, D:RW], x1r[:, t, D:RW]).then_inc(rows_out[t], 16)
            act.wait_ge(act_in, 3)
            act.activation(r4b[:, :, :], r4[:, :, :], ACT.Exp).then_inc(exp_done, 1)
            act.wait_ge(act_in, 4)
            act.activation(ex[:, :, :], dl[:, :, :], ACT.Exp).then_inc(exp_done, 1)


            def pair(i):
                for s in range(2):
                    n = 2 * i + s
                    act.wait_ge(ysb_free[s], i + 1)
                    act.wait_ge(gu_used, 4 * n + 4)
                    act.activation(sl_sb[:, :], ps[4 + s][:, 0:256], ACT.Silu).then_inc(sl_ready, 1)
                    act.wait_ge(at_mm, n + 1)
                    act.copy(aT[:, :], ps[6][:, 0:256]).then_inc(aT_ready, 1)
                    act.wait_ge(wd_used, 4 * n + 4)
                    act.copy(ysb[:, s, 0:512], ps[2][:, :]).then_inc(y0_ready, 1)

            with act.Fori(0, PAIRS) as i:
                pair(i)
            act.wait_ge(over_ready, 1)
            n_over = act.value_load(eid_i[0:1, 2 * OVP:2 * OVP + 1], min_val=0, max_val=2 * OVP)
            with act.Fori(0, OVP) as j:
                with act.If(n_over > 2 * j):
                    pair(PAIRS + j)
            for t in range(TT):
                act.wait_ge(fin_sum, t + 1)
                act.activation(yg[:, t, 1, :], yg[:, t, 0, :], ACT.Square, accum_out=ss[:, t:t + 1]).then_inc(act_chain, 1)
                act.wait_ge(act_in, 5 + t)
                act.activation(sq[:, t:t + 1], va[:, t:t + 1], ACT.Sqrt).then_inc(sqrt_done, 1)
                if t < TT - 1:
                    act.wait_ge(fin_rstd, t + 1)
                    act.wait_ge(gained, t + 1)
                    act.activation(yg[:, t, 0, :], x1r[:, t, 0:D], ACT.Copy, scale=rs[:, t:t + 1]).then_inc(scaled, 1)

        @block.vector
        def _(dve):
            ch = Chain(dve, dve_chain)
            link = ch.link

            def rsqrt(v, root, r, tmp, n):
                dve.wait_ge(sqrt_done, n)
                link(dve.reciprocal(r, root))
                link(dve.tensor_tensor(tmp, r, r, ALU.mult))
                link(dve.scalar_tensor_tensor(out=tmp, in0=tmp, scalar=-0.5, in1=v, op0=ALU.mult, op1=ALU.mult))
                link(dve.scalar_tensor_tensor(out=r, in0=tmp, scalar=1.5, in1=r, op0=ALU.add, op1=ALU.mult))

            for t in range(TT):
                dve.wait_ge(x_in[t], 16 if t < TT - 1 else 32)
                link(dve.tensor_tensor_reduce(out=words(arena, O_MIX, D, TR), in0=x1r[:, t, 0:D], in1=x1r[:, t, 0:D],
                                              scale=1.0, scalar=0.0, op0=ALU.mult, op1=ALU.add, accum_out=ss[:, t:t + 1]))
            dve.tensor_scalar(va[:, :], ss[:, :], 1.0 / D, EPS, ALU.mult, ALU.add).then_inc(act_in, 1)

            def odd_copy(k):
                dve.wait_ge(xT_mm, k + 1)
                dve.tensor_copy(xTk[:, k, :], ps[k % 4][:, 0:NTOK]).then_inc(xT_ready[1], 1)

            for k in range(1, 7, 2):
                odd_copy(k)
            dve.wait_ge(act_in, 1)
            rsqrt(va[:, :], sq[:, :], rs[:, :], tn[:, :], 1)
            dve.wait_ge(const_ready, 1)
            for t in range(TT):
                last = dve.tensor_scalar(diag[:, t, :], ident[0:TR, 0:TR], rs[:, t:t + 1], None, ALU.mult)
            last.then_inc(diag_ready, 1)
            for k in range(7, KT, 2):
                odd_copy(k)
            dve.wait_ge(rbc_mm, 1)
            dve.wait_ge(pvT_ready, 1)
            for k in range(KT):
                dve.wait_ge(xT_ready[k % 2], k // 2 + 1)
                dve.scalar_tensor_tensor(out=hT[:, k, :], in0=xTk[:, k, :], scalar=pgm[:, k:k + 1], in1=ps[4][:, 0:NTOK],
                                         op0=ALU.mult, op1=ALU.mult).then_inc(hT_ready, 1)
            dve.wait_ge(wr_in, 32)
            for k in range(KT):
                last = dve.tensor_scalar(wr3[:, k, :], wr3[:, k, :], pgf[:, k:k + 1], None, ALU.mult)
            last.then_inc(wrs_ready, 1)
            with dve.Fori(0, 4) as g:
                for cc in range(2):
                    dve.wait_ge(g_evac, 2 * g + cc + 1)
                    dve.tensor_tensor(aw[:, cc, HC:AEXT], vw[:, cc, :], sg[:, cc, :], ALU.mult).then_inc(glu_ready, 1)
                dve.wait_ge(glu_ready, 2 * g + 2)
                dve.wait_ge(work_ready, g + 1)
                for w in range(W):
                    for cc in range(2):
                        src, dst = aw[:, cc, w:w + SEQ], acc[:, cc, 0:SEQ]
                        fin = dyn(arena, O_YC + (2 * g + cc) * NTOK, SEQ)
                        if w == 0:
                            ins = dve.tensor_scalar(dst, src, wdw[:, cc, 0:1], wdw[:, cc, W:W + 1], ALU.mult, ALU.add)
                        else:
                            dve.wait_ge(conv_chain, PERC * g + 2 * w + cc - 1)
                            ins = dve.scalar_tensor_tensor(out=(fin if w == W - 1 else dst), in0=src, scalar=wdw[:, cc, w:w + 1],
                                                           in1=dst, op0=ALU.mult, op1=ALU.add)
                        ins.then_inc(conv_chain, 1)
                dve.wait_ge(prod_ready, 2 * g + 2)
                for cc in range(2):
                    dve.tensor_reduce(acc[:, cc, SEQ:NTOK], prod[:, cc, :, :], AXX, ALU.add).then_inc(conv_chain, 1)
                for cc in range(2):
                    dve.wait_ge(conv_chain, PERC * g + 2 * W + cc + 1)
                    dve.tensor_scalar(dyn(arena, O_YC + (2 * g + cc) * NTOK + SEQ, NS), acc[:, cc, SEQ:NTOK],
                                      wdw[:, cc, W:W + 1], None, ALU.add).then_inc(conv_chain, 1)
                dve.wait_ge(conv_chain, PERC * g + PERC)
                dve.wait_ge(keep_ready, g + 1)
            dve.wait_ge(nmean_ready, 1)
            dve.wait_ge(conv_chain, 4 * PERC)
            dve.tensor_tensor(yc, yc, nmean[:, None, :].to_broadcast([P, CT, NTOK]), ALU.add).then_inc(centred, 1)
            dve.wait_ge(sumsq_mm, 1)
            dve.tensor_scalar(lnv[:, :], ps[5][:, 0:NTOK], 1.0 / DC, EPS, ALU.mult, ALU.add).then_inc(var_ready, 1)
            dve.wait_ge(var_ready, 1)
            dve.wait_ge(centred, 1)
            rsqrt(lnv[:, :], lnr[:, :], nmean[:, :], lnt[:, :], 2)
            dve.tensor_tensor(yc, yc, nmean[:, None, :].to_broadcast([P, CT, NTOK]), ALU.mult).then_inc(yn_ready, 1)
            for i in range(CT):
                dve.wait_ge(wp_mm, i + 1)
                dve.tensor_scalar(mixT[:, CT + i, :], ps[6 + i % 2][:, 0:NTOK], pps[:, i:i + 1], None, ALU.mult).then_inc(wp_ready, 1)
            dve.sem_inc(row_evac, 1)
            with dve.Fori(0, 4) as o:
                for q in range(4):
                    dve.wait_ge(o_mm, 4 * o + q + 1)
                    dve.tensor_tensor(x1wk[:, q, :], ps[q % 2][:, 0:NTOK], dyn(xT, (4 * o + q) * NTOK, NTOK),
                                      ALU.add).then_inc(x1_ready[q % 2], 1)
                for t in range(TT):
                    dve.wait_ge(act_chain, TT * o + t + 1)
                    dve.tensor_copy(x1r[:, t, bass.DynSlice(512 * o, 512)], ps[2 + t][0:TR, :]).then_inc(row_evac, 1)
            dve.wait_ge(act_chain, 4 * TT)
            link(dve.tensor_reduce(ss[:, :], ssp3, AXX, ALU.add))
            dve.tensor_scalar(va[:, :], ss[:, :], 1.0 / D, EPS, ALU.mult, ALU.add).then_inc(act_in, 1)
            dve.wait_ge(act_in, 2)
            rsqrt(va[:, :], sq[:, :], rs[:, :], tn[:, :], 3)
            dve.sem_inc(rstd_ready, 1)
            dve.wait_ge(router_mm, 1)
            dve.wait_ge(bias_in, 32)
            for t in range(TT):
                ch.step(dve.scalar_tensor_tensor(out=lg[:, t, :], in0=ps[5 + t][0:TR, 0:NR], scalar=rs[:, t:t + 1],
                                                 in1=bias[:, :], op0=ALU.mult, op1=ALU.add))
            dve.wait_ge(dve_chain, ch.n)
            gl = lg[:, :, 0:NG]

            def over(a, n):
                return a.to_broadcast([TR, TT, n])

            link(dve.tensor_reduce(g1[:, :, :], gl, AXX, ALU.max))
            dve.tensor_tensor(r4[:, :, :], gl, over(g1[:, :, :], NG), ALU.subtract).then_inc(act_in, 1)
            dve.wait_ge(act_in, 3)
            dve.wait_ge(const_ready, 3)
            iota4 = iof[:, None, 0:NG].to_broadcast([TR, TT, NG])
            iota32 = iof[:, None, 0:NE].to_broadcast([TR, TT, NE])

            def first(onehot, values, top, tmp, n, iota):
                link(dve.tensor_tensor(tmp, values, over(top, n), ALU.is_equal))
                link(dve.scalar_tensor_tensor(out=tmp, in0=tmp, scalar=-64.0, in1=iota, op0=ALU.mult, op1=ALU.add))
                link(dve.tensor_reduce(ix[:, :, :], tmp, AXX, ALU.min))
                link(dve.scalar_tensor_tensor(out=onehot, in0=iota, scalar=-64.0, in1=over(ix[:, :, :], n), op0=ALU.add, op1=ALU.is_equal))

            first(r4c[:, :, :], gl, g1[:, :, :], r4d[:, :, :], NG, iota4)
            link(dve.tensor_scalar(r4c[:, :, :], r4c[:, :, :], BIG, -BIG, ALU.mult, ALU.add))
            link(dve.tensor_tensor(sel[:, :, :].rearrange("p t (g e) -> p t g e", g=NG),
                                   r4c[:, :, :, None].to_broadcast([TR, TT, NG, EG]),
                                   lg[:, :, NG:NR].rearrange("p t (g e) -> p t g e", g=NG), ALU.add))
            link(dve.tensor_reduce(m1[:, :, :], sel[:, :, :], AXX, ALU.max))
            first(oh1[:, :, :], sel[:, :, :], m1[:, :, :], ra[:, :, :], NE, iota32)
            link(dve.scalar_tensor_tensor(out=sel[:, :, :].rearrange("p t e -> p (t e)"), in0=oh1[:, :, :].rearrange("p t e -> p (t e)"),
                                          scalar=-2 * BIG, in1=sel[:, :, :].rearrange("p t e -> p (t e)"), op0=ALU.mult, op1=ALU.add))
            link(dve.tensor_reduce(m2[:, :, :], sel[:, :, :], AXX, ALU.max))
            dve.tensor_tensor(dl[:, :, :], m2[:, :, :], m1[:, :, :], ALU.subtract).then_inc(act_in, 1)
            first(oh2[:, :, :], sel[:, :, :], m2[:, :, :], ra[:, :, :], NE, iota32)
            dve.tensor_tensor(pick[:, :, :], oh1[:, :, :], oh2[:, :, :], ALU.add).then_inc(pick_ready, 1)
            dve.wait_ge(rank_mm, 1)
            ch.step(dve.tensor_copy(rk_i[:, 0:TT * NE], ps[0][0:TR, 0:TT * NE]))
            ch.step(dve.tensor_copy(rank[:, :, :].rearrange("p t e -> p (t e)"), ps[0][0:TR, 0:TT * NE]))
            link(dve.tensor_scalar(rk_i[:, TT * NE:], ps[0][0:TR, TT * NE:(TT + 1) * NE], -1.0, 0.0, ALU.add, ALU.max))
            link(dve.tensor_scalar(rk_i[:, :], rk_i[:, :], CAP.bit_length() - 1, None, ALU.logical_shift_right))
            link(dve.tensor_copy(rq[:, :, :].rearrange("p t e -> p (t e)"), rk_i[:, :]))
            rb, nov = rq[:, 0:TT, :], rq[:, TT, :]
            src, at, sh = nov, 0, 1
            while sh < NE:
                ch.step(dve.tensor_copy(cs[:, at, 0:sh], src[:, 0:sh]))
                link(dve.tensor_tensor(cs[:, at, sh:NE], src[:, sh:NE], src[:, 0:NE - sh], ALU.add))
                src, at, sh = cs[:, at, :], 1 - at, 2 * sh
            incl = src
            link(dve.tensor_tensor(cnt[:, :], incl, nov, ALU.subtract))
            link(dve.scalar_tensor_tensor(out=cnt[:, :], in0=cnt[:, :], scalar=float(NE - 1), in1=iof[:, 0:NE], op0=ALU.add, op1=ALU.subtract))
            link(dve.tensor_tensor(ra[:, :, :], rb, cnt[:, None, :].to_broadcast([TR, TT, NE]), ALU.add))
            link(dve.scalar_tensor_tensor(out=ra[:, :, :], in0=rb, scalar=0.0, in1=ra[:, :, :], op0=ALU.is_gt, op1=ALU.mult))
            ch.step(dve.tensor_tensor(ra[:, :, :], ra[:, :, :], iota32, ALU.add))
            link(dve.scalar_tensor_tensor(out=rc[:, :, :], in0=rb, scalar=-float(CAP), in1=rank[:, :, :], op0=ALU.mult, op1=ALU.add))
            link(dve.scalar_tensor_tensor(out=ra[:, :, :], in0=ra[:, :, :], scalar=float(BLK), in1=rc[:, :, :], op0=ALU.mult, op1=ALU.add))
            ch.step(dve.tensor_tensor(rc[:, :, :], ra[:, :, :], oh1[:, :, :], ALU.mult))
            link(dve.tensor_tensor(rc2[:, :, :], ra[:, :, :], oh2[:, :, :], ALU.mult))
            ch.step(dve.tensor_reduce(slot[:, 0, :], rc[:, :, :], AXX, ALU.add))
            link(dve.tensor_reduce(slot[:, 1, :], rc2[:, :, :], AXX, ALU.add))
            C6 = 2 * TT
            link(dve.tensor_copy(slot_i[:, :], slot[:, :, :].rearrange("p c t -> p (c t)")))
            ch.step(dve.tensor_scalar(cut_i[:, 0:C6], slot_i[:, :], P - 1, None, ALU.bitwise_and))
            ch.step(dve.tensor_scalar(cut_i[:, C6:2 * C6], slot_i[:, :], 7, None, ALU.logical_shift_right))
            link(dve.tensor_scalar(cut_i[:, 2 * C6:], slot_i[:, :], 6, None, ALU.logical_shift_right))
            link(dve.tensor_copy(cut[:, :, :].rearrange("p c o -> p (c o)"), cut_i[:, :]))
            lo, hi, blk = cut[:, 0:C6, :], cut[:, C6:2 * C6, :], cut[:, 2 * C6:, :]

            def spread(v, n):
                return v.rearrange("p c t -> p (c t)")[:, :, None].to_broadcast([TR, C6, n])

            ch.step(dve.tensor_tensor(ohl, iof[:, None, 0:P].to_broadcast([TR, C6, P]), lo.to_broadcast([TR, C6, P]), ALU.is_equal))
            link(dve.tensor_tensor(ohh, iof[:, None, 0:NCOL].to_broadcast([TR, C6, NCOL]), hi.to_broadcast([TR, C6, NCOL]), ALU.is_equal))
            dve.tensor_tensor(ohh, ohh, spread(tsrc[:, :, :], NCOL), ALU.mult).then_inc(oh_ready, 1)
            dve.wait_ge(tab_mm, 1)
            dve.tensor_scalar(tab_i[:, 0:1], ps[1][:, 0:1], float(PAD), float(NTOK - 1), ALU.add, ALU.min).then_inc(route_ready, 1)
            dve.tensor_scalar(tab_i[:, 1:NCOL], ps[1][:, 1:NCOL], float(PAD), None, ALU.add).then_inc(route_ready, 1)
            ch.step(dve.tensor_tensor(ohb, iof[:, None, 0:NBLK].to_broadcast([TR, C6, NBLK]), blk.to_broadcast([TR, C6, NBLK]), ALU.is_equal))
            link(dve.tensor_tensor(ohw[:, :, 0:BLK], ohl[:, :, 0:BLK], ohl[:, :, BLK:P], ALU.add))
            ch.step(dve.tensor_copy(ohw[:, :, BLK:P], ohw[:, :, 0:BLK]))
            dve.tensor_tensor(ohb, ohb, spread(cdst[:, :, :], NBLK), ALU.mult).then_inc(oh_ready, 1)
            dve.wait_ge(tab_mm, 2)
            dve.wait_ge(const_ready, 3)
            dve.tensor_scalar(dst_i[:, :], ps[7][:, 0:NBLK], half[:, :], float(PAD), ALU.add, ALU.add).then_inc(dst_ready, 1)

            def rest_of_routing():
                dve.wait_ge(exp_done, 2)
                link(dve.tensor_reduce(g2[:, :, :], r4b[:, :, :], AXX, ALU.add))
                link(dve.reciprocal(pg[:, :, :], g2[:, :, :]))
                link(dve.tensor_scalar(den[:, :, :], ex[:, :, :], 1.0, None, ALU.add))
                link(dve.reciprocal(den[:, :, :], den[:, :, :]))
                w0, w1 = wt[:, 0, :][:, :, None], wt[:, 1, :][:, :, None]
                link(dve.tensor_tensor(w0, den[:, :, :], pg[:, :, :], ALU.mult))
                link(dve.tensor_tensor(w1, w0, ex[:, :, :], ALU.mult))
                link(dve.tensor_tensor(ecmp[:, :, :], incl[:, None, :].to_broadcast([TR, 2 * OVP, NE]),
                                       iof[:, 0:2 * OVP, None].to_broadcast([TR, 2 * OVP, NE]), ALU.is_le))
                link(dve.tensor_reduce(eid[:, :, :], ecmp[:, :, :], AXX, ALU.add))
                ch.step(dve.tensor_scalar(eid_i[:, 0:2 * OVP], eid[:, :, :].rearrange("p j o -> p (j o)"), float(NE - 1), None, ALU.min))
                dve.wait_ge(dve_chain, ch.n)
                dve.tensor_copy(eid_i[:, 2 * OVP:2 * OVP + 1], incl[:, NE - 1:NE]).then_inc(over_ready, 1)

            rest_of_routing()

            def last_norm(t):
                dve.wait_ge(act_chain, 4 * TT + t + 2)
                dve.tensor_scalar(va[:, t:t + 1], ss[:, t:t + 1], 1.0 / D, EPS, ALU.mult, ALU.add).then_inc(act_in, 1)
                dve.wait_ge(act_in, 5 + t)
                rsqrt(va[:, t:t + 1], sq[:, t:t + 1], rs[:, t:t + 1], tn[:, t:t + 1], 4 + t)
                dve.sem_inc(fin_rstd, 1)
                if t == TT - 1:
                    dve.wait_ge(gfin_in, 16)
                    dve.scalar_tensor_tensor(out=yg[:, t, 0, :], in0=yg[:, t, 0, :], scalar=rs[:, t:t + 1], in1=gfin,
                                             op0=ALU.mult, op1=ALU.mult).then_inc(out_ready, 1)

            def pair(i):
                dve.wait_ge(xg_in, 16 * i + 16)
                dve.tensor_scalar(xgs, xg[:, 0:D], xg[:, D:D + 1], None, ALU.mult).then_inc(xs_ready, 1)
                for b in range(4):
                    dve.wait_ge(xgT_mm, 4 * i + b + 1)
                    dve.tensor_tensor(xgT[:, 4 * b:4 * b + 4, :], ps[b % 2][:, :].rearrange("p (k s) -> p k s", k=4),
                                      pgf[:, 4 * b:4 * b + 4, None].to_broadcast([P, 4, P]), ALU.mult).then_inc(xgT_ready, 1)
                for s in range(2):
                    n = 2 * i + s
                    dve.wait_ge(sl_ready, n + 1)
                    dve.tensor_tensor(a_sb[:, :], sl_sb[:, :], ps[4 + s][:, 256:512], ALU.mult).then_inc(a_ready, 1)
                    dve.wait_ge(wd_used, 4 * n + 4)
                    dve.tensor_copy(ysb[:, s, 512:1024], ps[3][:, :]).then_inc(y1_ready, 1)

            with dve.Fori(0, PAIRS) as i:
                pair(i)
            dve.wait_ge(over_ready, 1)
            n_over = dve.value_load(eid_i[0:1, 2 * OVP:2 * OVP + 1], min_val=0, max_val=2 * OVP)
            with dve.Fori(0, OVP) as j:
                with dve.If(n_over > 2 * j):
                    pair(PAIRS + j)
            for t in range(TT):
                a, b = yg[:, t, 0, :], yg[:, t, 1, :]
                dve.wait_ge(yg_in[t], 16)
                link(dve.scalar_tensor_tensor(out=a, in0=a, scalar=wt[:, 0, t:t + 1], in1=x1r[:, t, 0:D], op0=ALU.mult, op1=ALU.add))
                dve.scalar_tensor_tensor(out=a, in0=b, scalar=wt[:, 1, t:t + 1], in1=a, op0=ALU.mult, op1=ALU.add).then_inc(fin_sum, 1)
                if t:
                    last_norm(t - 1)
            last_norm(TT - 1)

        @block.gpsimd
        def _(pool):
            ch = Chain(pool, pool_chain)
            link = ch.link
            link(pool.memset(ident[:, :], 0.0))
            pool.affine_select(out=ident[:, :], in_=ident[:, :], compare_op=ALU.not_equal, fill=1.0, base=0,
                               pattern=[[-1, P]], channel_multiplier=1).then_inc(const_ready, 1)
            pool.wait_ge(const_ready, 1)
            pool.memset(ones[:, :], 1.0).then_inc(const_ready, 1)
            pool.dma_start(wdr, w_dw[0]).then_inc(wdr_in, 16)
            srow = state_conv[0].rearrange("s t c -> (s t) c")
            for a in range(2):
                pool.dma_start(crow[:, a, :], srow[120 * a:120 * (a + 1), :]).then_inc(st_in, 16)
            pool.dma_start(prow, state_pool[0].rearrange("s t c -> (s t) c")).then_inc(st_in, 16)
            pool.dma_start(wr3[:, :, 0:NG], w_rg[0].rearrange("(k p) c -> p k c", p=P)).then_inc(wr_in, 16)
            pool.dma_start(wr3[:, :, NG:NR], w_re[0].rearrange("(k p) c -> p k c", p=P)).then_inc(wr_in, 16)
            pool.dma_start(bias[:, 0:NG], b_rg[0:1, :].to_broadcast([TR, NG])).then_inc(bias_in, 16)
            pool.dma_start(bias[:, NG:NR], b_re[0:1, :].to_broadcast([TR, NE])).then_inc(bias_in, 16)
            pool.dma_start(conv_s[0, :, 0:HC - SLEN, :], state_conv[0, :, SLEN:HC, :]).then_inc(old_out, 16)
            pool.dma_start(pool_s[0, :, 0:HP - SLEN, :], state_pool[0, :, SLEN:HP, :]).then_inc(old_out, 16)

            link(pool.memset(aw[:, :, 0:HC], 0.0))
            link(pool.memset(uline[:, :, 0:HP], 0.0))
            link(pool.memset(zero[:, :], 0.0))
            for t in range(HP):
                ch.step(pool.memset(rcol[:, t:t + 1], 1.0 / (t + 1)))
            link(pool.memset(earlier[:, :], 1.0))
            link(pool.affine_select(out=earlier[:, :], in_=earlier[:, :], compare_op=ALU.is_gt, fill=0.0, base=0,
                                    pattern=[[1, TR]], channel_multiplier=-1))
            link(pool.iota(io_i[:, :], pattern=[[1, P]], base=0, channel_multiplier=0))
            link(pool.tensor_copy(iof[:, :], io_i[:, :]))
            link(pool.iota(tid_i[:, :], pattern=[[TR, TT]], base=0, channel_multiplier=1))
            for c in range(2):
                link(pool.tensor_scalar(tsrc[:, c, :], tid_i[:, :], float(-PAD), None, ALU.add))
                link(pool.tensor_scalar(cdst[:, c, :], tid_i[:, :], 4.0, float(2 * c - PAD), ALU.mult, ALU.add))
            link(pool.memset(half[0:BLK, :], 0.0))
            link(pool.memset(half[BLK:P, :], 1.0))
            pool.wait_ge(const_ready, 2)
            pool.sem_inc(const_ready, 1)
            pool.wait_ge(wdT_ready, 2)
            pool.wait_ge(hist_ready, 4)
            with pool.Fori(0, 4) as g:
                ch.loop(g, 1)
                pool.tensor_copy(wdw[:, :, :], dyn(wdT, 64 * g, 64).rearrange("p (c w) -> p c w", c=2))
                pool.tensor_copy(hw[:, :, :, 0:HC], dyn(arena, O_HIST + 2 * NSEQ * HC * g, 2 * NSEQ * HC)
                                 .rearrange("p (c s t) -> p c s t", c=2, s=NSEQ)).then_inc(work_ready, 1)
                pool.wait_ge(glu_ready, 2 * g + 2)
                pool.sem_inc(waited, 1)
                link(pool.tensor_copy(hw[:, :, :, HC:HC + SLEN], aw[:, :, HC + SEQ:AEXT].rearrange("p c (s t) -> p c s t", s=NSEQ)))
                for cc in range(2):
                    first_taps = hw[:, cc, :, 0:SLEN]
                    windows = bass.AP(first_taps.tensor, first_taps.offset, [first_taps.ap[0], [HC + SLEN, NSEQ], [1, SLEN], [1, W]])
                    taps = wdw[:, cc, 0:W][:, None, None, :].to_broadcast([P, NSEQ, SLEN, W])
                    pool.tensor_tensor(prod[:, cc, :, :].rearrange("p (s t) w -> p s t w", s=NSEQ), windows, taps,
                                       ALU.mult).then_inc(prod_ready, 1)
                pool.tensor_copy(dyn(arena, O_AK + 2 * AK * g, 2 * AK).rearrange("p (c t) -> p c t", c=2),
                                 aw[:, :, AEXT - AK:AEXT]).then_inc(keep_ready, 1)
                pool.wait_ge(conv_chain, PERC * (g + 1))
            ch.end(4)
            for m in range(NG):
                g = NG - 1 - m
                pool.wait_ge(u_evac[m % 2], 2 * (m // 2) + 2)
                x = uline[:, 2 * g:2 * g + 2, :]
                src, n = x, 1
                for step in range(g + 1):
                    dst = ws[:, step % 2, :, :]
                    lo_ = 2 * n - 1
                    link(pool.tensor_tensor(dst[:, :, lo_:ULINE], src[:, :, lo_:ULINE], src[:, :, lo_ - n:ULINE - n], ALU.add))
                    src, n = dst, 2 * n
                ch.step(pool.tensor_tensor(src[:, :, HP:HP + n - 1], src[:, :, HP:HP + n - 1],
                                           rcol[:, None, 0:n - 1].to_broadcast([P, 2, n - 1]), ALU.mult))
                link(pool.tensor_scalar(src[:, :, HP + n - 1:ULINE], src[:, :, HP + n - 1:ULINE], 1.0 / n, 1.0, ALU.mult, ALU.mult))
                ch.step(pool.tensor_tensor(sT[:, 2 * g:2 * g + 2, 0:SEQ], src[:, :, HP:SM0], x[:, :, HP:SM0], ALU.subtract))
                for a in range(2):
                    new = [v[:, a, SM0:ULINE].rearrange("p (s t) -> p s t", s=NSEQ)[:, :, HP:HP + SLEN] for v in (src, x)]
                    ins = pool.tensor_tensor(sT[:, 2 * g + a, SEQ:NTOK].rearrange("p (s t) -> p s t", s=NSEQ), new[0], new[1], ALU.subtract)
                    ins.then_inc(s_ready, 1)
                pool.wait_ge(s_ready, 2 * m + 2)
            pool.wait_ge(o_mm, KT)
            for t in range(TT):
                pool.wait_ge(rows_out[t], 16 * 5)

            def gather(i):
                pool.tensor_copy(cur_i[:, :], dyn(tab_i, i, 1)).then_inc(cur_ready, 1)
                pool.wait_ge(cur_ready, i + 1)
                pool.sem_inc(waited, 1)
                pool.indirect_dma_start(out=xg, out_offset=None, in_=rows_dram,
                                        in_offset=bass.IndirectOffsetOnAxis(ap=cur_i[:, 0:1], axis=0),
                                        bounds_check=NTOK - 1, oob_is_err=False).then_inc(xg_in, 16)

            def scatter(i):
                for s in range(2):
                    n = 2 * i + s
                    if not (isinstance(i, int) and i == 0):
                        pool.wait_ge(y_out[s], 16 * i)
                    pool.sem_inc(ysb_free[s], 1)
                    pool.tensor_copy(cur_d[:, s:s + 1], dyn(dst_i, n, 1)).then_inc(dcur_ready, 1)
                    pool.wait_ge(dcur_ready, n + 1)
                    pool.wait_ge(y0_ready, n + 1)
                    pool.wait_ge(y1_ready, n + 1)
                    pool.sem_inc(waited, 1)
                    pool.indirect_dma_start(out=yexp_dram, out_offset=bass.IndirectOffsetOnAxis(ap=cur_d[:, s:s + 1], axis=0),
                                            in_=ysb[:, s, :], in_offset=None,
                                            bounds_check=4 * NTOK - 1, oob_is_err=False).then_inc(y_out[s], 16)

            pool.wait_ge(route_ready, 1)
            gather(0)
            pool.wait_ge(route_ready, 2)
            pool.wait_ge(dst_ready, 1)

            def gather_next(i):
                pool.wait_ge(xs_ready, i)
                pool.sem_inc(waited, 1)
                gather(i)

            gather_next(1)
            scatter(0)
            with pool.Fori(2, PAIRS) as i:
                gather_next(i)
                scatter(i - 1)
            scatter(PAIRS - 1)
            pool.wait_ge(over_ready, 1)
            n_over = pool.value_load(eid_i[0:1, 2 * OVP:2 * OVP + 1], min_val=0, max_val=2 * OVP)
            with pool.Fori(0, OVP) as j:
                with pool.If(n_over > 2 * j):
                    gather_next(PAIRS + j)
                    scatter(PAIRS + j)
            pool.wait_ge(gfin_in, 16)
            for t in range(TT - 1):
                pool.wait_ge(fin_sum, t + 1)
                pool.tensor_tensor(x1r[:, t, 0:D], yg[:, t, 0, :], gfin, ALU.mult).then_inc(gained, 1)


_INS = ["x_prompt", "x_sample", "state_conv", "state_pool", "g_mix", "w_in", "w_dw", "b_dw", "ln_g", "ln_b", "w_pool",
        "pool_scale", "w_out", "g_ffn", "w_rg", "b_rg", "w_re", "b_re", "w_gate", "w_up", "w_down", "g_final"]
_OUTS = [(1, SEQ, D), (NSEQ, SLEN, D), (1, 1, HC, DC), (1, NSEQ, HC, DC), (1, 1, HP, DC), (1, NSEQ, HP, DC)]


def kernel(**inputs):
    import numpy as _np
    import concourse.bacc as _bacc
    from concourse import mybir as _mybir
    from concourse.bass_utils import run_bass_kernel_spmd as _run

    nc = _bacc.Bacc("TRN2", target_bir_lowering=False, num_devices=1)
    arrays, args = {}, []
    for name in _INS:
        a = _np.ascontiguousarray(inputs[name])
        arrays[f"in_{name}_dram"] = a
        args.append(nc.dram_tensor(f"in_{name}_dram", a.shape, _mybir.dt.from_np(a.dtype), kind="ExternalInput").ap())
    for i, shape in enumerate(_OUTS):
        args.append(nc.dram_tensor(f"out_{i}_dram", shape, _mybir.dt.float32, kind="ExternalOutput").ap())
    hybrid_decoder_step(nc, *args)
    r = _run(nc, [arrays], core_ids=[0])
    return tuple(r.results[0][f"out_{i}_dram"] for i in range(len(_OUTS)))
```

```python
import concourse.bass as bass
from concourse import mybir
from contextlib import ExitStack

F32 = mybir.dt.float32
I32 = mybir.dt.int32
ALU = mybir.AluOpType
ACT = mybir.ActivationFunctionType
AXX = mybir.AxisListType.X

P = 128
D = 2048
KT = D // P
SEQ, NSEQ, SLEN = 256, 8, 4
NS = NSEQ * SLEN
NTOK = SEQ + NS
TR = 96
TT = NTOK // TR
LASTP = SEQ - 2 * TR
CT = 8
DC = CT * P
W, HC = 31, 30
PERC = 2 * W + 4
HP = 15
AEXT = HC + NTOK
ULINE = HP + SEQ + NSEQ * (HP + SLEN)
SM0 = HP + SEQ
NE, NG, EG = 32, 4, 8
FE = 512
NR = NG + NE
EPS = 1e-6
BIG = 1e30

BLK = 64
CAP = 64
OVP = (2 * NTOK // CAP + 1) // 2
PAIRS = NE // 2
NBLK = 2 * (PAIRS + OVP)
PAD = 4096

AWAKE_START = (6, 10, 8)
AWAKE_ROUTE = (40, 18)
SELB = (0, 1, 7, 0)

GU_WORDS = KT * 2 * FE
WD_WORDS = (FE // P) * D
O_HT = 0
O_UL = O_HT + KT * NTOK
O_HIST = O_UL + CT * ULINE
O_ST = O_HIST + CT * NSEQ * HC
O_PROW = O_ST + CT * NTOK
O_AW = O_PROW + DC
O_HW = O_AW + 2 * AEXT
O_ACC = O_HW + 2 * NSEQ * (HC + SLEN)
O_VW = O_ACC + 2 * NTOK
O_SG = O_VW + 2 * NTOK
assert O_SG + 2 * NTOK <= GU_WORDS and CT * NTOK <= GU_WORDS - O_AW
O_MIX = GU_WORDS
O_WDR = O_MIX + CT * NTOK
O_WS = O_HIST
assert 4 * ULINE <= CT * NSEQ * HC
O_YC = O_MIX + KT * NTOK
O_AK = O_YC + CT * NTOK
AK = HC + NS
UK = HP + NS
O_UK = O_AK + CT * AK
assert 3 * TT * P <= 4 * NTOK and 2 * TT * NBLK <= KT * NR
assert D <= CT * NTOK and O_YC <= GU_WORDS + 3 * D
assert O_UK + CT * UK <= GU_WORDS + WD_WORDS

WSLOT = KT * 2 * P


class Chain:

    def __init__(self, engine, sem):
        self.engine, self.sem, self.base, self.n = engine, sem, 0, 0

    def step(self, ins):
        ins.then_inc(self.sem, 1)
        self.n += 1

    def link(self, ins):
        self.step(ins)
        self.engine.wait_ge(self.sem, self.base + self.n)

    def loop(self, i, per):
        self.start, self.per = self.base + self.n, per
        self.base, self.n = self.start + i * per, 0

    def end(self, times):
        assert self.n == self.per, (self.n, self.per)
        self.base, self.n = self.start + times * self.per, 0


def hybrid_decoder_step(nc, x_prompt, x_sample, state_conv, state_pool, g_mix, w_in, w_dw, b_dw, ln_g, ln_b,
                        w_pool, pool_scale, w_out, g_ffn, w_rg, b_rg, w_re, b_re, w_gate, w_up, w_down,
                        g_final, y_prompt, y_sample, conv_p, conv_s, pool_p, pool_s):
    ctx = ExitStack()
    with ctx:
        def sb(name, shape, dt=F32):
            return ctx.enter_context(nc.sbuf_tensor(name, shape, dt))

        def sem(name):
            return ctx.enter_context(nc.semaphore(name))

        yexp_dram = nc.dram_tensor("expert_rows", [NTOK * 4, D // 2], F32).ap()

        arena = sb("arena", [P, GU_WORDS + WD_WORDS])
        stage = sb("stage", [P, 2 * WSLOT])
        x1r = sb("x1r", [TR, TT, D])
        xT = sb("xT", [P, KT * NTOK])
        ysb = sb("ysb", [P, 2, 2 * FE])
        x1w = sb("x1w", [P, 4 * NTOK])
        wr = sb("wr", [P, KT * NR])
        ident = sb("ident", [P, P])
        ones = sb("ones", [P, P])
        earlier = sb("earlier", [TR, TR])
        pv = sb("pv", [64, P])
        pvT = sb("pvT", [P, 64])
        wdT = sb("wdT", [P, CT * 32])
        wdw = sb("wdw", [P, 2, 32])
        rcol = sb("rcol", [P, 16])
        nmean = sb("nmean", [P, NTOK])
        lnv = sb("lnv", [P, NTOK])
        lnr = sb("lnr", [P, NTOK])
        lnt = sb("lnt", [P, NTOK])
        a_sb = sb("a_sb", [P, 256])
        sl_sb = sb("sl_sb", [P, 256])
        aT = sb("aT", [P, 256])
        ss = sb("ss", [TR, TT])
        ssp = sb("ssp", [TR, TT * 4])
        va = sb("va", [TR, TT])
        sq = sb("sq", [TR, TT])
        rs = sb("rs", [TR, TT])
        tn = sb("tn", [TR, TT])
        zero = sb("zero", [P, TR])
        lg = sb("lg", [TR, TT, NR])
        bias = sb("bias", [TR, NR])
        io_i = sb("io_i", [TR, P], I32)
        iof = sb("iof", [TR, P])
        tid_i = sb("tid_i", [TR, TT], I32)
        r4 = sb("r4", [TR, TT, NG])
        r4b = sb("r4b", [TR, TT, NG])
        r4c = sb("r4c", [TR, TT, NG])
        r4d = sb("r4d", [TR, TT, NG])
        g1 = sb("g1", [TR, TT, 1])
        g2 = sb("g2", [TR, TT, 1])
        pg = sb("pg", [TR, TT, 1])
        m1 = sb("m1", [TR, TT, 1])
        m2 = sb("m2", [TR, TT, 1])
        ix = sb("ix", [TR, TT, 1])
        dl = sb("dl", [TR, TT, 1])
        ex = sb("ex", [TR, TT, 1])
        den = sb("den", [TR, TT, 1])
        wt = sb("wt", [TR, 2, TT])
        sel = sb("sel", [TR, TT, NE])
        ra = sb("ra", [TR, TT, NE])
        rc = sb("rc", [TR, TT, NE])
        oh1 = sb("oh1", [TR, TT, NE])
        oh2 = sb("oh2", [TR, TT, NE])
        pick = sb("pick", [TR, TT, NE])
        rank = sb("rank", [TR, TT, NE])
        cnt = sb("cnt", [TR, NE])
        rk_i = sb("rk_i", [TR, (TT + 1) * NE], I32)
        rq = sb("rq", [TR, TT + 1, NE])
        rc2 = sb("rc2", [TR, TT, NE])
        cs = sb("cs", [TR, 2, NE])
        slot = sb("slot", [TR, 2, TT])
        slot_i = sb("slot_i", [TR, 2 * TT], I32)
        cut_i = sb("cut_i", [TR, 2 * 2 * TT], I32)
        cut = sb("cut", [TR, 2 * 2 * TT, 1])
        dst_i = sb("dst_i", [P, NBLK], I32)
        cur_d = sb("cur_d", [P, 2], I32)
        half = sb("half", [P, 1])
        cdst = sb("cdst", [TR, 2, TT])
        ecmp = sb("ecmp", [TR, 2 * OVP, NE])
        eid = sb("eid", [TR, 2 * OVP, 1])
        eid_i = sb("eid_i", [TR, 2 * OVP + 1], I32)

        ps = [ctx.enter_context(nc.psum_tensor(f"bank{b}", [P, 512], F32)) for b in range(8)]

        def words(t, off, n, parts=P):
            return t[0:parts, off:off + n]

        def dyn(t, off, n, parts=P):
            return t[0:parts, bass.DynSlice(off, n)]

        hT = words(arena, O_HT, KT * NTOK).rearrange("p (k t) -> p k t", k=KT)
        uline = words(arena, O_UL, CT * ULINE).rearrange("p (j t) -> p j t", j=CT)
        crow = words(arena, O_ST, 2 * DC, 120).rearrange("p (a c) -> p a c", a=2)
        prow = words(arena, O_PROW, DC, 120)
        prod = words(arena, O_ST, 2 * NS * W).rearrange("p (c t w) -> p c t w", c=2, t=NS)
        sT = words(arena, O_ST, CT * NTOK).rearrange("p (j t) -> p j t", j=CT)
        aw = words(arena, O_AW, 2 * AEXT).rearrange("p (c t) -> p c t", c=2)
        hw = words(arena, O_HW, 2 * NSEQ * (HC + SLEN)).rearrange("p (c s t) -> p c s t", c=2, s=NSEQ)
        acc = words(arena, O_ACC, 2 * NTOK).rearrange("p (c t) -> p c t", c=2)
        vw = words(arena, O_VW, 2 * NTOK).rearrange("p (c t) -> p c t", c=2)
        sg = words(arena, O_SG, 2 * NTOK).rearrange("p (c t) -> p c t", c=2)
        sqw = words(arena, O_AW, CT * NTOK).rearrange("p (j t) -> p j t", j=CT)
        mixT = words(arena, O_MIX, KT * NTOK).rearrange("p (k t) -> p k t", k=KT)
        ws = words(arena, O_WS, 4 * ULINE).rearrange("p (a j t) -> p a j t", a=2, j=2)
        yc = words(arena, O_YC, CT * NTOK).rearrange("p (j t) -> p j t", j=CT)
        ak = words(arena, O_AK, CT * AK).rearrange("p (j t) -> p j t", j=CT)
        uk = words(arena, O_UK, CT * UK).rearrange("p (j t) -> p j t", j=CT)
        strow = words(arena, O_HT, 2 * DC, AK).rearrange("p (a c) -> p a c", a=2)
        wgu = words(arena, 0, GU_WORDS).rearrange("p (k g f) -> p k g f", k=KT, g=2)
        wdn = [[words(arena, GU_WORDS + q * D, D) for q in range(4)],
               [words(xT, 0, D), words(xT, D, D), words(stage, 2 * D, D), words(stage, 3 * D, D)]]
        wgu_first = words(stage, D, D).rearrange("p (k g f) -> p k g f", k=2, g=2)
        wsl = [words(stage, a * WSLOT, WSLOT).rearrange("p (k c) -> p k c", k=KT) for a in range(2)]
        xgT = words(stage, 0, D).rearrange("p (k s) -> p k s", k=KT)
        xTk = xT[:, :].rearrange("p (k t) -> p k t", k=KT)
        gfin = words(arena, 2 * TT * D, D, TR)
        yg = words(arena, 0, 2 * TT * D, TR).rearrange("p (t c d) -> p t c d", t=TT, c=2)
        wdr = words(arena, O_WDR, DC, W)
        diag = words(x1w, 0, TT * TR, TR).rearrange("p (t c) -> p t c", t=TT)
        ohw = words(x1w, 0, 2 * TT * P, TR).rearrange("p (c s) -> p c s", c=2 * TT)
        hot = words(x1w, 2 * TT * P, TT * P, TR).rearrange("p (t s) -> p t s", t=TT)
        hot0 = words(x1w, 0, TT * P, TR).rearrange("p (t s) -> p t s", t=TT)
        ohb = words(wr, 0, 2 * TT * NBLK, TR).rearrange("p (c s) -> p c s", c=2 * TT)
        x1wk = x1w[:, :].rearrange("p (k t) -> p k t", k=4)
        wr3 = wr[:, :].rearrange("p (k c) -> p k c", k=KT)
        wdT3 = wdT[:, :].rearrange("p (j w) -> p j w", j=CT)
        ssp3 = ssp[:, :].rearrange("p (t o) -> p t o", t=TT)
        pgm, pgf, pbd, plg, plb, pps = (pvT[:, a:b] for a, b in ((0, 16), (16, 32), (32, 40), (40, 48), (48, 56), (56, 64)))

        x_in = [sem(f"x_in{t}") for t in range(TT)]
        pv_in = sem("pv_in")
        wdr_in = sem("wdr_in")
        st_in = sem("st_in")
        wr_in = sem("wr_in")
        bias_in = sem("bias_in")
        gfin_in = sem("gfin_in")
        slot_in = [sem(f"slot_in{a}") for a in range(2)]
        first_in = sem("first_in")
        gu_in = [sem(f"gu_in{c}") for c in range(4)]
        wd_in = [[sem(f"wd_in{s}{q}") for q in range(4)] for s in range(2)]
        st_out = sem("st_out")
        old_out = sem("old_out")
        y_out = [sem(f"y_out{s}") for s in range(2)]
        fin_out = sem("fin_out")
        prod_ready = sem("prod_ready")
        const_ready = sem("const_ready")
        pool_chain = sem("pool_chain")
        work_ready = sem("work_ready")
        keep_ready = sem("keep_ready")
        s_ready = sem("s_ready")
        dcur_ready = sem("dcur_ready")
        ysb_free = [sem(f"ysb_free{s}") for s in range(2)]
        scattered = sem("scattered")
        waited = sem("waited")
        yg_in = [sem(f"yg_in{t}_{c}") for t in range(TT) for c in range(2)]
        pvT_mm = sem("pvT_mm")
        xT_mm = sem("xT_mm")
        rbc_mm = sem("rbc_mm")
        wdT_mm = sem("wdT_mm")
        hist_mm = sem("hist_mm")
        vg_mm = sem("vg_mm")
        u_mm = sem("u_mm")
        sum_mm = sem("sum_mm")
        sumsq_mm = sem("sumsq_mm")
        st_mm = sem("st_mm")
        wp_mm = sem("wp_mm")
        o_mm = sem("o_mm")
        row_mm = sem("row_mm")
        router_mm = sem("router_mm")
        rank_mm = sem("rank_mm")
        tab_mm = sem("tab_mm")
        xgT_mm = sem("xgT_mm")
        gu_used = sem("gu_used")
        at_mm = sem("at_mm")
        wd_used = sem("wd_used")
        pvT_ready = sem("pvT_ready")
        xT_ready = [sem(f"xT_ready{a}") for a in range(2)]
        wdT_ready = sem("wdT_ready")
        hist_ready = sem("hist_ready")
        v_evac = sem("v_evac")
        g_evac = sem("g_evac")
        u_evac = [sem("u_evac0"), sem("u_evac1")]
        sqrt_done = sem("sqrt_done")
        nmean_ready = sem("nmean_ready")
        sq_ready = sem("sq_ready")
        st_ready = sem("st_ready")
        wp_ready = sem("wp_ready")
        mix_ready = sem("mix_ready")
        row_evac = sem("row_evac")
        exp_done = sem("exp_done")
        sl_ready = sem("sl_ready")
        aT_ready = sem("aT_ready")
        y0_ready = sem("y0_ready")
        act_chain = sem("act_chain")
        dve_chain = sem("dve_chain")
        conv_chain = sem("conv_chain")
        diag_ready = sem("diag_ready")
        hT_ready = sem("hT_ready")
        glu_ready = sem("glu_ready")
        centred = sem("centred")
        var_ready = sem("var_ready")
        yn_ready = sem("yn_ready")
        wrs_ready = sem("wrs_ready")
        x1_ready = [sem("x1_ready0"), sem("x1_ready1")]
        act_in = sem("act_in")
        pick_ready = sem("pick_ready")
        oh_ready = sem("oh_ready")
        over_ready = sem("over_ready")
        dst_ready = sem("dst_ready")
        hot_ready = sem("hot_ready")
        key_ready = sem("key_ready")
        hot_chain = sem("hot_chain")
        xgT_ready = sem("xgT_ready")
        a_ready = sem("a_ready")
        y1_ready = sem("y1_ready")
        fin_sum = sem("fin_sum")
        fin_rstd = sem("fin_rstd")
        scaled = sem("scaled")
        gained = sem("gained")
        out_ready = sem("out_ready")

        block = ctx.enter_context(nc.Block())

        win = w_in[0].rearrange("(k p) c -> p k c", p=P)
        wout = w_out[0].rearrange("(k p) c -> p k c", p=P)
        wpool = w_pool[0].rearrange("g (a p) d -> p (g a) d", p=P)
        wgate = w_gate[0].rearrange("e (k p) f -> p e k f", p=P)
        wup = w_up[0].rearrange("e (k p) f -> p e k f", p=P)
        wdown = w_down[0].rearrange("e (q p) d -> p e q d", p=P)
        xs_rows = x_sample.rearrange("b t d -> (b t) d")
        COL = 2 * P

        @block.sync
        def _(sp):
            vecs = ((g_mix, 0, 16), (g_ffn, 16, 32), (b_dw, 32, 40), (ln_g, 40, 48), (ln_b, 48, 56), (pool_scale, 56, 64))
            for t in range(TT - 1):
                sp.dma_start(x1r[:, t, 0:D], x_prompt[0, t * TR:(t + 1) * TR, :]).then_inc(x_in[t], 16)
            sp.dma_start(x1r[0:LASTP, TT - 1, 0:D], x_prompt[0, (TT - 1) * TR:SEQ, :]).then_inc(x_in[TT - 1], 16)
            sp.dma_start(x1r[LASTP:TR, TT - 1, 0:D], xs_rows).then_inc(x_in[TT - 1], 16)
            for v, a, b in vecs:
                sp.dma_start(pv[a:b, :], v[0].rearrange("(j p) -> j p", p=P)).then_inc(pv_in, 16)
            sp.dma_start(wsl[0], win[:, :, 0:COL]).then_inc(slot_in[0], 16)
            sp.dma_start(wsl[1], win[:, :, DC:DC + COL]).then_inc(slot_in[1], 16)
            with sp.Fori(1, 4) as g:
                for a in range(2):
                    sp.wait_ge(vg_mm, 4 * g + 2 * a - 2)
                    sp.dma_start(wsl[a], win[:, :, bass.DynSlice(g * COL + a * DC, COL)]).then_inc(slot_in[a], 16)
            for c in range(4):
                sp.wait_ge(vg_mm if c < 2 else u_mm, 14 + 2 * c if c < 2 else 2 * c - 2)
                sp.dma_start(wsl[c % 2], win[:, :, 2 * DC + (3 - c) * COL:2 * DC + (4 - c) * COL]).then_inc(slot_in[c % 2], 16)
            sp.wait_ge(u_mm, 6)
            sp.dma_start(wsl[0][:, 0:CT, :], wpool).then_inc(slot_in[0], 16)

            def load_gu(e, c, s=0):
                k = 2 if s == 1 and c == 0 else 4 * c
                for g, src in ((0, wgate), (1, wup)):
                    w = src[:, bass.DynSlice(e, 1), k:4 * c + 4, :].rearrange("p o k f -> p (o k) f")
                    sp.dma_start(wgu[:, k:4 * c + 4, g, :], w).then_inc(gu_in[c], 16)

            def load_first(e):
                for g, src in ((0, wgate), (1, wup)):
                    w = src[:, bass.DynSlice(e, 1), 0:2, :].rearrange("p o k f -> p (o k) f")
                    sp.dma_start(wgu_first[:, :, g, :], w).then_inc(first_in, 16)

            def load_wd(e, s, q):
                w = wdown[:, bass.DynSlice(e, 1), q, :].rearrange("p o d -> p (o d)")
                sp.dma_start(wdn[s][q], w).then_inc(wd_in[s][q], 16)

            for c in range(8):
                if c == 0:
                    sp.wait_ge(u_mm, CT)
                elif c == 1:
                    sp.wait_ge(wp_mm, CT)
                else:
                    sp.wait_ge(o_mm, 2 * c - 2)
                sp.dma_start(wsl[(c + 1) % 2], wout[:, :, c * COL:(c + 1) * COL]).then_inc(slot_in[(c + 1) % 2], 16)
                if c == 1:
                    sp.wait_ge(st_out, 16 * 4)
                    sp.wait_ge(old_out, 16 * 2)
                if c in (1, 3, 4, 5):
                    load_gu(0, (1, 3, 4, 5).index(c))
                if c == 6:
                    sp.wait_ge(mix_ready, CT)
                    load_wd(0, 0, 3)
                    for a in range(2):
                        sp.wait_ge(x1_ready[a], CT // 2)
                    load_wd(1, 1, 0)
            sp.wait_ge(o_mm, KT - 2)
            load_wd(1, 1, 2)
            load_wd(1, 1, 3)
            sp.wait_ge(o_mm, KT)
            load_first(1)
            for q in range(3):
                load_wd(0, 0, q)
            for a in range(2):
                sp.wait_ge(x1_ready[a], CT)
            load_wd(1, 1, 1)

            def gate_up(e, n, s):
                for c in range(4):
                    sp.wait_ge(gu_used, 4 * n + c - 3)
                    load_gu(e, c, s)

            def first_gate_up(e, n):
                sp.wait_ge(gu_used, 4 * n - 7)
                load_first(e)

            def down(e, n, s):
                for q in range(4):
                    sp.wait_ge(wd_used, 4 * n + q - 7)
                    load_wd(e, s, q)

            def next_weights(e):
                gate_up(e, e, 1)
                down(e + 1, e + 1, 0)
                gate_up(e + 1, e + 1, 0)
                first_gate_up(e + 2, e + 2)

            with sp.Fori(0, PAIRS - 2) as i:
                next_weights(2 * i + 1)
                down(2 * i + 3, 2 * i + 3, 1)
            next_weights(NE - 3)
            gate_up(NE - 1, NE - 1, 1)
            down(NE - 1, NE - 1, 1)
            sp.wait_ge(over_ready, 1)
            n_over = sp.value_load(eid_i[0:1, 2 * OVP:2 * OVP + 1], min_val=0, max_val=2 * OVP)
            with sp.Fori(0, OVP) as j:
                with sp.If(n_over > 2 * j):
                    for s in range(2):
                        e = sp.value_load(eid_i[0:1, bass.DynSlice(2 * j + s, 1)], min_val=0, max_val=NE - 1)
                        if s == 1:
                            first_gate_up(e, NE + 2 * j + 1)
                        gate_up(e, NE + 2 * j + s, s)
                        down(e, NE + 2 * j + s, s)
                    for s in range(2):
                        sp.wait_ge(y_out[s], 16 * (PAIRS + j) + 16)
                        sp.sem_inc(scattered, 1)
            sp.wait_ge(gu_used, 4 * NE)
            sp.dma_start(gfin, g_final[None, :].to_broadcast([TR, D])).then_inc(gfin_in, 16)
            for s in range(2):
                sp.wait_ge(y_out[s], 16 * PAIRS)
            by_token = yexp_dram.rearrange("(t c) d -> t (c d)", c=4)
            for t in range(TT):
                for c in range(2):
                    sp.dma_start(yg[:, t, c, :], by_token[t * TR:(t + 1) * TR, c * D:(c + 1) * D]).then_inc(yg_in[2 * t + c], 16)
            for t in range(TT):
                sp.wait_ge(scaled, t + 1)
                if t == TT - 1:
                    sp.wait_ge(out_ready, 1)
                if t < TT - 1:
                    sp.dma_start(y_prompt[0, t * TR:(t + 1) * TR, :], yg[:, t, 0, :]).then_inc(fin_out, 16)
                else:
                    sp.dma_start(y_prompt[0, t * TR:SEQ, :], yg[0:LASTP, t, 0, :]).then_inc(fin_out, 16)
                    sp.dma_start(y_sample.rearrange("b t d -> (b t) d"), yg[LASTP:TR, t, 0, :]).then_inc(fin_out, 16)
            sp.wait_ge(fin_out, 16 * (TT + 1))

        @block.tensor
        def _(pe):
            def stay_awake(n):
                for _ in range(n):
                    pe.matmul(ps[1][:, 0:P], ones[:, :], ones[:, :], start=True, stop=True)

            pe.wait_ge(const_ready, 2)
            for k in range(KT):
                if k >= 4:
                    pe.wait_ge(xT_ready[k % 2], (k - 4) // 2 + 1)
                for t in range(TT):
                    if k == 0:
                        stay_awake(AWAKE_START[t])
                        pe.wait_ge(x_in[t], 16 if t < TT - 1 else 32)
                    last = pe.transpose(ps[k % 4][:, t * TR:(t + 1) * TR], x1r[:, t, k * P:(k + 1) * P], ident[0:TR, 0:TR])
                last.then_inc(xT_mm, 1)
            pe.wait_ge(pv_in, 16 * 6)
            pe.transpose(ps[7][:, 0:64], pv[:, :], ident[0:64, 0:64]).then_inc(pvT_mm, 1)
            pe.wait_ge(diag_ready, 1)
            for t in range(TT):
                last = pe.matmul(ps[4][:, t * TR:(t + 1) * TR], ones[0:TR, :], diag[:, t, :], start=True, stop=True)
            last.then_inc(rbc_mm, 1)
            pe.wait_ge(wdr_in, 16)
            for j in range(CT):
                last = pe.transpose(ps[5][:, 32 * j:32 * j + W], wdr[:, j * P:(j + 1) * P], ident[0:W, 0:W])
            last.then_inc(wdT_mm, 1)
            pe.wait_ge(st_in, 16 * 3)
            for a in range(2):
                pe.wait_ge(xT_ready[a], KT // 2)
            pe.wait_ge(pvT_ready, 1)
            for b in range(4):
                for j in (2 * b, 2 * b + 1):
                    for a in range(2):
                        o = (j % 2) * 240 + a * 120
                        last = pe.transpose(ps[b][:, o:o + 120], crow[:, a, j * P:(j + 1) * P], ident[0:120, 0:120])
                last.then_inc(hist_mm, 1)
            for b in range(2):
                for j in range(4 * b, 4 * b + 4):
                    o = (j % 4) * 120
                    last = pe.transpose(ps[6 + b][:, o:o + 120], prow[:, j * P:(j + 1) * P], ident[0:120, 0:120])
                last.then_inc(hist_mm, 1)
            pe.wait_ge(hist_ready, 4)

            def dense(bank, a, cc, rhs, order=range(KT), late=None, each=None):
                for n, k in enumerate(order):
                    if each:
                        pe.wait_ge(each, k + 1)
                    if late and n == KT // 2:
                        pe.wait_ge(*late)
                    last = pe.matmul(ps[bank][:, 0:NTOK], wsl[a][:, k, cc * P:(cc + 1) * P], rhs[:, k, :],
                                     start=(n == 0), stop=(n == KT - 1))
                return last

            with pe.Fori(0, 4) as g:
                for a in range(2):
                    pe.wait_ge(slot_in[a], 16 * g + 16)
                    if a:
                        pe.wait_ge(v_evac, 2 * g + 1)
                    for cc in range(2):
                        dense(2 * a + cc, a, cc, hT, each=hT_ready if a + cc == 0 else None).then_inc(vg_mm, 1)
                pe.wait_ge(v_evac, 2 * g + 2)

            def pool_inputs(m):
                c, r = m % 2, m // 2
                pe.wait_ge(slot_in[c], 16 * (5 + r))
                if r == 0:
                    pe.wait_ge(v_evac if c == 0 else g_evac, CT)
                else:
                    pe.wait_ge(u_evac[c], 2)
                for cc in range(2):
                    dense(2 * c + cc, c, cc, hT).then_inc(u_mm, 1)

            pool_inputs(0)
            pool_inputs(1)
            pe.wait_ge(conv_chain, 4 * PERC)
            for j in range(CT):
                last = pe.matmul(ps[4][:, 0:NTOK], ones[:, :], yc[:, j, :], start=(j == 0), stop=(j == CT - 1))
            last.then_inc(sum_mm, 1)
            pool_inputs(2)
            pe.wait_ge(sq_ready, 1)
            for j in range(CT):
                last = pe.matmul(ps[5][:, 0:NTOK], ones[:, :], sqw[:, j, :], start=(j == 0), stop=(j == CT - 1))
            last.then_inc(sumsq_mm, 1)
            pool_inputs(3)
            pe.wait_ge(keep_ready, CT // 2)
            pe.wait_ge(hist_ready, 6)
            for b in range(2):
                for j in range(4 * b, 4 * b + 4):
                    last = pe.transpose(ps[6 + b][0:AK, (j % 4) * P:(j % 4 + 1) * P], ak[:, j, :], ident[:, :])
                last.then_inc(st_mm, 1)
            pe.wait_ge(u_evac[0], 4)
            pe.wait_ge(u_evac[1], 4)
            for b in range(2):
                for j in range(4 * b, 4 * b + 4):
                    last = pe.transpose(ps[b][0:UK, (j % 4) * P:(j % 4 + 1) * P], uk[:, j, :], ident[:, :])
                last.then_inc(st_mm, 1)
            pe.wait_ge(slot_in[0], 16 * 7)
            pe.wait_ge(st_ready, 2)
            for i in range(CT):
                g, dd = NG - 1 - i // 2, i % 2
                pe.wait_ge(s_ready, 2 * (i // 2) + 2)
                if i >= 2:
                    pe.wait_ge(wp_ready, i - 1)
                for a in range(2):
                    last = pe.matmul(ps[6 + i % 2][:, 0:NTOK], wsl[0][:, 2 * g + a, dd * P:(dd + 1) * P], sT[:, 2 * g + a, :],
                                     start=(a == 0), stop=(a == 1))
                last.then_inc(wp_mm, 1)
            pe.wait_ge(st_ready, 4)
            pe.wait_ge(mix_ready, CT)
            pe.wait_ge(wrs_ready, 1)
            pe.wait_ge(var_ready, 1)

            def rows_and_router(o, q):
                pe.wait_ge(x1_ready[q % 2], 2 * o + q // 2 + 1)
                if q == 0:
                    pe.wait_ge(row_evac, TT * o + 1)
                for t in range(TT):
                    last = pe.transpose(ps[2 + t][0:TR, q * P:(q + 1) * P], x1wk[:, q, t * TR:(t + 1) * TR], ident[:, :])
                last.then_inc(row_mm, 1)
                for t in range(TT):
                    pe.matmul(ps[5 + t][0:TR, 0:NR], x1wk[:, q, t * TR:(t + 1) * TR], dyn(wr, (4 * o + q) * NR, NR),
                              start=False, stop=False)

            def projection(o, first=False):
                for q in range(4):
                    a = 1 - q // 2
                    if q % 2 == 0:
                        pe.wait_ge(slot_in[a], 16 * o + (16 * 7 if a else 16 * 8))
                    dense(q % 2, a, q % 2, mixT, late=(wp_ready, CT) if first and q == 0 else None).then_inc(o_mm, 1)
                    if q:
                        rows_and_router(o, q - 1)
                    elif first:
                        for t in range(TT):
                            pe.matmul(ps[5 + t][0:TR, 0:NR], zero[:, :], wr3[:, 0, :], start=True, stop=False)
                    else:
                        rows_and_router(o - 1, 3)

            projection(0, first=True)
            with pe.Fori(1, 4) as o:
                projection(o)
            rows_and_router(3, 3)
            for t in range(TT):
                last = pe.matmul(ps[5 + t][0:TR, 0:NR], zero[:, :], wr3[:, 0, :], start=False, stop=True)
            last.then_inc(router_mm, 1)

            stay_awake(AWAKE_ROUTE[0])
            pe.wait_ge(pick_ready, 1)
            pe.matmul(ps[6][0:TR, 0:TT * NE], earlier[:, :], pick[:, :, :].rearrange("p t e -> p (t e)"), start=True, stop=False)
            for b in range(TT - 1):
                last = pe.matmul(ps[6][0:TR, (b + 1) * NE:TT * NE].rearrange("p (t e) -> p t e", e=NE), ones[0:TR, 0:TR],
                                 pick[:, b:b + 1, :].to_broadcast([TR, TT - 1 - b, NE]), start=False, stop=(b == TT - 2))
            last.then_inc(rank_mm, 1)
            for b in range(TT):
                last = pe.matmul(ps[5][0:TR, 0:NE], ones[0:TR, 0:TR], pick[:, b, :], start=(b == 0), stop=(b == TT - 1))
            last.then_inc(rank_mm, 1)
            stay_awake(AWAKE_ROUTE[1])
            pe.wait_ge(row_evac, 4 * TT + 1)

            def select(m, b):
                if b == 0:
                    pe.wait_ge(hot_ready, m + 1)
                if b == 3:
                    pe.wait_ge(xgT_ready, 4 * m + 1)
                for k in range(4 * b, 4 * b + 4):
                    for t in range(TT):
                        last = pe.matmul(ps[SELB[b]][:, (k % 4) * P:(k % 4 + 1) * P], x1r[:, t, k * P:(k + 1) * P], hot[:, t, :],
                                         start=(t == 0), stop=(t == TT - 1))
                last.then_inc(xgT_mm, 1)

            def pair(i, first=False, ahead=True):
                for s in range(2):
                    n = 2 * i + s
                    for c in range(4):
                        if first and s == 0:
                            for b in ((0, 1), (2,), (3,), ())[c]:
                                select(0, b)
                        if s == 0:
                            pe.wait_ge(xgT_ready, 4 * i + c + 1)
                        pe.wait_ge(gu_in[c], 32 * n + 32)
                        if s == 1 and c == 0:
                            pe.wait_ge(first_in, 32 * i + 32)
                        for k in range(4 * c, 4 * c + 4):
                            for h in range(2):
                                last = pe.matmul(ps[4 + s][BLK * h:BLK * (h + 1), :], xgT[:, k, BLK * s:BLK * (s + 1)],
                                                 (wgu_first if s == 1 and k < 2 else wgu)[:, k, :, 256 * h:256 * (h + 1)], start=(k == 0), stop=(k == KT - 1))
                        last.then_inc(gu_used, 1)
                    if first and s == 1:
                        pe.wait_ge(dst_ready, 1)
                    if ahead:
                        for b in (2 * s, 2 * s + 1):
                            select(i + 1, b)
                    pe.wait_ge(a_ready, n + 1)
                    for j in range(2):
                        last = pe.transpose(ps[6][:, j * P:(j + 1) * P], a_sb[:, j * P:(j + 1) * P], ident[:, :])
                    last.then_inc(at_mm, 1)
                    pe.wait_ge(aT_ready, n + 1)
                    for q in range(4):
                        half, j = q // 2, q % 2
                        pe.wait_ge(wd_in[s][q], 16 * i + 16)
                        for m in range(2):
                            for h in range(2):
                                last = pe.matmul(ps[2 + m][BLK * h:BLK * (h + 1), :],
                                                 aT[:, j * P + BLK * half:j * P + BLK * (half + 1)],
                                                 wdn[s][q][:, 1024 * h + 512 * m:1024 * h + 512 * (m + 1)],
                                                 start=(q == 0), stop=(q == 3))
                        last.then_inc(wd_used, 1)
                    if first and s == 0:
                        pe.wait_ge(oh_ready, 1)
                        for c in range(2 * TT):
                            last = pe.matmul(ps[7][:, 0:NBLK], ohw[:, c, :], ohb[:, c, :], start=(c == 0), stop=(c == 2 * TT - 1))
                        last.then_inc(tab_mm, 1)

            pair(0, first=True)
            with pe.Fori(1, PAIRS - 1) as i:
                pair(i)
            pair(PAIRS - 1, ahead=False)
            pe.wait_ge(over_ready, 1)
            n_over = pe.value_load(eid_i[0:1, 2 * OVP:2 * OVP + 1], min_val=0, max_val=2 * OVP)
            with pe.Fori(0, OVP) as j:
                with pe.If(n_over > 2 * j):
                    for b in range(4):
                        select(PAIRS + j, b)
                    pair(PAIRS + j, ahead=False)

        @block.scalar
        def _(act):
            for k in range(0, KT, 2):
                act.wait_ge(xT_mm, k + 1)
                act.copy(xTk[:, k, :], ps[k % 4][:, 0:NTOK]).then_inc(xT_ready[0], 1)
                if k == 4:
                    act.wait_ge(act_in, 1)
                    act.activation(sq[:, :], va[:, :], ACT.Sqrt).then_inc(sqrt_done, 1)
            act.wait_ge(pvT_mm, 1)
            act.copy(pvT[:, :], ps[7][:, 0:64]).then_inc(pvT_ready, 1)
            act.wait_ge(wdT_mm, 1)
            act.copy(wdT3[:, :, 0:W], ps[5][:, 0:256].rearrange("p (j w) -> p j w", j=CT)[:, :, 0:W]).then_inc(wdT_ready, 1)
            act.wait_ge(pvT_ready, 1)
            act.copy(wdT3[:, :, W:32].rearrange("p j o -> p (j o)"), pbd).then_inc(wdT_ready, 1)
            for b in range(4):
                act.wait_ge(hist_mm, b + 1)
                act.copy(words(arena, O_HIST + 480 * b, 480), ps[b][:, 0:480]).then_inc(hist_ready, 1)
            for b in range(2):
                act.wait_ge(hist_mm, 5 + b)
                for j in range(4):
                    dst = uline[:, 4 * b + j, SM0:ULINE].rearrange("p (s t) -> p s t", s=NSEQ)[:, :, 0:HP]
                    last = act.copy(dst, ps[6 + b][:, 120 * j:120 * (j + 1)].rearrange("p (s t) -> p s t", s=NSEQ))
                last.then_inc(hist_ready, 1)
            with act.Fori(0, 4) as g:
                for cc in range(2):
                    act.wait_ge(vg_mm, 4 * g + cc + 1)
                    act.copy(vw[:, cc, :], ps[cc][:, 0:NTOK]).then_inc(v_evac, 1)
                for cc in range(2):
                    act.wait_ge(vg_mm, 4 * g + cc + 3)
                    act.activation(sg[:, cc, :], ps[2 + cc][:, 0:NTOK], ACT.Sigmoid).then_inc(g_evac, 1)
                act.wait_ge(glu_ready, 2 * g + 2)

            def pool_line(n):
                c, j = n % 4, CT - 2 - 2 * (n // 2) + n % 2
                act.wait_ge(u_mm, n + 1)
                act.copy(uline[:, j, HP:SM0], ps[c][:, 0:SEQ])
                act.copy(uk[:, j, :], ps[c][:, SEQ - HP:NTOK])
                act.copy(uline[:, j, SM0:ULINE].rearrange("p (s t) -> p s t", s=NSEQ)[:, :, HP:HP + SLEN],
                         ps[c][:, SEQ:NTOK].rearrange("p (s t) -> p s t", s=NSEQ)).then_inc(u_evac[c // 2], 1)

            for n in range(4):
                pool_line(n)
            act.wait_ge(sum_mm, 1)
            act.activation(nmean[:, :], ps[4][:, 0:NTOK], ACT.Copy, scale=-1.0 / DC).then_inc(nmean_ready, 1)
            act.wait_ge(centred, 1)
            act.wait_ge(keep_ready, 4)
            act.activation(words(arena, O_AW, CT * NTOK), words(arena, O_YC, CT * NTOK), ACT.Square).then_inc(sq_ready, 1)
            pool_line(4)
            pool_line(5)
            act.wait_ge(var_ready, 1)
            act.activation(lnr[:, :], lnv[:, :], ACT.Sqrt).then_inc(sqrt_done, 1)
            pool_line(6)
            act.wait_ge(yn_ready, 1)
            for j in range(CT):
                act.activation(mixT[:, j, :], yc[:, j, :], ACT.Silu, bias=plb[:, j:j + 1], scale=plg[:, j:j + 1]).then_inc(mix_ready, 1)
            pool_line(7)
            for n, (b, r) in enumerate(((6, AK), (7, AK), (0, UK), (1, UK))):
                act.wait_ge(st_mm, n + 1)
                act.copy(strow[0:r, n // 2, (n % 2) * 512:(n % 2 + 1) * 512], ps[b][0:r, :]).then_inc(st_ready, 1)
            act.wait_ge(st_ready, 4)
            act.dma_start(conv_p[0, 0], strow[0:HC, 0, :]).then_inc(st_out, 16)
            act.dma_start(conv_s[0, :, HC - SLEN:HC, :], strow[HC:AK, 0, :]).then_inc(st_out, 16)
            act.dma_start(pool_p[0, 0], strow[0:HP, 1, :]).then_inc(st_out, 16)
            act.dma_start(pool_s[0, :, HP - SLEN:HP, :], strow[HP:UK, 1, :]).then_inc(st_out, 16)
            with act.Fori(0, 4) as o:
                act.wait_ge(row_mm, 4 * o + 4)
                for t in range(TT):
                    act.activation(ysb[0:TR, t % 2, (t // 2) * 512:(t // 2 + 1) * 512], ps[2 + t][0:TR, :], ACT.Square,
                                   accum_out=dyn(ssp, 4 * t + o, 1, TR)).then_inc(act_chain, 1)
            act.wait_ge(act_in, 2)
            act.activation(sq[:, :], va[:, :], ACT.Sqrt).then_inc(sqrt_done, 1)
            act.wait_ge(act_in, 3)
            act.activation(r4b[:, :, :], r4[:, :, :], ACT.Exp).then_inc(exp_done, 1)
            act.wait_ge(act_in, 4)
            act.activation(ex[:, :, :], dl[:, :, :], ACT.Exp).then_inc(exp_done, 1)


            def pair(i):
                for s in range(2):
                    n = 2 * i + s
                    act.wait_ge(ysb_free[s], i + 1)
                    act.wait_ge(gu_used, 4 * n + 4)
                    act.activation(sl_sb[:, :], ps[4 + s][:, 0:256], ACT.Silu).then_inc(sl_ready, 1)
                    act.wait_ge(at_mm, n + 1)
                    act.copy(aT[:, :], ps[6][:, 0:256]).then_inc(aT_ready, 1)
                    act.wait_ge(wd_used, 4 * n + 4)
                    act.copy(ysb[:, s, 0:512], ps[2][:, :]).then_inc(y0_ready, 1)

            with act.Fori(0, PAIRS) as i:
                pair(i)
            act.wait_ge(over_ready, 1)
            n_over = act.value_load(eid_i[0:1, 2 * OVP:2 * OVP + 1], min_val=0, max_val=2 * OVP)
            with act.Fori(0, OVP) as j:
                with act.If(n_over > 2 * j):
                    pair(PAIRS + j)
            def squares(t):
                act.wait_ge(fin_sum, t + 1)
                act.activation(yg[:, t, 1, :], yg[:, t, 0, :], ACT.Square, accum_out=ss[:, t:t + 1]).then_inc(act_chain, 1)

            def root(t):
                act.wait_ge(act_in, 5 + t)
                act.activation(sq[:, t:t + 1], va[:, t:t + 1], ACT.Sqrt).then_inc(sqrt_done, 1)

            def scale(t):
                act.wait_ge(gained, t + 1)
                act.wait_ge(fin_rstd, t + 1)
                c = 0 if t < TT - 1 else D // 2
                act.activation(yg[:, t, 0, c:D], x1r[:, t, c:D], ACT.Copy, scale=rs[:, t:t + 1]).then_inc(scaled, 1)

            squares(0)
            root(0)
            squares(1)
            scale(0)
            root(1)
            squares(2)
            root(2)
            scale(1)
            scale(2)

        @block.vector
        def _(dve):
            ch = Chain(dve, dve_chain)
            link = ch.link

            def rsqrt(v, root, r, tmp, n):
                dve.wait_ge(sqrt_done, n)
                link(dve.reciprocal(r, root))
                link(dve.tensor_tensor(tmp, r, r, ALU.mult))
                link(dve.scalar_tensor_tensor(out=tmp, in0=tmp, scalar=-0.5, in1=v, op0=ALU.mult, op1=ALU.mult))
                link(dve.scalar_tensor_tensor(out=r, in0=tmp, scalar=1.5, in1=r, op0=ALU.add, op1=ALU.mult))

            for t in range(TT):
                dve.wait_ge(x_in[t], 16 if t < TT - 1 else 32)
                link(dve.tensor_tensor_reduce(out=words(arena, O_MIX, D, TR), in0=x1r[:, t, 0:D], in1=x1r[:, t, 0:D],
                                              scale=1.0, scalar=0.0, op0=ALU.mult, op1=ALU.add, accum_out=ss[:, t:t + 1]))
            dve.tensor_scalar(va[:, :], ss[:, :], 1.0 / D, EPS, ALU.mult, ALU.add).then_inc(act_in, 1)

            def odd_copy(k):
                dve.wait_ge(xT_mm, k + 1)
                dve.tensor_copy(xTk[:, k, :], ps[k % 4][:, 0:NTOK]).then_inc(xT_ready[1], 1)

            for k in range(1, 7, 2):
                odd_copy(k)
            dve.wait_ge(act_in, 1)
            rsqrt(va[:, :], sq[:, :], rs[:, :], tn[:, :], 1)
            dve.wait_ge(const_ready, 1)
            for t in range(TT):
                last = dve.tensor_scalar(diag[:, t, :], ident[0:TR, 0:TR], rs[:, t:t + 1], None, ALU.mult)
            last.then_inc(diag_ready, 1)
            for k in range(7, KT, 2):
                odd_copy(k)
            dve.wait_ge(rbc_mm, 1)
            dve.wait_ge(pvT_ready, 1)
            for k in range(KT):
                dve.wait_ge(xT_ready[k % 2], k // 2 + 1)
                dve.scalar_tensor_tensor(out=hT[:, k, :], in0=xTk[:, k, :], scalar=pgm[:, k:k + 1], in1=ps[4][:, 0:NTOK],
                                         op0=ALU.mult, op1=ALU.mult).then_inc(hT_ready, 1)
            dve.wait_ge(wr_in, 32)
            for k in range(KT):
                last = dve.tensor_scalar(wr3[:, k, :], wr3[:, k, :], pgf[:, k:k + 1], None, ALU.mult)
            last.then_inc(wrs_ready, 1)
            with dve.Fori(0, 4) as g:
                for cc in range(2):
                    dve.wait_ge(g_evac, 2 * g + cc + 1)
                    dve.tensor_tensor(aw[:, cc, HC:AEXT], vw[:, cc, :], sg[:, cc, :], ALU.mult).then_inc(glu_ready, 1)
                dve.wait_ge(glu_ready, 2 * g + 2)
                dve.wait_ge(work_ready, g + 1)
                for w in range(W):
                    for cc in range(2):
                        src, dst = aw[:, cc, w:w + SEQ], acc[:, cc, 0:SEQ]
                        fin = dyn(arena, O_YC + (2 * g + cc) * NTOK, SEQ)
                        if w == 0:
                            ins = dve.tensor_scalar(dst, src, wdw[:, cc, 0:1], wdw[:, cc, W:W + 1], ALU.mult, ALU.add)
                        else:
                            dve.wait_ge(conv_chain, PERC * g + 2 * w + cc - 1)
                            ins = dve.scalar_tensor_tensor(out=(fin if w == W - 1 else dst), in0=src, scalar=wdw[:, cc, w:w + 1],
                                                           in1=dst, op0=ALU.mult, op1=ALU.add)
                        ins.then_inc(conv_chain, 1)
                dve.wait_ge(prod_ready, 2 * g + 2)
                for cc in range(2):
                    dve.tensor_reduce(acc[:, cc, SEQ:NTOK], prod[:, cc, :, :], AXX, ALU.add).then_inc(conv_chain, 1)
                for cc in range(2):
                    dve.wait_ge(conv_chain, PERC * g + 2 * W + cc + 1)
                    dve.tensor_scalar(dyn(arena, O_YC + (2 * g + cc) * NTOK + SEQ, NS), acc[:, cc, SEQ:NTOK],
                                      wdw[:, cc, W:W + 1], None, ALU.add).then_inc(conv_chain, 1)
                dve.wait_ge(conv_chain, PERC * g + PERC)
                dve.wait_ge(keep_ready, g + 1)
            dve.wait_ge(nmean_ready, 1)
            dve.wait_ge(conv_chain, 4 * PERC)
            dve.tensor_tensor(yc, yc, nmean[:, None, :].to_broadcast([P, CT, NTOK]), ALU.add).then_inc(centred, 1)
            dve.wait_ge(sumsq_mm, 1)
            dve.tensor_scalar(lnv[:, :], ps[5][:, 0:NTOK], 1.0 / DC, EPS, ALU.mult, ALU.add).then_inc(var_ready, 1)
            dve.wait_ge(var_ready, 1)
            dve.wait_ge(centred, 1)
            rsqrt(lnv[:, :], lnr[:, :], nmean[:, :], lnt[:, :], 2)
            dve.tensor_tensor(yc, yc, nmean[:, None, :].to_broadcast([P, CT, NTOK]), ALU.mult).then_inc(yn_ready, 1)
            for i in range(CT):
                dve.wait_ge(wp_mm, i + 1)
                j = CT - 2 - 2 * (i // 2) + i % 2
                dve.tensor_scalar(mixT[:, CT + j, :], ps[6 + i % 2][:, 0:NTOK], pps[:, j:j + 1], None, ALU.mult).then_inc(wp_ready, 1)
            dve.sem_inc(row_evac, 1)
            def residual(o):
                for q in range(4):
                    dve.wait_ge(o_mm, 4 * o + q + 1)
                    dve.tensor_tensor(x1wk[:, q, :], ps[q % 2][:, 0:NTOK], dyn(xT, (4 * o + q) * NTOK, NTOK),
                                      ALU.add).then_inc(x1_ready[q % 2], 1)

            def rows(o):
                for t in range(TT):
                    dve.wait_ge(act_chain, TT * o + t + 1)
                    dve.tensor_copy(x1r[:, t, bass.DynSlice(512 * o, 512)], ps[2 + t][0:TR, :]).then_inc(row_evac, 1)

            with dve.Fori(0, 3) as o:
                residual(o)
                rows(o)
            residual(3)
            dve.wait_ge(act_chain, 4 * TT)
            link(dve.tensor_reduce(ss[:, :], ssp3, AXX, ALU.add))
            dve.tensor_scalar(va[:, :], ss[:, :], 1.0 / D, EPS, ALU.mult, ALU.add).then_inc(act_in, 1)
            rows(3)
            dve.wait_ge(act_in, 2)
            rsqrt(va[:, :], sq[:, :], rs[:, :], tn[:, :], 3)
            dve.wait_ge(router_mm, 1)
            dve.wait_ge(bias_in, 32)
            for t in range(TT):
                ch.step(dve.scalar_tensor_tensor(out=lg[:, t, :], in0=ps[5 + t][0:TR, 0:NR], scalar=rs[:, t:t + 1],
                                                 in1=bias[:, :], op0=ALU.mult, op1=ALU.add))
            dve.wait_ge(dve_chain, ch.n)
            gl = lg[:, :, 0:NG]

            def over(a, n):
                return a.to_broadcast([TR, TT, n])

            link(dve.tensor_reduce(g1[:, :, :], gl, AXX, ALU.max))
            dve.tensor_tensor(r4[:, :, :], gl, over(g1[:, :, :], NG), ALU.subtract).then_inc(act_in, 1)
            dve.wait_ge(act_in, 3)
            dve.wait_ge(const_ready, 3)
            iota4 = iof[:, None, 0:NG].to_broadcast([TR, TT, NG])
            iota32 = iof[:, None, 0:NE].to_broadcast([TR, TT, NE])

            def first(onehot, values, top, tmp, n, iota):
                link(dve.tensor_tensor(tmp, values, over(top, n), ALU.is_equal))
                link(dve.scalar_tensor_tensor(out=tmp, in0=tmp, scalar=-64.0, in1=iota, op0=ALU.mult, op1=ALU.add))
                link(dve.tensor_reduce(ix[:, :, :], tmp, AXX, ALU.min))
                link(dve.scalar_tensor_tensor(out=onehot, in0=iota, scalar=-64.0, in1=over(ix[:, :, :], n), op0=ALU.add, op1=ALU.is_equal))

            first(r4c[:, :, :], gl, g1[:, :, :], r4d[:, :, :], NG, iota4)
            link(dve.tensor_scalar(r4c[:, :, :], r4c[:, :, :], BIG, -BIG, ALU.mult, ALU.add))
            link(dve.tensor_tensor(sel[:, :, :].rearrange("p t (g e) -> p t g e", g=NG),
                                   r4c[:, :, :, None].to_broadcast([TR, TT, NG, EG]),
                                   lg[:, :, NG:NR].rearrange("p t (g e) -> p t g e", g=NG), ALU.add))
            link(dve.tensor_reduce(m1[:, :, :], sel[:, :, :], AXX, ALU.max))
            first(oh1[:, :, :], sel[:, :, :], m1[:, :, :], ra[:, :, :], NE, iota32)
            link(dve.scalar_tensor_tensor(out=sel[:, :, :].rearrange("p t e -> p (t e)"), in0=oh1[:, :, :].rearrange("p t e -> p (t e)"),
                                          scalar=-2 * BIG, in1=sel[:, :, :].rearrange("p t e -> p (t e)"), op0=ALU.mult, op1=ALU.add))
            link(dve.tensor_reduce(m2[:, :, :], sel[:, :, :], AXX, ALU.max))
            dve.tensor_tensor(dl[:, :, :], m2[:, :, :], m1[:, :, :], ALU.subtract).then_inc(act_in, 1)
            first(oh2[:, :, :], sel[:, :, :], m2[:, :, :], ra[:, :, :], NE, iota32)
            dve.tensor_tensor(pick[:, :, :], oh1[:, :, :], oh2[:, :, :], ALU.add).then_inc(pick_ready, 1)
            slots = iof[:, None, 0:P].to_broadcast([TR, TT, P])

            def one_hot(m):
                if not (isinstance(m, int) and m == 0):
                    dve.tensor_scalar(slot[:, :, :], slot[:, :, :], float(-P), None, ALU.add).then_inc(key_ready, 1)
                    dve.wait_ge(key_ready, m)
                for c, dst in ((0, hot0), (1, hot)):
                    dve.tensor_tensor(dst, slots, slot[:, c, :][:, :, None].to_broadcast([TR, TT, P]), ALU.is_equal).then_inc(hot_chain, 1)
                dve.wait_ge(hot_chain, 3 * m + 2)
                dve.tensor_tensor(hot, hot, hot0, ALU.add).then_inc(hot_chain, 1)
                dve.wait_ge(hot_chain, 3 * m + 3)
                dve.tensor_tensor(hot, hot, rs[:, :, None].to_broadcast([TR, TT, P]), ALU.mult).then_inc(hot_ready, 1)

            def inputs(m, b):
                dve.wait_ge(xgT_mm, 4 * m + b + 1)
                dve.tensor_tensor(xgT[:, 4 * b:4 * b + 4, :], ps[SELB[b]][:, :].rearrange("p (k s) -> p k s", k=4),
                                  pgf[:, 4 * b:4 * b + 4, None].to_broadcast([P, 4, P]), ALU.mult).then_inc(xgT_ready, 1)

            dve.wait_ge(rank_mm, 1)
            picked_rank = ps[6][0:TR, 0:TT * NE].rearrange("p (t e) -> p t e", e=NE)

            def take(v):
                ch.step(dve.tensor_tensor(rc[:, :, :], v, oh1[:, :, :], ALU.mult))
                link(dve.tensor_tensor(rc2[:, :, :], v, oh2[:, :, :], ALU.mult))
                ch.step(dve.tensor_reduce(slot[:, 0, :], rc[:, :, :], AXX, ALU.add))
                link(dve.tensor_reduce(slot[:, 1, :], rc2[:, :, :], AXX, ALU.add))

            ch.step(dve.tensor_scalar(ra[:, :, :], picked_rank, float(CAP), float(PAD), ALU.is_ge, ALU.mult))
            link(dve.scalar_tensor_tensor(out=rc[:, :, :], in0=iota32, scalar=float(BLK), in1=picked_rank, op0=ALU.mult, op1=ALU.add))
            link(dve.tensor_tensor(ra[:, :, :], ra[:, :, :], rc[:, :, :], ALU.add))
            take(ra[:, :, :])
            one_hot(0)
            ch.step(dve.tensor_copy(rk_i[:, 0:TT * NE], ps[6][0:TR, 0:TT * NE]))
            ch.step(dve.tensor_copy(rank[:, :, :].rearrange("p t e -> p (t e)"), ps[6][0:TR, 0:TT * NE]))
            dve.wait_ge(rank_mm, 2)
            link(dve.tensor_scalar(rk_i[:, TT * NE:], ps[5][0:TR, 0:NE], -1.0, 0.0, ALU.add, ALU.max))
            link(dve.tensor_scalar(rk_i[:, :], rk_i[:, :], CAP.bit_length() - 1, None, ALU.logical_shift_right))
            link(dve.tensor_copy(rq[:, :, :].rearrange("p t e -> p (t e)"), rk_i[:, :]))
            rb, nov = rq[:, 0:TT, :], rq[:, TT, :]
            src, at, sh = nov, 0, 1
            while sh < NE:
                ch.step(dve.tensor_copy(cs[:, at, 0:sh], src[:, 0:sh]))
                link(dve.tensor_tensor(cs[:, at, sh:NE], src[:, sh:NE], src[:, 0:NE - sh], ALU.add))
                src, at, sh = cs[:, at, :], 1 - at, 2 * sh
            incl = src
            inputs(0, 0)
            link(dve.tensor_tensor(cnt[:, :], incl, nov, ALU.subtract))
            link(dve.scalar_tensor_tensor(out=cnt[:, :], in0=cnt[:, :], scalar=float(NE - 1), in1=iof[:, 0:NE], op0=ALU.add, op1=ALU.subtract))
            link(dve.tensor_tensor(ra[:, :, :], rb, cnt[:, None, :].to_broadcast([TR, TT, NE]), ALU.add))
            link(dve.scalar_tensor_tensor(out=ra[:, :, :], in0=rb, scalar=0.0, in1=ra[:, :, :], op0=ALU.is_gt, op1=ALU.mult))
            ch.step(dve.tensor_tensor(ra[:, :, :], ra[:, :, :], iota32, ALU.add))
            link(dve.scalar_tensor_tensor(out=rc[:, :, :], in0=rb, scalar=-float(CAP), in1=rank[:, :, :], op0=ALU.mult, op1=ALU.add))
            link(dve.scalar_tensor_tensor(out=ra[:, :, :], in0=ra[:, :, :], scalar=float(BLK), in1=rc[:, :, :], op0=ALU.mult, op1=ALU.add))
            take(ra[:, :, :])
            C6 = 2 * TT
            ch.step(dve.tensor_copy(slot_i[:, :], slot[:, :, :].rearrange("p c t -> p (c t)")))
            for b in range(1, 4):
                inputs(0, b)
            one_hot(1)

            def results_table():
                dve.wait_ge(dve_chain, ch.n)
                ch.step(dve.tensor_scalar(cut_i[:, 0:C6], slot_i[:, :], BLK - 1, None, ALU.bitwise_and))
                link(dve.tensor_scalar(cut_i[:, C6:], slot_i[:, :], BLK.bit_length() - 1, None, ALU.logical_shift_right))
                link(dve.tensor_copy(cut[:, :, :].rearrange("p c o -> p (c o)"), cut_i[:, :]))
                place, blk = cut[:, 0:C6, :], cut[:, C6:, :]
                ch.step(dve.tensor_tensor(ohb, iof[:, None, 0:NBLK].to_broadcast([TR, C6, NBLK]), blk.to_broadcast([TR, C6, NBLK]), ALU.is_equal))
                link(dve.tensor_tensor(ohw[:, :, 0:BLK], iof[:, None, 0:BLK].to_broadcast([TR, C6, BLK]), place.to_broadcast([TR, C6, BLK]), ALU.is_equal))
                ch.step(dve.tensor_copy(ohw[:, :, BLK:P], ohw[:, :, 0:BLK]))
                link(dve.tensor_tensor(ohb, ohb, cdst[:, :, :].rearrange("p c t -> p (c t)")[:, :, None].to_broadcast([TR, C6, NBLK]), ALU.mult))
                dve.sem_inc(oh_ready, 1)
                dve.wait_ge(tab_mm, 1)
                dve.tensor_scalar(dst_i[:, :], ps[7][:, 0:NBLK], half[:, :], float(PAD), ALU.add, ALU.add).then_inc(dst_ready, 1)

            def rest_of_routing():
                dve.wait_ge(exp_done, 2)
                link(dve.tensor_reduce(g2[:, :, :], r4b[:, :, :], AXX, ALU.add))
                link(dve.reciprocal(pg[:, :, :], g2[:, :, :]))
                link(dve.tensor_scalar(den[:, :, :], ex[:, :, :], 1.0, None, ALU.add))
                link(dve.reciprocal(den[:, :, :], den[:, :, :]))
                w0, w1 = wt[:, 0, :][:, :, None], wt[:, 1, :][:, :, None]
                link(dve.tensor_tensor(w0, den[:, :, :], pg[:, :, :], ALU.mult))
                link(dve.tensor_tensor(w1, w0, ex[:, :, :], ALU.mult))
                link(dve.tensor_tensor(ecmp[:, :, :], incl[:, None, :].to_broadcast([TR, 2 * OVP, NE]),
                                       iof[:, 0:2 * OVP, None].to_broadcast([TR, 2 * OVP, NE]), ALU.is_le))
                link(dve.tensor_reduce(eid[:, :, :], ecmp[:, :, :], AXX, ALU.add))
                ch.step(dve.tensor_scalar(eid_i[:, 0:2 * OVP], eid[:, :, :].rearrange("p j o -> p (j o)"), float(NE - 1), None, ALU.min))
                dve.wait_ge(dve_chain, ch.n)
                dve.tensor_copy(eid_i[:, 2 * OVP:2 * OVP + 1], incl[:, NE - 1:NE]).then_inc(over_ready, 1)

            def last_variance(t):
                dve.wait_ge(act_chain, 4 * TT + t + 1)
                dve.tensor_scalar(va[:, t:t + 1], ss[:, t:t + 1], 1.0 / D, EPS, ALU.mult, ALU.add).then_inc(act_in, 1)

            def last_norm(t):
                dve.wait_ge(act_in, 5 + t)
                rsqrt(va[:, t:t + 1], sq[:, t:t + 1], rs[:, t:t + 1], tn[:, t:t + 1], 4 + t)
                dve.sem_inc(fin_rstd, 1)
                if t == TT - 1:
                    dve.wait_ge(gfin_in, 16)
                    dve.scalar_tensor_tensor(out=yg[:, t, 0, 0:D // 2], in0=yg[:, t, 0, 0:D // 2], scalar=rs[:, t:t + 1], in1=gfin[:, 0:D // 2],
                                             op0=ALU.mult, op1=ALU.mult).then_inc(out_ready, 1)

            def pair(i, first=False, ahead=True):
                for s in range(2):
                    n = 2 * i + s
                    dve.wait_ge(sl_ready, n + 1)
                    dve.tensor_tensor(a_sb[:, :], sl_sb[:, :], ps[4 + s][:, 256:512], ALU.mult).then_inc(a_ready, 1)
                    if first and s == 0:
                        results_table()
                    if ahead and s == 1:
                        for b in range(4):
                            inputs(i + 1, b)
                        one_hot(i + 2)
                    dve.wait_ge(wd_used, 4 * n + 4)
                    dve.tensor_copy(ysb[:, s, 512:1024], ps[3][:, :]).then_inc(y1_ready, 1)

            pair(0, first=True)
            rest_of_routing()
            with dve.Fori(1, PAIRS - 1) as i:
                pair(i)
            pair(PAIRS - 1, ahead=False)
            dve.wait_ge(over_ready, 1)
            n_over = dve.value_load(eid_i[0:1, 2 * OVP:2 * OVP + 1], min_val=0, max_val=2 * OVP)
            with dve.Fori(0, OVP) as j:
                with dve.If(n_over > 2 * j):
                    for b in range(4):
                        inputs(PAIRS + j, b)
                    one_hot(PAIRS + j + 1)
                    pair(PAIRS + j, ahead=False)
            for t in range(TT):
                a, b = yg[:, t, 0, :], yg[:, t, 1, :]
                dve.wait_ge(yg_in[2 * t], 16)
                link(dve.scalar_tensor_tensor(out=a, in0=a, scalar=wt[:, 0, t:t + 1], in1=x1r[:, t, 0:D], op0=ALU.mult, op1=ALU.add))
                if t:
                    last_variance(t - 1)
                dve.wait_ge(yg_in[2 * t + 1], 16)
                dve.scalar_tensor_tensor(out=a, in0=b, scalar=wt[:, 1, t:t + 1], in1=a, op0=ALU.mult, op1=ALU.add).then_inc(fin_sum, 1)
                if t:
                    last_norm(t - 1)
            last_variance(TT - 1)
            last_norm(TT - 1)

        @block.gpsimd
        def _(pool):
            ch = Chain(pool, pool_chain)
            link = ch.link
            link(pool.memset(ident[:, :], 0.0))
            pool.affine_select(out=ident[:, :], in_=ident[:, :], compare_op=ALU.not_equal, fill=1.0, base=0,
                               pattern=[[-1, P]], channel_multiplier=1).then_inc(const_ready, 1)
            pool.wait_ge(const_ready, 1)
            pool.memset(ones[:, :], 1.0).then_inc(const_ready, 1)
            pool.dma_start(wdr, w_dw[0]).then_inc(wdr_in, 16)
            srow = state_conv[0].rearrange("s t c -> (s t) c")
            for a in range(2):
                pool.dma_start(crow[:, a, :], srow[120 * a:120 * (a + 1), :]).then_inc(st_in, 16)
            pool.dma_start(prow, state_pool[0].rearrange("s t c -> (s t) c")).then_inc(st_in, 16)
            pool.dma_start(wr3[:, :, 0:NG], w_rg[0].rearrange("(k p) c -> p k c", p=P)).then_inc(wr_in, 16)
            pool.dma_start(wr3[:, :, NG:NR], w_re[0].rearrange("(k p) c -> p k c", p=P)).then_inc(wr_in, 16)
            pool.dma_start(bias[:, 0:NG], b_rg[0:1, :].to_broadcast([TR, NG])).then_inc(bias_in, 16)
            pool.dma_start(bias[:, NG:NR], b_re[0:1, :].to_broadcast([TR, NE])).then_inc(bias_in, 16)
            pool.dma_start(conv_s[0, :, 0:HC - SLEN, :], state_conv[0, :, SLEN:HC, :]).then_inc(old_out, 16)
            pool.dma_start(pool_s[0, :, 0:HP - SLEN, :], state_pool[0, :, SLEN:HP, :]).then_inc(old_out, 16)

            link(pool.memset(aw[:, :, 0:HC], 0.0))
            link(pool.memset(uline[:, :, 0:HP], 0.0))
            link(pool.memset(zero[:, :], 0.0))
            for t in range(HP):
                ch.step(pool.memset(rcol[:, t:t + 1], 1.0 / (t + 1)))
            link(pool.memset(earlier[:, :], 1.0))
            link(pool.affine_select(out=earlier[:, :], in_=earlier[:, :], compare_op=ALU.is_gt, fill=0.0, base=0,
                                    pattern=[[1, TR]], channel_multiplier=-1))
            link(pool.iota(io_i[:, :], pattern=[[1, P]], base=0, channel_multiplier=0))
            link(pool.tensor_copy(iof[:, :], io_i[:, :]))
            link(pool.iota(tid_i[:, :], pattern=[[TR, TT]], base=0, channel_multiplier=1))
            for c in range(2):
                link(pool.tensor_scalar(cdst[:, c, :], tid_i[:, :], 4.0, float(2 * c - PAD), ALU.mult, ALU.add))
            link(pool.memset(half[0:BLK, :], 0.0))
            link(pool.memset(half[BLK:P, :], 1.0))
            pool.wait_ge(const_ready, 2)
            pool.sem_inc(const_ready, 1)
            pool.wait_ge(wdT_ready, 2)
            pool.wait_ge(hist_ready, 4)
            with pool.Fori(0, 4) as g:
                ch.loop(g, 1)
                pool.tensor_copy(wdw[:, :, :], dyn(wdT, 64 * g, 64).rearrange("p (c w) -> p c w", c=2))
                pool.tensor_copy(hw[:, :, :, 0:HC], dyn(arena, O_HIST + 2 * NSEQ * HC * g, 2 * NSEQ * HC)
                                 .rearrange("p (c s t) -> p c s t", c=2, s=NSEQ)).then_inc(work_ready, 1)
                pool.wait_ge(glu_ready, 2 * g + 2)
                pool.sem_inc(waited, 1)
                link(pool.tensor_copy(hw[:, :, :, HC:HC + SLEN], aw[:, :, HC + SEQ:AEXT].rearrange("p c (s t) -> p c s t", s=NSEQ)))
                for cc in range(2):
                    first_taps = hw[:, cc, :, 0:SLEN]
                    windows = bass.AP(first_taps.tensor, first_taps.offset, [first_taps.ap[0], [HC + SLEN, NSEQ], [1, SLEN], [1, W]])
                    taps = wdw[:, cc, 0:W][:, None, None, :].to_broadcast([P, NSEQ, SLEN, W])
                    pool.tensor_tensor(prod[:, cc, :, :].rearrange("p (s t) w -> p s t w", s=NSEQ), windows, taps,
                                       ALU.mult).then_inc(prod_ready, 1)
                pool.tensor_copy(dyn(arena, O_AK + 2 * AK * g, 2 * AK).rearrange("p (c t) -> p c t", c=2),
                                 aw[:, :, AEXT - AK:AEXT]).then_inc(keep_ready, 1)
                pool.wait_ge(conv_chain, PERC * (g + 1))
            ch.end(4)
            for m in range(NG):
                g = NG - 1 - m
                pool.wait_ge(u_evac[m % 2], 2 * (m // 2) + 2)
                x = uline[:, 2 * g:2 * g + 2, :]
                src, n = x, 1
                for step in range(g + 1):
                    dst = ws[:, step % 2, :, :]
                    lo_ = 2 * n - 1
                    link(pool.tensor_tensor(dst[:, :, lo_:ULINE], src[:, :, lo_:ULINE], src[:, :, lo_ - n:ULINE - n], ALU.add))
                    src, n = dst, 2 * n
                ch.step(pool.tensor_tensor(src[:, :, HP:HP + n - 1], src[:, :, HP:HP + n - 1],
                                           rcol[:, None, 0:n - 1].to_broadcast([P, 2, n - 1]), ALU.mult))
                link(pool.tensor_scalar(src[:, :, HP + n - 1:ULINE], src[:, :, HP + n - 1:ULINE], 1.0 / n, 1.0, ALU.mult, ALU.mult))
                ch.step(pool.tensor_tensor(sT[:, 2 * g:2 * g + 2, 0:SEQ], src[:, :, HP:SM0], x[:, :, HP:SM0], ALU.subtract))
                for a in range(2):
                    new = [v[:, a, SM0:ULINE].rearrange("p (s t) -> p s t", s=NSEQ)[:, :, HP:HP + SLEN] for v in (src, x)]
                    ins = pool.tensor_tensor(sT[:, 2 * g + a, SEQ:NTOK].rearrange("p (s t) -> p s t", s=NSEQ), new[0], new[1], ALU.subtract)
                    ins.then_inc(s_ready, 1)
                pool.wait_ge(s_ready, 2 * m + 2)
            def scatter(i):
                for s in range(2):
                    n = 2 * i + s
                    if not (isinstance(i, int) and i == 0):
                        pool.wait_ge(y_out[s], 16 * i)
                    pool.sem_inc(ysb_free[s], 1)
                    if isinstance(i, int) and i == 0:
                        pool.wait_ge(dst_ready, 1)
                    pool.tensor_copy(cur_d[:, s:s + 1], dyn(dst_i, n, 1)).then_inc(dcur_ready, 1)
                    pool.wait_ge(dcur_ready, n + 1)
                    pool.wait_ge(y0_ready, n + 1)
                    pool.wait_ge(y1_ready, n + 1)
                    pool.sem_inc(waited, 1)
                    pool.indirect_dma_start(out=yexp_dram, out_offset=bass.IndirectOffsetOnAxis(ap=cur_d[:, s:s + 1], axis=0),
                                            in_=ysb[:, s, :], in_offset=None,
                                            bounds_check=4 * NTOK - 1, oob_is_err=False).then_inc(y_out[s], 16)

            scatter(0)
            with pool.Fori(1, PAIRS) as i:
                scatter(i)
            pool.wait_ge(over_ready, 1)
            n_over = pool.value_load(eid_i[0:1, 2 * OVP:2 * OVP + 1], min_val=0, max_val=2 * OVP)
            with pool.Fori(0, OVP) as j:
                with pool.If(n_over > 2 * j):
                    scatter(PAIRS + j)
            pool.wait_ge(gfin_in, 16)
            for t in range(TT):
                c = 0 if t < TT - 1 else D // 2
                pool.wait_ge(fin_sum, t + 1)
                pool.tensor_tensor(x1r[:, t, c:D], yg[:, t, 0, c:D], gfin[:, c:D], ALU.mult).then_inc(gained, 1)


_INS = ["x_prompt", "x_sample", "state_conv", "state_pool", "g_mix", "w_in", "w_dw", "b_dw", "ln_g", "ln_b", "w_pool",
        "pool_scale", "w_out", "g_ffn", "w_rg", "b_rg", "w_re", "b_re", "w_gate", "w_up", "w_down", "g_final"]
_OUTS = [(1, SEQ, D), (NSEQ, SLEN, D), (1, 1, HC, DC), (1, NSEQ, HC, DC), (1, 1, HP, DC), (1, NSEQ, HP, DC)]


def kernel(**inputs):
    import numpy as _np
    import concourse.bacc as _bacc
    from concourse import mybir as _mybir
    from concourse.bass_utils import run_bass_kernel_spmd as _run

    nc = _bacc.Bacc("TRN2", target_bir_lowering=False, num_devices=1)
    arrays, args = {}, []
    for name in _INS:
        a = _np.ascontiguousarray(inputs[name])
        arrays[f"in_{name}_dram"] = a
        args.append(nc.dram_tensor(f"in_{name}_dram", a.shape, _mybir.dt.from_np(a.dtype), kind="ExternalInput").ap())
    for i, shape in enumerate(_OUTS):
        args.append(nc.dram_tensor(f"out_{i}_dram", shape, _mybir.dt.float32, kind="ExternalOutput").ap())
    hybrid_decoder_step(nc, *args)
    r = _run(nc, [arrays], core_ids=[0])
    return tuple(r.results[0][f"out_{i}_dram"] for i in range(len(_OUTS)))
```
